# Optimizing a Trainium2 kernel written in Bass

```python
import jax
import jax.numpy as jnp
from jax import lax
import numpy as np
import jax, jax.numpy as jnp

D_MODEL = 1024
BATCH = 1
SEQ = 1024
DEPTH = 1

N_META = 16
GLA_WIDTH = D_MODEL // 2
GLA_HEADS = 4
GLA_DV = GLA_WIDTH // GLA_HEADS
GLA_DK = GLA_DV // 2
GLA_QK = GLA_HEADS * GLA_DK
GATE_RANK = 16
GATE_NORM = 16.0
CHUNK = 64
SUB = 16
CONV_CH = D_MODEL - GLA_WIDTH
CONV_K = 3
D_FF = 4 * D_MODEL
EPS = 1e-6
PROJ_SIZES = (GLA_QK, GLA_QK, GLA_WIDTH, GLA_WIDTH, GATE_RANK, CONV_CH, CONV_CH, CONV_CH)
PROJ_WIDTH = 2 * GLA_QK + 2 * GLA_WIDTH + GATE_RANK + 3 * CONV_CH


def rms_norm(x, w):
    xf = x.astype(jnp.float32)
    y = xf * lax.rsqrt(jnp.mean(xf * xf, axis=-1, keepdims=True) + EPS)
    return (y * w.astype(jnp.float32)).astype(x.dtype)

def split_cols(p):
    outs = []
    start = 0
    for s in PROJ_SIZES:
        outs.append(p[..., start:start + s])
        start += s
    return outs

def gla_chunked(q, k, v, gk):
    Bsz, Lp, H, dk = q.shape
    dv = v.shape[-1]
    N = Lp // CHUNK
    S = CHUNK // SUB

    def blk(t):
        return t.reshape(Bsz, N, S, SUB, H, t.shape[-1]).transpose(0, 4, 1, 2, 3, 5)

    q, k, v, gk = blk(q), blk(k), blk(v), blk(gk)
    b = jnp.cumsum(gk.reshape(Bsz, H, N, CHUNK, dk), axis=3).reshape(Bsz, H, N, S, SUB, dk)

    b_end = b[..., -1, :]
    r = jnp.concatenate([jnp.zeros_like(b_end[:, :, :, :1]), b_end[:, :, :, :-1]], axis=3)
    q_r = q * jnp.exp(b - r[..., None, :])
    lower = jnp.arange(S)[:, None] > jnp.arange(S)[None, :]
    expo = r[:, :, :, :, None, None, :] - b[:, :, :, None, :, :, :]
    expo = jnp.where(lower[:, :, None, None], expo, -jnp.inf)
    k_rel = k[:, :, :, None] * jnp.exp(expo)
    a_off = jnp.einsum('bhnsid,bhnstjd->bhnsitj', q_r, k_rel)

    causal = jnp.tril(jnp.ones((SUB, SUB), dtype=bool))
    pair = b[..., :, None, :] - b[..., None, :, :]
    pair = jnp.where(causal[:, :, None], pair, -jnp.inf)
    a_diag = jnp.einsum('bhnsid,bhnsjd,bhnsijd->bhnsij', q, k, jnp.exp(pair))
    eye = jnp.eye(S, dtype=a_off.dtype)
    a = a_off + a_diag[..., None, :] * eye[:, None, :, None]
    a = a.reshape(Bsz, H, N, CHUNK, CHUNK)

    qc = q.reshape(Bsz, H, N, CHUNK, dk)
    kc = k.reshape(Bsz, H, N, CHUNK, dk)
    vc = v.reshape(Bsz, H, N, CHUNK, dv)
    bc = b.reshape(Bsz, H, N, CHUNK, dk)
    o_intra = jnp.einsum('bhnij,bhnjv->bhniv', a, vc)

    b_last = bc[..., -1, :]
    kv = jnp.einsum('bhncd,bhncv->bhndv', kc * jnp.exp(b_last[..., None, :] - bc), vc)

    def step(h, inp):
        decay, kv_n = inp
        return h * decay[..., None] + kv_n, h

    h0 = jnp.zeros((Bsz, H, dk, dv), dtype=q.dtype)
    _, h_prev = lax.scan(step, h0, (jnp.moveaxis(jnp.exp(b_last), 2, 0), jnp.moveaxis(kv, 2, 0)))
    h_prev = jnp.moveaxis(h_prev, 0, 2)
    o_inter = jnp.einsum('bhncd,bhndv->bhncv', qc * jnp.exp(bc), h_prev)

    o = o_intra + o_inter
    return o.transpose(0, 2, 3, 1, 4).reshape(Bsz, Lp, H, dv)

def gla_branch(q, k, v, g, gr, w_gate_up, b_gate, norm_w):
    Bsz, L, _ = q.shape
    f32 = jnp.float32
    qh = q.astype(f32).reshape(Bsz, L, GLA_HEADS, GLA_DK) * (GLA_DK ** -0.5)
    kh = k.astype(f32).reshape(Bsz, L, GLA_HEADS, GLA_DK)
    vh = v.astype(f32).reshape(Bsz, L, GLA_HEADS, GLA_DV)
    gk = jax.nn.log_sigmoid(gr.astype(f32) @ w_gate_up.astype(f32) + b_gate.astype(f32)) / GATE_NORM
    gk = gk.reshape(Bsz, L, GLA_HEADS, GLA_DK)
    front = (-N_META) % CHUNK
    back = (-(front + L)) % CHUNK

    def padf(t):
        return jnp.pad(t, ((0, 0), (front, back), (0, 0), (0, 0)))

    o = gla_chunked(padf(qh), padf(kh), padf(vh), padf(gk))[:, front:front + L]
    o = rms_norm(o, norm_w)
    o = o.reshape(Bsz, L, GLA_WIDTH) * jax.nn.silu(g.astype(f32))
    return o.astype(q.dtype)

def short_conv_branch(cb, cc, cx, conv_w):
    u = cc * cx
    y = lax.conv_general_dilated(
        u, conv_w[:, None, :].astype(u.dtype), window_strides=(1,),
        padding=[(CONV_K - 1, 0)], dimension_numbers=('NWC', 'WIO', 'NWC'),
        feature_group_count=CONV_CH)
    return cb * y

def first_inputs(seed: int = 0) -> dict:
    key = jax.random.key(seed)
    ks = jax.random.split(key, 14)
    n = jax.random.normal
    return {
        'x': n(ks[0], (BATCH, SEQ, D_MODEL), jnp.float32),
        'meta_tokens': n(ks[1], (N_META, D_MODEL), jnp.float32),
        'norm_mix_w': 1.0 + 0.01 * n(ks[2], (DEPTH, D_MODEL), jnp.float32),
        'w_in': n(ks[3], (DEPTH, D_MODEL, PROJ_WIDTH), jnp.float32) * D_MODEL ** -0.5,
        'w_gate_up': n(ks[4], (DEPTH, GATE_RANK, GLA_QK), jnp.float32) * GATE_RANK ** -0.5,
        'b_gate': 0.1 * n(ks[5], (DEPTH, GLA_QK), jnp.float32),
        'gla_norm_w': 1.0 + 0.01 * n(ks[6], (DEPTH, GLA_DV), jnp.float32),
        'conv_w': n(ks[7], (DEPTH, CONV_K, CONV_CH), jnp.float32) * CONV_K ** -0.5,
        'w_out': n(ks[8], (DEPTH, D_MODEL, D_MODEL), jnp.float32) * D_MODEL ** -0.5,
        'norm_mlp_w': 1.0 + 0.01 * n(ks[9], (DEPTH, D_MODEL), jnp.float32),
        'w_up': n(ks[10], (DEPTH, D_MODEL, D_FF), jnp.float32) * D_MODEL ** -0.5,
        'w_down': n(ks[11], (DEPTH, D_FF, D_MODEL), jnp.float32) * D_FF ** -0.5,
        'norm_final_w': 1.0 + 0.01 * n(ks[12], (D_MODEL,), jnp.float32),
    }

def first_block(x, meta_tokens, norm_mix_w, w_in, w_gate_up, b_gate, gla_norm_w, conv_w,
              w_out, norm_mlp_w, w_up, w_down, norm_final_w):
    Bsz = x.shape[0]
    meta = jnp.broadcast_to(meta_tokens.astype(x.dtype)[None], (Bsz, N_META, D_MODEL))
    h = jnp.concatenate([meta, x], axis=1)
    for layer in range(DEPTH):
        hn = rms_norm(h, norm_mix_w[layer])
        proj = hn @ w_in[layer]
        q, k, v, g, gr, cb, cc, cx = split_cols(proj)
        y_gla = gla_branch(q, k, v, g, gr, w_gate_up[layer], b_gate[layer], gla_norm_w[layer])
        y_conv = short_conv_branch(cb, cc, cx, conv_w[layer]).astype(h.dtype)
        mixed = jnp.concatenate([y_gla.astype(h.dtype), y_conv], axis=-1) @ w_out[layer]
        h = h + mixed
        hn = rms_norm(h, norm_mlp_w[layer])
        h = h + jnp.square(jax.nn.relu(hn @ w_up[layer])) @ w_down[layer]
    out = rms_norm(h, norm_final_w)
    return out[:, N_META:]


_first_inputs = first_inputs


def first_inputs(seed=0):
    import zlib

    import numpy as np

    out = dict(_first_inputs(seed))
    spreads = {}
    factors = {'norm_mix_w': 4.48,
     'b_gate': 3.429,
     'gla_norm_w': 8.0,
     'norm_mlp_w': 7.164,
     'norm_final_w': 5.758}
    for name, (base, spread) in spreads.items():
        noise = np.random.default_rng([zlib.crc32(name.encode()), seed]).standard_normal(out[name].shape)
        drawn = base * np.exp(spread * noise) if base else spread * noise
        out[name] = jnp.asarray(drawn.astype(out[name].dtype))
    for name, factor in factors.items():
        out[name] = (out[name] * factor).astype(out[name].dtype)
    return out


_narrow_inputs = first_inputs


def first_inputs(seed=0):

    out = dict(_narrow_inputs(seed))
    wider = {'norm_mix_w': 3.26, 'gla_norm_w': 12.0, 'norm_mlp_w': 7.97, 'norm_final_w': 6.48}
    for name, times in wider.items():
        mean = out[name].mean()
        out[name] = (mean + times * (out[name] - mean)).astype(out[name].dtype)
    return out


HEAD_DIM = 64
W_FOX = (D_MODEL * 3 // 8) // HEAD_DIM * HEAD_DIM
N_HEADS_FOX = W_FOX // HEAD_DIM
CONV_CH_2 = D_MODEL // 4
W_DIL = D_MODEL - W_FOX - CONV_CH_2
N_HEADS_DIL = W_DIL // HEAD_DIM
DILATION_PAIRS = ((128, 1), (512, 4), (2048, 16))
CONV_K_2 = 31
FFN_CONV_K = 3
D_FF_2 = ((8 * D_MODEL // 3 + 127) // 128) * 128
Q_BLOCK = 128
OFF_QA = 0
OFF_KA = OFF_QA + W_FOX
OFF_VA = OFF_KA + W_FOX
OFF_FA = OFF_VA + W_FOX
OFF_QB = OFF_FA + N_HEADS_FOX
OFF_KB = OFF_QB + W_DIL
OFF_VB = OFF_KB + W_DIL
OFF_GV = OFF_VB + W_DIL
OFF_GG = OFF_GV + CONV_CH_2
N_IN = OFF_GG + CONV_CH_2


def rmsnorm(x, g):
    xf = x.astype(jnp.float32)
    y = xf * lax.rsqrt(jnp.mean(xf * xf, axis=-1, keepdims=True) + EPS)
    return (y * g.astype(jnp.float32)).astype(x.dtype)

def layernorm(x, g, b):
    xf = x.astype(jnp.float32)
    mu = jnp.mean(xf, axis=-1, keepdims=True)
    xc = xf - mu
    y = xc * lax.rsqrt(jnp.mean(xc * xc, axis=-1, keepdims=True) + EPS)
    return (y * g.astype(jnp.float32) + b.astype(jnp.float32)).astype(x.dtype)

def causal_dwconv(x, w, b):
    k, c = w.shape
    y = lax.conv_general_dilated(x, w[:, None, :].astype(x.dtype), window_strides=(1,),
                                 padding=[(k - 1, 0)], dimension_numbers=('NWC', 'WIO', 'NWC'),
                                 feature_group_count=c)
    return y + b.astype(x.dtype)

def forgetting_attention(q, k, v, log_f):
    B, S, H, Dh = q.shape
    nb = S // Q_BLOCK
    c = jnp.cumsum(log_f, axis=1)
    c_k = jnp.transpose(c, (0, 2, 1))[:, :, None, :]
    qb = q.reshape(B, nb, Q_BLOCK, H, Dh).swapaxes(0, 1)
    cb = c.reshape(B, nb, Q_BLOCK, H).swapaxes(0, 1)
    kpos = jnp.arange(S)
    scale = Dh ** -0.5

    def block(args):
        qi, ci, i = args
        s = jnp.einsum('bqhd,bkhd->bhqk', qi, k, preferred_element_type=jnp.float32) * scale
        s = s + jnp.transpose(ci, (0, 2, 1))[..., None] - c_k
        qpos = i * Q_BLOCK + jnp.arange(Q_BLOCK)
        s = jnp.where(kpos[None, :] <= qpos[:, None], s, -jnp.inf)
        p = jax.nn.softmax(s, axis=-1)
        return jnp.einsum('bhqk,bkhd->bqhd', p.astype(v.dtype), v)

    o = lax.map(block, (qb, cb, jnp.arange(nb)))
    return o.swapaxes(0, 1).reshape(B, S, H, Dh)

def dilated_branch(q, k, v, window, dilation):
    B, S, H, Dh = q.shape
    blk = window // dilation
    span = blk * dilation
    sp = -(-S // span) * span
    nb = sp // span
    pad = ((0, 0), (0, sp - S), (0, 0), (0, 0))

    def strided(t):
        return jnp.pad(t, pad).reshape(B, nb, blk, dilation, H, Dh)

    qs, ks, vs = strided(q), strided(k), strided(v)
    def with_prev(t):
        prev = jnp.concatenate([jnp.zeros_like(t[:, :1]), t[:, :-1]], axis=1)
        return jnp.concatenate([prev, t], axis=2)
    kc, vc = with_prev(ks), with_prev(vs)
    s = jnp.einsum('bnqrhd,bnkrhd->bnrhqk', qs, kc, preferred_element_type=jnp.float32) * (Dh ** -0.5)
    qi = blk + jnp.arange(blk)
    ki = jnp.arange(2 * blk)
    delta = qi[:, None] - ki[None, :]
    band = (delta >= 0) & (delta <= blk)
    first = (jnp.arange(nb) == 0)[:, None, None] & (ki < blk)[None, None, :]
    valid = band[None] & ~first
    s = jnp.where(valid[None, :, None, None], s, -jnp.inf)
    m = jnp.max(s, axis=-1, keepdims=True)
    e = jnp.exp(s - m)
    l = jnp.sum(e, axis=-1)
    num = jnp.einsum('bnrhqk,bnkrhd->bnqrhd', e.astype(v.dtype), vc,
                     preferred_element_type=jnp.float32)
    num = num.reshape(B, sp, H, Dh)[:, :S]
    def to_seq(t):
        return jnp.transpose(t, (0, 1, 4, 2, 3)).reshape(B, sp, H)[:, :S]
    return num, to_seq(m[..., 0]), to_seq(l)

def dilated_mixture(q, k, v):
    parts = [dilated_branch(q, k, v, w, d) for (w, d) in DILATION_PAIRS]
    m_all = parts[0][1]
    for _, m, _ in parts[1:]:
        m_all = jnp.maximum(m_all, m)
    num = 0.0
    den = 0.0
    for n_p, m_p, l_p in parts:
        a = jnp.exp(m_p - m_all)
        num = num + a[..., None] * n_p
        den = den + a * l_p
    return (num / den[..., None]).astype(q.dtype)

def second_inputs(seed: int = 0) -> dict:
    key = jax.random.key(seed)
    ks = jax.random.split(key, 20)
    f32 = jnp.float32
    def nrm(k, shape, scale):
        return jax.random.normal(k, shape, f32) * scale
    return {
        'x': nrm(ks[0], (BATCH, SEQ, D_MODEL), 1.0),
        'ln1_g': 1.0 + nrm(ks[1], (DEPTH, D_MODEL), 0.02),
        'w_in': nrm(ks[2], (DEPTH, D_MODEL, N_IN), D_MODEL ** -0.5),
        'b_forget': jax.random.uniform(ks[3], (DEPTH, N_HEADS_FOX), f32, 1.0, 4.0),
        'g_out_fox': 1.0 + nrm(ks[4], (DEPTH, W_FOX), 0.02),
        'g_out_dil': 1.0 + nrm(ks[5], (DEPTH, W_DIL), 0.02),
        'conv_w': nrm(ks[6], (DEPTH, CONV_K_2, CONV_CH_2), CONV_K_2 ** -0.5),
        'conv_b': nrm(ks[7], (DEPTH, CONV_CH_2), 0.02),
        'cnorm_g': 1.0 + nrm(ks[8], (DEPTH, CONV_CH_2), 0.02),
        'cnorm_b': nrm(ks[9], (DEPTH, CONV_CH_2), 0.02),
        'w_o': nrm(ks[10], (DEPTH, D_MODEL, D_MODEL), D_MODEL ** -0.5),
        'ln2_g': 1.0 + nrm(ks[11], (DEPTH, D_MODEL), 0.02),
        'w_up': nrm(ks[12], (DEPTH, D_MODEL, 2 * D_FF_2), D_MODEL ** -0.5),
        'ffn_conv_w': nrm(ks[13], (DEPTH, FFN_CONV_K, 2 * D_FF_2), FFN_CONV_K ** -0.5),
        'ffn_conv_b': nrm(ks[14], (DEPTH, 2 * D_FF_2), 0.02),
        'w_down': nrm(ks[15], (DEPTH, D_FF_2, D_MODEL), D_FF_2 ** -0.5),
        'g_final': 1.0 + nrm(ks[16], (D_MODEL,), 0.02),
    }

def second_block(x, ln1_g, w_in, b_forget, g_out_fox, g_out_dil, conv_w, conv_b, cnorm_g, cnorm_b,
              w_o, ln2_g, w_up, ffn_conv_w, ffn_conv_b, w_down, g_final):
    B, S, _ = x.shape
    for l in range(DEPTH):
        h = rmsnorm(x, ln1_g[l])
        p = jnp.einsum('bsd,dn->bsn', h, w_in[l])
        qa = p[..., OFF_QA:OFF_KA].reshape(B, S, N_HEADS_FOX, HEAD_DIM)
        ka = p[..., OFF_KA:OFF_VA].reshape(B, S, N_HEADS_FOX, HEAD_DIM)
        va = p[..., OFF_VA:OFF_FA].reshape(B, S, N_HEADS_FOX, HEAD_DIM)
        log_f = jax.nn.log_sigmoid(p[..., OFF_FA:OFF_QB].astype(jnp.float32)
                                   + b_forget[l].astype(jnp.float32))
        ya = forgetting_attention(qa, ka, va, log_f).reshape(B, S, W_FOX)
        ya = rmsnorm(ya, g_out_fox[l])
        qb = p[..., OFF_QB:OFF_KB].reshape(B, S, N_HEADS_DIL, HEAD_DIM)
        kb = p[..., OFF_KB:OFF_VB].reshape(B, S, N_HEADS_DIL, HEAD_DIM)
        vb = p[..., OFF_VB:OFF_GV].reshape(B, S, N_HEADS_DIL, HEAD_DIM)
        yb = dilated_mixture(qb, kb, vb).reshape(B, S, W_DIL)
        yb = rmsnorm(yb, g_out_dil[l])
        yc = p[..., OFF_GV:OFF_GG] * jax.nn.sigmoid(p[..., OFF_GG:N_IN])
        yc = causal_dwconv(yc, conv_w[l], conv_b[l])
        yc = jax.nn.silu(layernorm(yc, cnorm_g[l], cnorm_b[l]))
        y = jnp.concatenate([ya, yb, yc], axis=-1)
        x = x + jnp.einsum('bsd,de->bse', y, w_o[l])
        h2 = rmsnorm(x, ln2_g[l])
        u = jnp.einsum('bsd,df->bsf', h2, w_up[l])
        u = causal_dwconv(u, ffn_conv_w[l], ffn_conv_b[l])
        hidden = jax.nn.silu(u[..., :D_FF_2]) * u[..., D_FF_2:]
        x = x + jnp.einsum('bsf,fd->bsd', hidden, w_down[l])
    return rmsnorm(x, g_final)


_first_inputs_2 = second_inputs


def second_inputs(seed=0):
    import zlib

    import numpy as np

    out = dict(_first_inputs_2(seed))
    spreads = {}
    factors = {'g_out_fox': 5.617,
     'g_out_dil': 5.144,
     'conv_b': 5.781,
     'cnorm_g': 8.0,
     'cnorm_b': 8.0,
     'ln2_g': 4.691,
     'ffn_conv_b': 4.942,
     'g_final': 2.862}
    for name, (base, spread) in spreads.items():
        noise = np.random.default_rng([zlib.crc32(name.encode()), seed]).standard_normal(out[name].shape)
        drawn = base * np.exp(spread * noise) if base else spread * noise
        out[name] = __import__('jax').numpy.asarray(drawn.astype(out[name].dtype))
    for name, factor in factors.items():
        out[name] = (out[name] * factor).astype(out[name].dtype)
    return out


_narrow_inputs_2 = second_inputs


def second_inputs(seed=0):

    out = dict(_narrow_inputs_2(seed))
    wider = {'g_out_fox': 3.61, 'g_out_dil': 3.62, 'cnorm_g': 4.6, 'cnorm_b': 4.33, 'g_final': 3.23}
    for name, times in wider.items():
        mean = out[name].mean()
        out[name] = (mean + times * (out[name] - mean)).astype(out[name].dtype)
    return out


D_MIX = D_MODEL
D_A = D_MIX // 2
D_B = D_MIX - D_A
N_HEADS_A = 4
HEAD_DIM_A = D_A // N_HEADS_A
CHUNK_3 = 128
POOL_WINDOWS = (2, 4, 8, 16)
N_POOL_GROUPS = len(POOL_WINDOWS)
POOL_GROUP_DIM = D_B // N_POOL_GROUPS
D_FF_3 = 4 * D_MODEL
N_MOD = 6


def rms_norm_3(x, g):
    xf = x.astype(jnp.float32)
    y = xf * lax.rsqrt(jnp.mean(xf * xf, axis=-1, keepdims=True) + EPS)
    return (y * g.astype(jnp.float32)).astype(x.dtype)

def layer_norm(x, g, b):
    xf = x.astype(jnp.float32)
    mu = jnp.mean(xf, axis=-1, keepdims=True)
    var = jnp.mean(jnp.square(xf - mu), axis=-1, keepdims=True)
    y = (xf - mu) * lax.rsqrt(var + EPS)
    return (y * g.astype(jnp.float32) + b.astype(jnp.float32)).astype(x.dtype)

def spatial_gating(z_a, w_spatial, b_spatial, ln_v_gain, ln_v_bias):
    b, s, _ = z_a.shape
    z_a = jax.nn.gelu(z_a)
    u, v = z_a[..., :D_A], z_a[..., D_A:]
    v = layer_norm(v, ln_v_gain, ln_v_bias)
    v = v.reshape(b, s // CHUNK_3, CHUNK_3, N_HEADS_A, HEAD_DIM_A)
    mask = jnp.tril(jnp.ones((CHUNK_3, CHUNK_3), dtype=w_spatial.dtype))
    w_causal = w_spatial * mask[None]
    mixed = jnp.einsum("hts,bnshd->bnthd", w_causal, v)
    mixed = mixed + b_spatial.T[:, :, None]
    return u * mixed.reshape(b, s, D_A)

def multiscale_pool(z_b, w_pool, b_pool, pool_scale):
    b, s, _ = z_b.shape
    zg = z_b.reshape(b, s, N_POOL_GROUPS, POOL_GROUP_DIM)
    zf = zg.astype(jnp.float32)
    cs = jnp.concatenate(
        [jnp.zeros((b, 1, N_POOL_GROUPS, POOL_GROUP_DIM), jnp.float32), jnp.cumsum(zf, axis=1)],
        axis=1)
    pos = jnp.arange(s, dtype=jnp.float32)
    pooled = []
    for g, w in enumerate(POOL_WINDOWS):
        csg = cs[:, :, g]
        lower = jnp.concatenate(
            [jnp.zeros((b, w - 1, POOL_GROUP_DIM), jnp.float32), csg[:, : s + 1 - w]], axis=1)
        count = jnp.minimum(pos + 1.0, float(w))[None, :, None]
        pooled.append((csg[:, 1:] - lower) / count)
    pooled = jnp.stack(pooled, axis=2)
    diff = (pooled - zf).astype(z_b.dtype)
    y = jnp.einsum("bsgc,gcd->bsgd", diff, w_pool) + b_pool
    return y.reshape(b, s, D_B) * pool_scale

def third_inputs(seed: int = 0) -> dict:
    key = jax.random.key(seed)
    ks = jax.random.split(key, 20)
    f32 = jnp.float32
    nrm = lambda k, shape, scale: jax.random.normal(k, shape, f32) * scale
    return {
        "x": nrm(ks[0], (BATCH, SEQ, D_MODEL), 1.0),
        "c": nrm(ks[1], (BATCH, D_MODEL), 1.0),
        "w_ada": nrm(ks[2], (D_MODEL, N_MOD * D_MODEL), 0.5 * D_MODEL ** -0.5),
        "b_ada": nrm(ks[3], (N_MOD * D_MODEL,), 0.01),
        "norm1_pre": 1.0 + nrm(ks[4], (D_MODEL,), 0.02),
        "norm1_post": 1.0 + nrm(ks[5], (D_MODEL,), 0.02),
        "w_in": nrm(ks[6], (D_MODEL, 2 * D_A + D_B), D_MODEL ** -0.5),
        "w_spatial": nrm(ks[7], (N_HEADS_A, CHUNK_3, CHUNK_3), 0.5 * CHUNK_3 ** -0.5),
        "b_spatial": 1.0 + nrm(ks[8], (N_HEADS_A, CHUNK_3), 0.02),
        "ln_v_gain": 1.0 + nrm(ks[9], (D_A,), 0.02),
        "ln_v_bias": nrm(ks[10], (D_A,), 0.02),
        "w_pool": nrm(ks[11], (N_POOL_GROUPS, POOL_GROUP_DIM, POOL_GROUP_DIM), POOL_GROUP_DIM ** -0.5),
        "b_pool": nrm(ks[12], (N_POOL_GROUPS, POOL_GROUP_DIM), 0.02),
        "pool_scale": 1.0 + nrm(ks[13], (D_B,), 0.02),
        "w_out": nrm(ks[14], (D_MIX, D_MODEL), D_MIX ** -0.5),
        "norm2_pre": 1.0 + nrm(ks[15], (D_MODEL,), 0.02),
        "norm2_post": 1.0 + nrm(ks[16], (D_MODEL,), 0.02),
        "w_fc1": nrm(ks[17], (DEPTH, D_MODEL, D_FF_3), D_MODEL ** -0.5)[0],
        "w_fc2": nrm(ks[18], (D_FF_3, D_MODEL), D_FF_3 ** -0.5),
    }

def third_block(x, c, w_ada, b_ada, norm1_pre, norm1_post, w_in, w_spatial, b_spatial,
              ln_v_gain, ln_v_bias, w_pool, b_pool, pool_scale, w_out,
              norm2_pre, norm2_post, w_fc1, w_fc2):
    mod = jax.nn.silu(c) @ w_ada + b_ada
    shift1, scale1, gate1, shift2, scale2, gate2 = [
        m[:, None, :] for m in jnp.split(mod, N_MOD, axis=-1)]

    for _ in range(DEPTH):
        h = rms_norm_3(x, norm1_pre) * (1.0 + scale1) + shift1
        z = h @ w_in
        y_a = spatial_gating(z[..., : 2 * D_A], w_spatial, b_spatial, ln_v_gain, ln_v_bias)
        y_b = multiscale_pool(z[..., 2 * D_A:], w_pool, b_pool, pool_scale)
        mix = jnp.concatenate([y_a, y_b], axis=-1) @ w_out
        x = x + gate1 * rms_norm_3(mix, norm1_post)

        h = rms_norm_3(x, norm2_pre) * (1.0 + scale2) + shift2
        f = jnp.square(jax.nn.relu(h @ w_fc1)) @ w_fc2
        x = x + gate2 * rms_norm_3(f, norm2_post)
    return x


_first_inputs_3 = third_inputs


def third_inputs(seed=0):
    import zlib

    import numpy as np

    out = dict(_first_inputs_3(seed))
    spreads = {}
    factors = {'b_ada': 3.996,
     'norm1_pre': 22.156,
     'norm1_post': 8.0,
     'b_spatial': 176.082,
     'ln_v_gain': 200.0,
     'ln_v_bias': 200.0,
     'b_pool': 84.804,
     'pool_scale': 132.049,
     'norm2_pre': 28.473,
     'norm2_post': 98.714}
    for name, (base, spread) in spreads.items():
        noise = np.random.default_rng([zlib.crc32(name.encode()), seed]).standard_normal(out[name].shape)
        drawn = base * np.exp(spread * noise) if base else spread * noise
        out[name] = __import__('jax').numpy.asarray(drawn.astype(out[name].dtype))
    for name, factor in factors.items():
        out[name] = (out[name] * factor).astype(out[name].dtype)
    return out


_narrow_inputs_3 = third_inputs


def third_inputs(seed=0):

    out = dict(_narrow_inputs_3(seed))
    wider = {'b_spatial': 4.71,
     'ln_v_gain': 10.93,
     'ln_v_bias': 10.09,
     'pool_scale': 4.67,
     'norm2_post': 3.22}
    for name, times in wider.items():
        mean = out[name].mean()
        out[name] = (mean + times * (out[name] - mean)).astype(out[name].dtype)
    return out


def setup_inputs(seed=0):
    out = dict(first_inputs(seed))
    for name, value in second_inputs(seed + 1).items():
        if name != "x":
            out[name + "_2"] = value
    for name, value in third_inputs(seed + 2).items():
        if name != "x":
            out[name + "_3"] = value
    return out


def reference(
    x, meta_tokens, norm_mix_w, w_in, w_gate_up, b_gate, gla_norm_w, conv_w, w_out, norm_mlp_w,
    w_up, w_down, norm_final_w, ln1_g_2, w_in_2, b_forget_2, g_out_fox_2, g_out_dil_2, conv_w_2,
    conv_b_2, cnorm_g_2, cnorm_b_2, w_o_2, ln2_g_2, w_up_2, ffn_conv_w_2, ffn_conv_b_2,
    w_down_2, g_final_2, c_3, w_ada_3, b_ada_3, norm1_pre_3, norm1_post_3, w_in_3, w_spatial_3,
    b_spatial_3, ln_v_gain_3, ln_v_bias_3, w_pool_3, b_pool_3, pool_scale_3, w_out_3,
    norm2_pre_3, norm2_post_3, w_fc1_3, w_fc2_3,
):
    x = first_block(
        x, meta_tokens, norm_mix_w, w_in, w_gate_up, b_gate, gla_norm_w, conv_w, w_out,
        norm_mlp_w, w_up, w_down, norm_final_w,
    )
    x = second_block(
        x, ln1_g_2, w_in_2, b_forget_2, g_out_fox_2, g_out_dil_2, conv_w_2, conv_b_2, cnorm_g_2,
        cnorm_b_2, w_o_2, ln2_g_2, w_up_2, ffn_conv_w_2, ffn_conv_b_2, w_down_2, g_final_2,
    )
    return third_block(
        x, c_3, w_ada_3, b_ada_3, norm1_pre_3, norm1_post_3, w_in_3, w_spatial_3, b_spatial_3,
        ln_v_gain_3, ln_v_bias_3, w_pool_3, b_pool_3, pool_scale_3, w_out_3, norm2_pre_3,
        norm2_post_3, w_fc1_3, w_fc2_3,
    )


_drawn_inputs = setup_inputs


def setup_inputs(seed=0):
    import zlib

    import numpy as np

    out = dict(_drawn_inputs(seed))
    spreads = {}
    factors = {'norm1_pre_3': 3.638, 'norm1_post_3': 3.91, 'b_pool_3': 3.636}
    for name, (base, spread) in spreads.items():
        noise = np.random.default_rng([zlib.crc32(name.encode()), seed]).standard_normal(out[name].shape)
        drawn = base * np.exp(spread * noise) if base else spread * noise
        out[name] = jnp.asarray(drawn.astype(out[name].dtype))
    for name, factor in factors.items():
        out[name] = (out[name] * factor).astype(out[name].dtype)
    return out
```

```python
from contextlib import ExitStack

import numpy as np

import concourse.bass as bass
from concourse import mybir

F = mybir.dt.float32
R = mybir.dt.float32r
BF = mybir.dt.bfloat16
U8 = mybir.dt.uint8
ALU = mybir.AluOpType
ACT = mybir.ActivationFunctionType
AX = mybir.AxisListType
MUL, ADD, SUB, MAX, MIN = ALU.mult, ALU.add, ALU.subtract, ALU.max, ALU.min

P = 128
S = 1024
NMETA = 16
EPS = 1e-6
FF2 = 2816
NPAIR = FF2 // 128
LEVELS = (64, 32, 16, 8, 4, 2, 1)
NEG = -1e30
W2 = 6

COLS = {}


def _columns():
    at = 0
    for name, n in (("norm_mix", 8), ("norm_mlp", 8), ("norm_final", 8), ("b_gate", 2), ("gla_norm", 1),
                    ("conv1", 12), ("ln1", 8), ("ln2", 8), ("g_final", 8), ("fox", 3), ("dil", 3),
                    ("conv2", 62), ("conv2_b", 2), ("cn_g", 2), ("cn_b", 2), ("ffn_w", 132), ("ffn_b", 44),
                    ("b_ada", 48), ("n1pre", 8), ("n1post", 8), ("n2pre", 8), ("n2post", 8),
                    ("pscale", 4), ("b_pool", 4), ("b_forget", 1), ("c", 8), ("rcnt", 64)):
        COLS[name] = (at, n)
        at += n
    return at


NCOL = _columns()


class Engine:

    def __init__(self, name, sem):
        self.name, self.sem, self.count, self.todo, self.seen = name, sem, 0, [], {}

    def wait(self, *tokens):
        for sem, value in tokens:
            if self.seen.get(sem.name, 0) < value:
                self.seen[sem.name] = value
                self.todo.append(lambda e, s=sem, v=value: e.wait_ge(s, v))

    def go(self, fn, *tokens):
        self.wait(*tokens)
        self.todo.append(fn)

    def op(self, fn, *tokens):
        self.wait(*tokens)
        self.count += 1
        self.todo.append(lambda e: fn(e).then_inc(self.sem, 1))
        return (self.sem, self.count)

    @property
    def last(self):
        return (self.sem, self.count)

    def run(self, e):
        for fn in self.todo:
            fn(e)


class Slot:

    def __init__(self, ap):
        self.ap, self._busy, self.held = ap, [], False

    @property
    def busy(self):
        return self._busy

    @busy.setter
    def busy(self, tokens):
        self._busy, self.held = tokens, False


class Ring:
    def __init__(self, slots):
        self.slots, self.at = slots, 0

    def take(self):
        for _ in self.slots:
            s = self.slots[self.at % len(self.slots)]
            self.at += 1
            if not s.held:
                s.held = True
                return s
        raise AssertionError("every buffer is held")


def build(nc, d, out, upto=3):
    ctx = ExitStack()
    with ctx:
        def sem(name):
            return ctx.enter_context(nc.semaphore(name))

        pe, act, dve, pool, sp = (Engine(n, sem("s_" + n)) for n in ("pe", "act", "dve", "pool", "sp"))

        class Dsem:
            def __init__(self, name):
                self.sem, self.count = sem("d_" + name), 0

        def dma(q, ds, o, i, *tokens):
            q.wait(*tokens)
            ds.count += 16
            q.todo.append(lambda e: e.dma_start(o, i).then_inc(ds.sem, 16))
            return (ds.sem, ds.count)

        base = -(-nc.sbuf_base // 64) * 64
        XO, HO = base, base + 32768
        GO = HO + 65536
        WO = GO + 65536
        TO = WO + 28672
        CO = TO + 12288
        names = [0]

        def at(off, shape, dt=F, name=None):
            names[0] += 1
            return nc.alloc_sbuf_tensor_at(name or f"b{names[0]}", list(shape), dt, offset=off)

        catch = [CO]

        def const(shape, dt=F):
            n = int(np.prod(shape[1:])) * {F: 4, R: 4, BF: 2, U8: 1}[dt]
            t = at(catch[0], shape, dt)
            catch[0] += -(-n // 32) * 32
            assert catch[0] <= nc.sbuf_usable_end, catch[0]
            return t

        def unit(region, n, shape, dt=F):
            return at(region + 4096 * n, shape, dt)

        X = at(XO, [P, 8, S])
        HH, HL = at(HO, [P, 8, S], R), at(HO + 32768, [P, 8, S], R)
        GH, GL = at(GO, [P, 8, S], R), at(GO + 32768, [P, 8, S], R)
        raw = [at(WO + 4096 * i, [P, 1024]) for i in range(3)]
        whi = [at(WO + 12288 + 4096 * i, [P, 1024], R) for i in range(2)]
        wlo = [at(WO + 20480 + 4096 * i, [P, 1024], R) for i in range(2)]
        T = [Slot(at(TO + 4096 * i, [P, S])) for i in range(3)]
        tring = Ring(T)

        psl = [Slot(ctx.enter_context(nc.psum_tensor(f"ps{i}", [P, 1024], F))) for i in range(3)]
        pring = Ring(psl)
        misc = Slot(ctx.enter_context(nc.psum_tensor("ps3", [P, 1024], F)))

        ident = const([P, P])
        ones = const([P, P])
        identb = const([P, P], BF)
        cols = const([P, NCOL])
        masks = const([P, 8, P], U8)
        negm = const([P, 3, P], BF)
        st = const([P, 8])
        rr = const([P, 8])
        HMH, HML = const([P, 8, NMETA], R), const([P, 8, NMETA], R)
        mod = const([P, 48])
        gx = const([P, 16])
        epsc = const([P, 1])
        onec = const([P, 1])

        def col(name, i=0, n=1):
            a, m = COLS[name]
            return cols[:, a + i:a + i + n]

        dc = Dsem("const")
        for o, i in ((ident[:], "ident"), (cols[:], "cols"), (T[0].ap[:], "masks"), (T[1].ap[:, 0:384], "negm")):
            tc = dma(sp, dc, o, d[i])
        tones = dve.op(lambda e: e.memset(ones[:], 1.0))
        dve.op(lambda e: e.memset(epsc[:], EPS))
        dve.op(lambda e: e.memset(onec[:], 1.0))
        dve.op(lambda e: e.tensor_copy(masks[:].rearrange("p a b -> p (a b)"), T[0].ap[:]), tc)
        dve.op(lambda e: e.tensor_copy(negm[:].rearrange("p a b -> p (a b)"), T[1].ap[:, 0:384]))
        dve.op(lambda e: e.tensor_copy(identb[:], ident[:]))
        consts = [tc, dve.last]
        T[0].busy = T[1].busy = [dve.last]
        for q in (pe, act, dve, pool):
            q.wait(*consts)


        def A(o, i, func, *w, scale=1.0, bias=None, accum=None):
            kw = {"scale": scale}
            if bias is not None:
                kw["bias"] = bias
            if accum is not None:
                kw["accum_out"] = accum
            return act.op(lambda e: e.activation(o, i, func, **kw), *w)

        def TT(o, a, b, op, *w, q=dve):
            return q.op(lambda e: e.tensor_tensor(o, a, b, op), *w)

        def TS(o, a, s1, s2, o1, o2, *w, q=dve):
            if o2 is None:
                return q.op(lambda e: e.tensor_scalar(o, a, s1, None, o1), *w)
            return q.op(lambda e: e.tensor_scalar(o, a, s1, s2, o1, o2), *w)

        def STT(o, a, s, b, o1, o2, *w):
            return dve.op(lambda e: e.scalar_tensor_tensor(out=o, in0=a, scalar=s, in1=b, op0=o1, op1=o2), *w)

        def CP(o, a, *w, q=dve):
            return q.op(lambda e: e.tensor_copy(o, a), *w)

        def split(src, hi, lo, *w, q=pool):
            t = A(hi, src, ACT.Copy, *w)
            return TT(lo, src, hi.bitcast(F), SUB, t, *w, q=q)


        wl = []

        def plan(name, ap, split=True):
            wl.append((name, ap, split))

        class Stream:
            def __init__(self):
                self.cur = self.dma = self.spl = 0
                self.ds = [Dsem(f"w{i}") for i in range(3)]
                self.landed, self.free, self.ready, self.slot = {}, {}, {}, {}
                self.nspl = 0
                self.used = {}

            def pump(self, i):
                while True:
                    moved = False
                    if self.dma < len(wl) and self.dma <= i + 4 and (self.dma < 3 or self.dma - 3 in self.free):
                        j = self.dma
                        ap = wl[j][1]
                        n = int(np.prod(ap.shape[1:]))
                        w = [self.free[j - 3]] if j >= 3 else []
                        dst = raw[j % 3][:, 0:n]
                        if len(ap.shape) == 3:
                            dst = dst.rearrange("p (k m) -> p k m", k=ap.shape[1])
                        self.landed[j] = dma(sp, self.ds[j % 3], dst, ap, *w)
                        self.dma += 1
                        moved = True
                    if self.spl < len(wl) and self.spl <= i + 1 and self.spl in self.landed:
                        j = self.spl
                        if wl[j][2]:
                            s = self.nspl % 2
                            if self.nspl < 2 or (self.nspl - 2) in self.used:
                                n = int(np.prod(wl[j][1].shape[1:]))
                                w = [self.used[self.nspl - 2]] if self.nspl >= 2 else []
                                t = split(raw[j % 3][:, 0:n], whi[s][:, 0:n], wlo[s][:, 0:n], self.landed[j], *w)
                                self.free[j] = self.ready[j] = t
                                self.slot[j] = (s, self.nspl)
                                self.nspl += 1
                                self.spl += 1
                                moved = True
                        else:
                            self.spl += 1
                            moved = True
                    if not moved:
                        return

            def take(self, name):
                i = self.cur
                assert wl[i][0] == name, (wl[i][0], name)
                self.cur += 1
                self.pump(i)
                return i

            def done(self, i, tok):
                if wl[i][2]:
                    self.used[self.slot[i][1]] = tok
                else:
                    self.free[i] = tok

        ws = Stream()

        class Rhs:

            def __init__(self, hi, lo, toks, meta=None):
                self.hi, self.lo, self.toks, self.meta = hi, lo, toks, meta

        def job(name, rhs, nk, k0=0, m=P, meta=False, into=None):
            i = ws.take(name)
            s, _ = ws.slot[i]
            hi = whi[s][:, 0:nk * m].rearrange("p (k m) -> p k m", k=nk)
            lo = wlo[s][:, 0:nk * m].rearrange("p (k m) -> p k m", k=nk)
            sl = pring.take()
            pe.wait(ws.ready[i], *sl.busy)
            if meta:
                pe.wait(*misc.busy)
            tot = 3 * nk
            n = 0
            for k in range(nk):
                pe.wait(rhs.toks[k0 + k])
                last = k == nk - 1
                for hf in range(2):
                    cs = slice(512 * hf, 512 * hf + 512)
                    o = sl.ap[0:m, cs]
                    pe.go(lambda e, o=o, k=k, cs=cs: e.matmul(o, hi[:, k, :], rhs.hi[:, k0 + k, cs], start=(k == 0), stop=False))
                    pe.go(lambda e, o=o, k=k, cs=cs: e.matmul(o, hi[:, k, :], rhs.lo[:, k0 + k, cs], start=False, stop=False))
                if meta:
                    o = misc.ap[0:m, 0:NMETA]
                    pe.go(lambda e, o=o, k=k: e.matmul(o, hi[:, k, :], HMH[:, k, :], start=(k == 0), stop=False))
                    pe.go(lambda e, o=o, k=k: e.matmul(o, hi[:, k, :], HML[:, k, :], start=False, stop=False))
                    pe.go(lambda e, o=o, k=k, last=last: e.matmul(o, lo[:, k, :], HMH[:, k, :], start=False, stop=last))
                for hf in range(2):
                    cs = slice(512 * hf, 512 * hf + 512)
                    o = sl.ap[0:m, cs]
                    f = lambda e, o=o, k=k, cs=cs, last=last: e.matmul(o, lo[:, k, :], rhs.hi[:, k0 + k, cs], start=False, stop=last)
                    if last and hf == 1:
                        tok = pe.op(f)
                    else:
                        pe.go(f)
            ws.done(i, tok)
            return sl, tok

        def job_tm(name, rhs, nk, meta=False):
            i = ws.take(name)
            s, _ = ws.slot[i]
            hi = whi[s][:, 0:nk * P].rearrange("p (k m) -> p k m", k=nk)
            lo = wlo[s][:, 0:nk * P].rearrange("p (k m) -> p k m", k=nk)
            sl = pring.take()
            pe.wait(ws.ready[i], *sl.busy)
            for k in range(nk):
                pe.wait(rhs.toks[k])
            for b in range(8):
                cs = slice(P * b, P * b + P)
                for k in range(nk):
                    last = k == nk - 1
                    o = sl.ap[:, cs]
                    pe.go(lambda e, o=o, k=k, cs=cs: e.matmul(o, rhs.hi[:, k, cs], hi[:, k, :], start=(k == 0), stop=False))
                    pe.go(lambda e, o=o, k=k, cs=cs: e.matmul(o, rhs.hi[:, k, cs], lo[:, k, :], start=False, stop=False))
                    f = lambda e, o=o, k=k, cs=cs, last=last: e.matmul(o, rhs.lo[:, k, cs], hi[:, k, :], start=False, stop=last)
                    if last and b == 7 and not meta:
                        tok = pe.op(f)
                    else:
                        pe.go(f)
            if meta:
                pe.wait(*misc.busy)
                o = misc.ap[0:32, 0:P]
                for k in range(nk):
                    last = k == nk - 1
                    hm, lm, wh, wlow = HMH[:, k, :], HML[:, k, :], hi[:, k, :], lo[:, k, :]
                    pe.go(lambda e, a=hm, b=wh, k=k: e.matmul(misc.ap[0:NMETA, 0:P], a.bitcast(F), b.bitcast(F), start=(k == 0), stop=False))
                    pe.go(lambda e, a=lm, b=wh: e.matmul(misc.ap[0:NMETA, 0:P], a.bitcast(F), b.bitcast(F), start=False, stop=False))
                    f = lambda e, a=hm, b=wlow, last=last: e.matmul(misc.ap[0:NMETA, 0:P], a.bitcast(F), b.bitcast(F), start=False, stop=last)
                    if last:
                        tok = pe.op(f)
                    else:
                        pe.go(f)
            ws.done(i, tok)
            return sl, tok

        def v3(ap, n):
            return ap.rearrange("p (a b) -> p a b", a=n)

        def compact_to_R(width, part, *w):
            D = width
            t = A(st[0:part, :], misc.ap[0:part, 0:8], ACT.Sqrt, *w, scale=1.0 / D, bias=epsc[0:part, :])
            t = dve.op(lambda e: e.reciprocal(rr[0:part, :], st[0:part, :]), t)
            return t

        def norm_R(xs, toks, width):
            acc = T[2]
            prev = None
            for k, (x, tk) in enumerate(zip(xs, toks)):
                if k == 0:
                    prev = A(acc.ap[:], x, ACT.Square, tk, *acc.busy)
                    continue
                b = T[(k - 1) % 2]
                t = A(b.ap[:], x, ACT.Square, tk, *b.busy)
                prev = TT(acc.ap[:], acc.ap[:], b.ap[:], ADD, t, prev)
                b.busy = [prev]
            pe.wait(prev, *misc.busy)
            for b in range(8):
                f = lambda e, b=b: e.matmul(misc.ap[:, b:b + 1], acc.ap[:, P * b:P * b + P], ones[:, 0:1], start=(b == 0), stop=True, skip_group_check=True)
                t = pe.op(f) if b == 7 else pe.go(f)
            acc.busy = [t]
            t = compact_to_R(width, P, t)
            g = T[0]
            t = TT(v3(g.ap[:], 8), ident[:].unsqueeze(1).broadcast_to([P, 8, P]),
                   rr[:].unsqueeze(2).broadcast_to([P, 8, P]), MUL, t, *g.busy)
            for hf in range(2):
                f = lambda e, hf=hf: e.matmul(misc.ap[:, 512 * hf:512 * hf + 512], ones[:], g.ap[:, 512 * hf:512 * hf + 512], start=True, stop=True)
                pe.wait(t)
                t2 = pe.op(f)
            g.busy = [t2]
            return t2

        def normed(xs, g, tR, hi, lo, *w, shift=None):
            toks = []
            for k, x in enumerate(xs):
                b = tring.take()
                t = STT(b.ap[:], x, g(k), misc.ap[:], MUL, MUL, tR, *b.busy, *w)
                if shift is not None:
                    t = TS(b.ap[:], b.ap[:], shift(k), None, ADD, None, t)
                t2 = split(b.ap[:], hi[:, k, :], lo[:, k, :], t, *w)
                b.busy = [t2]
                toks.append(t2)
            misc.busy = [dve.last]
            return Rhs(hi, lo, toks)

        def normed_in_place(xs, g, tR, *w):
            toks = []
            for k, x in enumerate(xs):
                toks.append(STT(x, x, g(k), misc.ap[:], MUL, MUL, tR, *w))
            misc.busy = [dve.last]
            return toks

        def drain_relu2(sl, tok, k):
            b = tring.take()
            t = A(b.ap[:], sl.ap[:], ACT.Relu, tok, *b.busy)
            sl.busy = [t]
            t = TT(b.ap[:], b.ap[:], b.ap[:], MUL, t)
            return b, t

        hidden = {"free": [[], []], "toks": [None] * 8}

        def mlp(name_up, name_down, rhs, ngroups, kin, one_up, acc, acc_toks, first_copy=False, sizes=None):
            sizes = sizes or [4] * ngroups
            gh = Rhs(GH, GL, hidden["toks"])

            def ups(g):
                for j in range(sizes[g]):
                    slot = 4 * (g % 2) + j
                    b, t = one_up(4 * g + j)
                    t = split(b.ap[:], GH[:, slot, :], GL[:, slot, :], t, *hidden["free"][g % 2])
                    b.busy = [t]
                    hidden["toks"][slot] = t

            ups(0)
            for g in range(ngroups):
                if g + 1 < ngroups:
                    ups(g + 1)
                for m in range(8):
                    sl, tok = job(f"{name_down}{g}_{m}", gh, sizes[g], k0=4 * (g % 2))
                    if g == 0 and first_copy:
                        t = A(acc[:, m, :], sl.ap[:], ACT.Copy, tok, *acc_toks[m])
                    else:
                        t = TT(acc[:, m, :], sl.ap[:], acc[:, m, :], ADD, tok, *acc_toks[m])
                    acc_toks[m] = [t]
                    sl.busy = [t]
                hidden["free"][g % 2] = [pe.last]
            return [a[0] for a in acc_toks]

        def plan_mlp(up, dn, name_up, name_down, ng, nk, sizes=None, pairs=False):
            sizes = sizes or [4] * ng

            def ups(g):
                for j in range(sizes[g]):
                    m = 4 * g + j
                    if pairs:
                        plan(f"{name_up}a{m}", d[up][m])
                        plan(f"{name_up}b{m}", d[up][NPAIR + m])
                        for q in range(3 if m < 16 and upto >= 3 else 0):
                            plan(f"ada{3 * m + q}", d["w_ada"][3 * m + q], split=False)
                    else:
                        plan(f"{name_up}{m}", d[up][m])
            ups(0)
            for g in range(ng):
                if g + 1 < ng:
                    ups(g + 1)
                for m in range(8):
                    plan(f"{name_down}{g}_{m}", d[dn][m, :, 4 * g * P:(4 * g + sizes[g]) * P])

        plan("gr", d["w_gr"])
        for n, m0 in (("k0", 2), ("k1", 3), ("q0", 0), ("q1", 1), ("v0", 4), ("v1", 5), ("v2", 6), ("v3", 7),
                      ("g0", 8), ("g1", 9), ("g2", 10), ("g3", 11)):
            plan(n, d["w_in"][m0])
        for m in range(4):
            plan(f"cc{m}", d["w_in"][16 + m])
            plan(f"cx{m}", d["w_in"][20 + m])
            plan(f"cb{m}", d["w_in"][12 + m])
        for m in range(8):
            plan(f"wo{m}", d["w_out"][m])
        plan_mlp("w_up", "w_down", "up", "dn", 8, 8)
        if upto >= 2:
            plan_block2(plan, plan_mlp, d, upto)
        if upto >= 3:
            plan_block3(plan, plan_mlp, d)

        ysc = nc.dram_tensor("ysc", (P, 8, S), F, kind="Internal").ap()
        sgsc = nc.dram_tensor("sgsc", (P, 4, S), F, kind="Internal").ap()
        xsc = nc.dram_tensor("xsc", (P, 8, S), F, kind="Internal").ap()

        dx = [Dsem(f"x{k}") for k in range(8)]
        dm = Dsem("meta")
        XM = unit(GO, 0, [P, 8, NMETA])
        SQM = at(GO + 1024, [P, 8, NMETA])
        DGM = at(GO + 2048, [NMETA, NMETA])
        TM = at(GO + 4096, [P, 8, NMETA])
        tm = dma(sp, dm, XM[:], d["metaT"])
        xt = [dma(sp, dx[k], X[:, k, :], d["xT"][:, k, :]) for k in range(8)]
        ws.pump(-1)

        t = A(SQM[:], XM[:], ACT.Square, tm)
        pe.wait(t)
        for k in range(8):
            f = lambda e, k=k: e.matmul(misc.ap[0:NMETA, 0:1], SQM[:, k, :], ones[:, 0:1], start=(k == 0), stop=(k == 7))
            t = pe.op(f) if k == 7 else pe.go(f)
        t = A(st[0:NMETA, 0:1], misc.ap[0:NMETA, 0:1], ACT.Sqrt, t, scale=1.0 / 1024, bias=epsc[0:NMETA, :])
        t = dve.op(lambda e: e.reciprocal(rr[0:NMETA, 0:1], st[0:NMETA, 0:1]), t)
        t = TS(DGM[:], ident[0:NMETA, 0:NMETA], rr[0:NMETA, 0:1], None, MUL, None, t)
        t = pe.op(lambda e: e.matmul(misc.ap[:, 0:NMETA], ones[0:NMETA, :], DGM[:], start=True, stop=True), t)
        for k in range(8):
            tw = STT(TM[:, k, :], XM[:, k, :], col("norm_mix", k), misc.ap[:, 0:NMETA], MUL, MUL, t)
        misc.busy = [tw]
        tmeta = split(TM[:], HMH[:], HML[:], tw)

        xs = [X[:, k, :] for k in range(8)]
        tR = norm_R(xs, xt, 1024)
        h = normed(xs, lambda k: col("norm_mix", k), tR, HH, HL)
        h_done = h.toks[-1]
        pe.wait(tmeta)
        xfree = [dve.last, act.last]
        gfree = [tmeta, h_done]

        def G(n, shape, dt=F):
            return unit(GO, n, shape, dt)

        Q, K, B, V, D, AT = (G(0, [P, 2, S]), G(2, [P, 2, S]), G(4, [P, 2, S]), G(6, [P, 8, 512]), G(10, [P, 2, S]),
                             G(12, [P, 4, S]))
        XL = [Slot(unit(XO, 0, [P, 2, S])), Slot(unit(XO, 2, [P, 2, S]))]
        QI = unit(XO, 4, [P, 2, S])
        U = unit(XO, 6, [P, 1026])
        mo = XO + 7 * 4096 + 64
        KM, BM, VM, KDM, EM = (at(mo, [P, 2, NMETA]), at(mo + 128, [P, 2, NMETA]), at(mo + 256, [NMETA, 512]),
                               at(mo + 2304, [NMETA, 256]), at(mo + 3328, [P, 2, NMETA]))
        KDT, SA = unit(XO, 0, [P, 8, 256]), unit(XO, 2, [P, 8, 256])

        tz = pool.op(lambda e: e.memset(AT[:], 0.0), *gfree)
        sl, tok = job("gr", h, 8, m=16, meta=True)
        gr = T[0]
        grm = T[1]
        t1 = CP(gr.ap[0:16, :], sl.ap[0:16, :], tok, *gr.busy)
        t2 = CP(grm.ap[0:16, 0:NMETA], misc.ap[0:16, 0:NMETA], tok, *grm.busy)
        sl.busy = [t1]
        misc.busy = [t2]
        wg = T[2]
        dg = Dsem("wg")
        tw = dma(sp, dg, wg.ap[0:16, 0:256], d["w_gate_up"], *wg.busy)

        def logsig(zs, bias, o_abs, o_min, o_g, *w):
            t = A(o_abs, zs, ACT.Abs, *w, bias=bias)
            tmn = TS(o_min, zs, bias, 0.0, ADD, MIN, t, *w)
            t2 = A(o_abs, o_abs, ACT.Exp, t, scale=-1.0)
            t2 = A(o_abs, o_abs, ACT.Ln, t2, bias=onec[0:o_abs.shape[0], :])
            return TT(o_g, o_min, o_abs, SUB, t2, tmn), t, tmn

        zt = []
        for m in range(2):
            sz = pring.take()
            pe.wait(t1, tw, *sz.busy)
            for hf in range(2):
                f = lambda e, hf=hf, m=m, sz=sz: e.matmul(sz.ap[:, 512 * hf:512 * hf + 512], wg.ap[0:16, P * m:P * m + P], gr.ap[0:16, 512 * hf:512 * hf + 512], start=True, stop=True)
                t = pe.op(f)
            g_, ta, tb = logsig(sz.ap[:], col("b_gate", m), D[:, m, :], B[:, m, :], D[:, m, :], t, *gfree)
            sz.busy = [ta, tb]
            zt.append(g_)
        gr.busy = [pe.last]
        zm = []
        for m in range(2):
            pe.wait(t2, *misc.busy)
            t = pe.op(lambda e, m=m: e.matmul(misc.ap[:, 0:NMETA], wg.ap[0:16, P * m:P * m + P], grm.ap[0:16, 0:NMETA], start=True, stop=True))
            g_, ta, tb = logsig(misc.ap[:, 0:NMETA], col("b_gate", m), EM[:, m, :], BM[:, m, :], EM[:, m, :], t, *xfree)
            misc.busy = [ta, tb]
            zm.append(g_)
        wg.busy = [pe.last]
        grm.busy = [pe.last]
        keep = T[2]
        ta = pool.op(lambda e: e.memset(keep.ap[:], 1.0), *keep.busy)
        ta = pool.op(lambda e: e.memset(v3(keep.ap[:], 8)[:, :, 0:1], 0.0), ta)
        tb = []
        for m in range(2):
            tb.append(dve.op(lambda e, m=m: e.tensor_tensor_scan(B[:, m, :], keep.ap[:], D[:, m, :], 0.0, MUL, ADD), ta, zt[m]))
            tbm = dve.op(lambda e, m=m: e.tensor_tensor_scan(BM[:, m, :], keep.ap[:, 1:1 + NMETA], EM[:, m, :], 0.0, MUL, ADD), ta, zm[m])
        keep.busy = [tbm]
        tb.append(tbm)

        tk, tq = [], []
        for m in range(2):
            sl, tok = job(f"k{m}", h, 8, meta=True)
            t = A(K[:, m, :], sl.ap[:], ACT.Copy, tok, *gfree)
            sl.busy = [t]
            t2 = CP(KM[:, m, :], misc.ap[:, 0:NMETA], tok, *xfree)
            misc.busy = [t2]
            tk += [t, t2]
        for m in range(2):
            sl, tok = job(f"q{m}", h, 8)
            t = A(Q[:, m, :], sl.ap[:], ACT.Copy, tok, *gfree, scale=0.125)
            sl.busy = [t]
            tq.append(t)

        fill = []
        stt = {}

        def level(li):
            if li == 7:
                stt["x"] = None
                return
            hsz = LEVELS[li]
            nb = S // (2 * hsz)
            bv = B[:].rearrange("p t (n w) -> p (t n) w", w=2 * hsz)
            dv = D[:].rearrange("p t (n w) -> p (t n) w", w=2 * hsz)
            ref = bv[:, :, hsz - 1:hsz].broadcast_to([P, 2 * nb, 2 * hsz])
            t = TT(dv, bv, ref, SUB, *tb, *stt.get("dfree", []))
            t = A(D[:], D[:], ACT.Abs, t)
            t = A(D[:], D[:], ACT.Exp, t, scale=-1.0 / 16)
            x = XL[li % 2]
            xv = x.ap[:].rearrange("p t (n w) -> p (t n) w", w=2 * hsz)
            qv = Q[:].rearrange("p t (n w) -> p (t n) w", w=2 * hsz)
            kv = K[:].rearrange("p t (n w) -> p (t n) w", w=2 * hsz)
            TT(xv[:, :, hsz:], dv[:, :, hsz:], qv[:, :, hsz:], MUL, t, *tq, *x.busy, *xfree)
            t = TT(xv[:, :, :hsz], dv[:, :, :hsz], kv[:, :, :hsz], MUL, *tk)
            stt["dfree"] = [t]
            stt["x"] = (x, t)

        def level_head(li, hd):
            t_, hh = hd // 2, hd % 2
            sl = pring.take()
            pe.wait(*sl.busy)
            if stt["x"] is None:
                a, b = K, Q
                pe.wait(*tq, *tk)
            else:
                a = b = stt["x"][0].ap
                pe.wait(stt["x"][1])
            for c in range(8):
                cs = slice(P * c, P * c + P)
                f = lambda e, c=c, cs=cs, a=a, b=b: e.matmul(sl.ap[:, cs], a[64 * hh:64 * hh + 64, t_, cs], b[64 * hh:64 * hh + 64, t_, cs], start=True, stop=True)
                t = pe.op(f) if c == 7 else pe.go(f)
            if stt["x"] is not None:
                stt["x"][0].busy = [t]
            t = dve.op(lambda e: e.copy_predicated(v3(AT[:, hd, :], 8), masks[:, li, :].unsqueeze(1).broadcast_to([P, 8, P]), v3(sl.ap[:], 8)), t, tz)
            sl.busy = [t]
            stt["at"] = t

        for li in range(8):
            fill.append(lambda li=li: (level(li), level_head(li, 0)))
            for hd in range(1, 4):
                fill.append(lambda li=li, hd=hd: level_head(li, hd))

        bl = B[:].rearrange("p t (n w) -> p (t n) w", w=P)[:, :, P - 1:P]

        def decays():
            dv = D[:].rearrange("p t (n w) -> p (t n) w", w=P)
            bv = B[:].rearrange("p t (n w) -> p (t n) w", w=P)
            t = A(gx[:].unsqueeze(2), bl, ACT.Exp, *tb, scale=1.0 / 16)
            stt["dec"] = t
            t = A(QI[:], B[:], ACT.Exp, *tb, *xfree, scale=1.0 / 16)
            stt["qi"] = TT(QI[:], QI[:], Q[:], MUL, t, *tq)
            t = TT(dv, bv, bl.broadcast_to([P, 16, P]), SUB, *stt["dfree"])
            t = A(D[:], D[:], ACT.Exp, t, scale=-1.0 / 16)
            stt["kd"] = TT(D[:], D[:], K[:], MUL, t)
            t = TT(EM[:], BM[:], BM[:, :, NMETA - 1:NMETA].broadcast_to([P, 2, NMETA]), SUB, tb[-1])
            t = A(EM[:], EM[:], ACT.Exp, t, scale=-1.0 / 16)
            stt["kdm"] = TT(EM[:], EM[:], KM[:], MUL, t, *tk)
            stt["xl"] = [pe.last]

        def kd_turn(m):
            sl = pring.take()
            pe.wait(stt["kd"], *sl.busy)
            for c in range(8):
                f = lambda e, c=c: e.transpose(sl.ap[:, P * c:P * c + P], D[:, m, P * c:P * c + P], ident[:])
                t = pe.op(f) if c == 7 else pe.go(f)
            t = A(KDT[:, :, P * m:P * m + P], v3(sl.ap[:], 8), ACT.Copy, t, *stt["xl"])
            sl.busy = [t]
            stt[f"kdt{m}"] = t

        def meta_state():
            sl = pring.take()
            pe.wait(stt["kdm"], *sl.busy)
            for m in range(2):
                t = pe.op(lambda e, m=m: e.transpose(sl.ap[0:NMETA, P * m:P * m + P], EM[:, m, :], ident[:]))
            t = CP(KDM[:], sl.ap[0:NMETA, 0:256], t)
            sl.busy = [t]
            kv_mm(0, lambda h: KDM[0:NMETA, 64 * h:64 * h + 64], lambda h: VM[0:NMETA, P * h:P * h + P], t, stt["vm"])

        def kv_mm(c, lhs, rhs, *w):
            sl = pring.take()
            pe.wait(*w, *sl.busy)
            for hd in range(4):
                t_, hh = hd // 2, hd % 2
                f = lambda e, hd=hd, t_=t_, hh=hh: e.matmul(sl.ap[64 * hh:64 * hh + 64, P * t_:P * t_ + P], lhs(hd), rhs(hd), start=True, stop=True)
                t = pe.op(f) if hd == 3 else pe.go(f)
            if c == 0:
                t = CP(SA[:, 0, :], sl.ap[:, 0:256], t, *stt["xl"])
            else:
                for m in range(2):
                    tt = STT(SA[:, c, P * m:P * m + P], SA[:, c - 1, P * m:P * m + P], gx[:, 8 * m + c - 1:8 * m + c],
                             sl.ap[:, P * m:P * m + P], MUL, ADD, t, stt["dec"], stt["s"])
                t = tt
            sl.busy = [t]
            stt["s"] = t

        fill.append(decays)
        fill.append(lambda: kd_turn(0))
        fill.append(lambda: kd_turn(1))
        fill.append(meta_state)
        for c in range(1, 8):
            fill.append(lambda c=c: kv_mm(c, lambda h: KDT[:, c - 1, 64 * h:64 * h + 64],
                                          lambda h: V[:, c - 1, P * h:P * h + P], stt["kdt0"], stt["kdt1"], stt["v"]))

        def fills(n):
            for _ in range(n):
                if fill:
                    fill.pop(0)()

        for m in range(4):
            sl, tok = job_tm(f"v{m}", h, 8, meta=True)
            t = A(V[:, :, P * m:P * m + P], v3(sl.ap[:], 8), ACT.Copy, tok, *gfree)
            sl.busy = [t]
            stt["v"] = t
            t = CP(VM[:, P * m:P * m + P], misc.ap[0:NMETA, 0:P], tok)
            stt["vm"] = t
            misc.busy = [t]
            fills(3)
        dsg = [Dsem(f"sg{m}") for m in range(4)]
        tsg = []
        for m in range(4):
            sl, tok = job(f"g{m}", h, 8)
            b = tring.take()
            t = A(b.ap[:], sl.ap[:], ACT.Silu, tok, *b.busy)
            sl.busy = [t]
            t = dma(sp, dsg[m], sgsc[:, m, :], b.ap[:], t)
            b.busy = [t]
            tsg.append(t)
            fills(3)
        dyc = [Dsem(f"yc{m}") for m in range(4)]
        tyc = []
        ufree = list(xfree)
        for m in range(4):
            def cw(k, m=m):
                return col("conv1", 3 * m + k)
            sl, tok = job(f"cc{m}", h, 8, meta=True)
            t = A(U[:, 2:], sl.ap[:], ACT.Copy, tok, *ufree)
            sl.busy = [t]
            tc2 = A(U[:, 0:2], misc.ap[:, NMETA - 2:NMETA], ACT.Copy, tok, *ufree)
            misc.busy = [tc2]
            fills(2)
            sl, tok = job(f"cx{m}", h, 8, meta=True)
            t = TT(U[:, 2:], U[:, 2:], sl.ap[:], MUL, tok, t)
            sl.busy = [t]
            t2 = TT(U[:, 0:2], U[:, 0:2], misc.ap[:, NMETA - 2:NMETA], MUL, tok, tc2)
            misc.busy = [t2]
            b = tring.take()
            t3 = A(b.ap[:], U[:, 2:], ACT.Copy, t, *b.busy, scale=cw(2))
            t4 = STT(b.ap[:], U[:, 1:1025], cw(1), b.ap[:], MUL, ADD, t3, t2)
            t5 = STT(b.ap[:], U[:, 0:1024], cw(0), b.ap[:], MUL, ADD, t4)
            ufree = [t5, t3]
            fills(2)
            sl, tok = job(f"cb{m}", h, 8)
            t = TT(b.ap[:], b.ap[:], sl.ap[:], MUL, tok, t5)
            sl.busy = [t]
            t = dma(sp, dyc[m], ysc[:, 4 + m, :], b.ap[:], t)
            b.busy = [t]
            tyc.append(t)
            fills(3)
        fills(len(fill))
        hfree = [pe.last]
        SG, Y = unit(HO, 0, [P, 4, S]), unit(HO, 4, [P, 8, S])
        dl = Dsem("sgl")
        tl = dma(sp, dl, SG[:], sgsc, *tsg, *hfree)
        dl2 = [Dsem(f"yl{m}") for m in range(4)]
        tyl = [dma(sp, dl2[m], Y[:, 4 + m, :], ysc[:, 4 + m, :], tyc[m], *hfree) for m in range(4)]
        st4 = Ring([Slot(st[:, 0:4]), Slot(st[:, 4:8])])
        yt = []

        def o_front(c):
            sl = pring.take()
            pe.wait(stt["at"], stt["qi"], stt["v"], stt["s"], *sl.busy)
            cs = slice(P * c, P * c + P)
            for hd in range(4):
                t_, hh = hd // 2, hd % 2
                oc = 512 * hh + P * t_
                pe.go(lambda e, hd=hd, oc=oc: e.matmul(sl.ap[:, oc:oc + P], AT[:, hd, cs], V[:, c, P * hd:P * hd + P], start=True, stop=False))
                f = lambda e, oc=oc, t_=t_, hh=hh: e.matmul(sl.ap[:, oc:oc + P], QI[64 * hh:64 * hh + 64, t_, cs], SA[64 * hh:64 * hh + 64, c, P * t_:P * t_ + P], start=False, stop=True)
                t = pe.op(f) if hd == 3 else pe.go(f)
            b = tring.take()
            s4 = st4.take()
            act.wait(*b.busy, *s4.busy)
            for hd in range(4):
                oc = 512 * (hd // 2) + P * (hd % 2)
                t5 = A(b.ap[:, 512 + P * hd:512 + P * hd + P], sl.ap[:, oc:oc + P], ACT.Square, t, accum=s4.ap[:, hd:hd + 1])
            t5 = A(s4.ap, s4.ap, ACT.Sqrt, t5, scale=1.0 / P, bias=epsc[:])
            t5 = dve.op(lambda e: e.reciprocal(s4.ap, s4.ap), t5)
            t5 = TT(b.ap[:, 0:512].rearrange("p (a b c) -> p a b c", a=2, b=2),
                    sl.ap[:].rearrange("p (a b c) -> p a b c", a=2, b=4)[:, :, 0:2, :],
                    s4.ap.rearrange("p (a b) -> p a b", a=2).unsqueeze(3).broadcast_to([P, 2, 2, P]), MUL, t5, *b.busy)
            sl.busy = [t5]
            s4.busy = [t5]
            return b, t5

        def o_back(c, b, t5):
            cs = slice(P * c, P * c + P)
            s2 = pring.take()
            pe.wait(t5, *s2.busy)
            for hd in range(4):
                at_ = P * (2 * (hd % 2) + hd // 2)
                f = lambda e, hd=hd, at_=at_: e.transpose(s2.ap[:, P * hd:P * hd + P], b.ap[:, at_:at_ + P], ident[:])
                t = pe.op(f) if hd == 3 else pe.go(f)
            b.busy = [t]
            t = STT(Y[:, 0:4, cs], v3(s2.ap[:, 0:512], 4), col("gla_norm"), SG[:, :, cs], MUL, MUL, t, tl)
            s2.busy = [t]
            return t

        prev = None
        for c in range(8):
            cur = (c, *o_front(c))
            if prev:
                ty = o_back(*prev)
            prev = cur
        ty = o_back(*prev)
        gfree = [pe.last, ty]
        toks = []
        for k in list(range(4, 8)) + list(range(4)):
            toks.append((k, split(Y[:, k, :], GH[:, k, :], GL[:, k, :], *(gfree if k >= 4 else [ty]), *([tyl[k - 4]] if k >= 4 else []))))
        toks = [t for _, t in sorted(toks)]
        xfree = [pe.last, dve.last, act.last]
        xt = [dma(sp, dx[k], X[:, k, :], d["xT"][:, k, :], *xfree) for k in range(8)]
        yr = Rhs(GH, GL, toks)

        def add_to_x(name, r, toks):
            res = []
            for m in range(8):
                sl, tok = job(f"{name}{m}", r, 8)
                t = TT(X[:, m, :], sl.ap[:], X[:, m, :], ADD, tok, toks[m])
                sl.busy = [t]
                res.append(t)
            return res

        xt = add_to_x("wo", yr, xt)
        hidden["free"] = [[pe.last], [pe.last]]
        tR = norm_R(xs, xt, 1024)
        h = normed(xs, lambda k: col("norm_mlp", k), tR, HH, HL, ty, toks[-1], toks[3])

        def relu_up(name, h):
            def one(j):
                sl, tok = job(f"{name}{j}", h, 8)
                return drain_relu2(sl, tok, j)
            return one

        xt = mlp("up", "dn", h, 8, 8, relu_up("up", h), X, [[t] for t in xt])
        tR = norm_R(xs, xt, 1024)
        xt = normed_in_place(xs, lambda k: col("norm_final", k), tR)

        if upto >= 2:
            tspill = [dma(sp, dx[k], xsc[:, k, :], X[:, k, :], xt[k]) for k in range(8)]
            gfree = [pe.last]
            tR = norm_R(xs, xt, 1024)
            h = normed(xs, lambda k: col("ln1", k), tR, HH, HL, pe.last)
            xfree = [*tspill, dve.last, act.last]
            QA, KA, QB, KB = G(0, [P, 3, S]), G(3, [P, 3, S]), G(6, [P, 3, S]), G(9, [P, 3, S])
            VA, CF = G(12, [P, 8, 384]), G(15, [P, S])
            UC, YC, VB = unit(XO, 0, [P, 2, 1054]), unit(XO, 3, [P, 2, S]), unit(XO, 5, [P, 8, 384])
            tpad = pool.op(lambda e: e.memset(UC[:, :, 0:30], 0.0), *xfree)
            ctok = [None, None]
            for m in range(2):
                sl, tok = job(f"gg{m}", h, 8)
                b = tring.take()
                t = A(b.ap[:], sl.ap[:], ACT.Sigmoid, tok, *b.busy)
                sl.busy = [t]
                sl, tok = job(f"gv{m}", h, 8)
                t = TT(UC[:, m, 30:], b.ap[:], sl.ap[:], MUL, tok, t, *xfree)
                sl.busy = [t]
                b.busy = [t]
                ctok[m] = A(YC[:, m, :], UC[:, m, 30:], ACT.Identity, t, *xfree, scale=col("conv2", 31 * m + 30), bias=col("conv2_b", m))
            dve.wait(tpad)

            def taps(m, k0, k1):
                for k in range(k0, k1):
                    ctok[m] = STT(YC[:, m, :], UC[:, m, k:k + S], col("conv2", 31 * m + k), YC[:, m, :], MUL, ADD, ctok[m])

            def ln_mean():
                pe.wait(*ctok, *misc.busy)
                for hf in range(2):
                    cs = slice(512 * hf, 512 * hf + 512)
                    for m in range(2):
                        t = pe.op(lambda e, m=m, cs=cs: e.matmul(misc.ap[:, cs], ones[:], YC[:, m, cs], start=(m == 0), stop=(m == 1)))
                for m in range(2):
                    ctok[m] = STT(YC[:, m, :], misc.ap[:], -1.0 / 256, YC[:, m, :], MUL, ADD, t)
                misc.busy = [dve.last]

            def ln_rest():
                tR = norm_R([YC[:, 0, :], YC[:, 1, :]], ctok, 256)
                for m in range(2):
                    t = STT(YC[:, m, :], YC[:, m, :], col("cn_g", m), misc.ap[:], MUL, MUL, tR)
                    ctok[m] = A(YC[:, m, :], YC[:, m, :], ACT.Silu, t, bias=col("cn_b", m))
                misc.busy = [dve.last]

            fill = []
            for m in range(2):
                for k in range(0, 30, 5):
                    fill.append(lambda m=m, k=k: taps(m, k, k + 5))
            fill += [ln_mean, ln_rest]

            sl, tok = job("fa", h, 8, m=W2)
            a6, b6, o6 = T[0], T[1], T[2]
            for s_ in (a6, b6, o6):
                act.wait(*s_.busy)
                dve.wait(*s_.busy)
            g_, ta, tb_ = logsig(sl.ap[0:6, :], cols[0:6, COLS["b_forget"][0]:COLS["b_forget"][0] + 1], a6.ap[0:6, :], b6.ap[0:6, :], a6.ap[0:6, :], tok)
            sl.busy = [tb_]
            t1 = dve.op(lambda e: e.memset(o6.ap[0:6, :], 1.0))
            tcf = dve.op(lambda e: e.tensor_tensor_scan(CF[0:6, :], o6.ap[0:6, :], a6.ap[0:6, :], 0.0, MUL, ADD), t1, g_, *gfree)
            for s_ in (a6, b6, o6):
                s_.busy = [tcf]
            tq2 = []

            def proj(n, dst, scale=1.0):
                for m in range(3):
                    sl, tok = job(f"{n}{m}", h, 8)
                    t = A(dst[:, m, :], sl.ap[:], ACT.Copy, tok, *gfree, scale=scale)
                    sl.busy = [t]
                    fills(1)
                return t

            def projv(n, dst, *w):
                for m in range(3):
                    sl, tok = job_tm(f"{n}{m}", h, 8)
                    t = A(dst[:, :, P * m:P * m + P], v3(sl.ap[:], 8), ACT.Copy, tok, *w)
                    sl.busy = [t]
                    fills(1)
                return t

            projv("vb", VB, *xfree)
            tvb = act.last
            vsc = nc.dram_tensor("vsc", (S, 384), F, kind="Internal").ap()
            dv_ = Dsem("vs")
            tvs = dma(sp, dv_, vsc.rearrange("(b p) c -> p b c", p=P), VB[:], tvb)
            proj("qa", QA, 0.125)
            proj("ka", KA)
            projv("va", VA, *gfree)
            proj("qb", QB, 0.125)
            proj("kb", KB)
            fills(len(fill))
            tproj = act.last
            hfree = [pe.last]

            def Hu(n, shape, dt=F):
                return unit(HO, n, shape, dt)

            sring = Ring([Slot(Hu(0, [P, S])), Slot(Hu(1, [P, S]))])
            prng = Ring([Slot(Hu(2, [P, S])), Slot(Hu(3, [P, S]))])
            ptring = Ring([Slot(Hu(4, [P, S])), Slot(Hu(5, [P, S]))])
            CN = Hu(6, [P, 6, S])
            SEL = Hu(12, [6, 6, P])
            V4, V16 = Hu(13, [P, 8, 384]), unit(XO, 0, [P, 8, 384])
            dsel, dv4, dv16 = Dsem("sel"), Dsem("v4"), Dsem("v16")
            tsel = dma(sp, dsel, SEL[:], d["sel"], *hfree)
            for n in range(2):
                tv4 = dma(sp, dv4, V4[:, 4 * n:4 * n + 4, :], vsc[512 * n:512 * n + 512, :].rearrange("(j r) c -> j r c", r=4), tvs, *hfree)
            tv16 = dma(sp, dv16, V16[:], vsc.rearrange("(j u) c -> j u c", u=8), tvs, *ctok)
            for hd in range(6):
                pe.wait(tsel, tcf, *misc.busy)
                for hf in range(2):
                    t = pe.op(lambda e, hf=hf, hd=hd: e.matmul(misc.ap[:, 512 * hf:512 * hf + 512], SEL[0:6, hd, :], CF[0:6, 512 * hf:512 * hf + 512], start=True, stop=True))
                tcn = A(CN[:, hd, :], misc.ap[:], ACT.Copy, t, *hfree, scale=-1.0)
                misc.busy = [tcn]
            stat = Ring([Slot(st), Slot(rr)])
            mhalf = [Slot(misc.ap[:, 0:512]), Slot(misc.ap[:, 512:1024])]
            mhalf[0].busy = mhalf[1].busy = [tcn]
            lz = const([P, 16])
            lzs = [Slot(lz[:, 0:8]), Slot(lz[:, 8:16])]
            dys = [Dsem(f"ys{i}") for i in range(3)]
            ystoks = {}
            yring = Ring([Slot(CF[:, 0:512]), Slot(CF[:, 512:1024])])
            for s_ in yring.slots:
                s_.busy = [tcn]

            def pt_copy(n, dst, src, *w):
                if n % 2:
                    return A(dst, src, ACT.Copy, *w)
                return CP(dst, src, *w)

            def rms_rows(b, i, gname, f0, t, *w):
                s_ = stat.take()
                b2 = yring.take()
                t2 = A(b2.ap[:, 0:384], b.ap[:, 0:384], ACT.Square, t, *b2.busy, *s_.busy, accum=s_.ap[:, 0:1])
                t2 = A(s_.ap[:, 1:2], s_.ap[:, 0:1], ACT.Sqrt, t2, scale=1.0 / 384, bias=epsc[:])
                t2 = dve.op(lambda e: e.reciprocal(s_.ap[:, 2:3], s_.ap[:, 1:2]), t2)
                t2 = TS(b.ap[:, 0:384], b.ap[:, 0:384], s_.ap[:, 2:3], None, MUL, None, t2)
                s_.busy = [t2]

                def back():
                    sl = pring.take()
                    pe.wait(t2, *sl.busy)
                    for m in range(3):
                        f = lambda e, m=m: e.transpose(sl.ap[:, P * m:P * m + P], b.ap[:, P * m:P * m + P], ident[:])
                        t = pe.op(f) if m == 2 else pe.go(f)
                    b.busy = [t]
                    for m in range(3):
                        t3 = TS(b2.ap[:, P * m:P * m + P], sl.ap[:, P * m:P * m + P], col(gname, m), None, MUL, None, t)
                    sl.busy = [t3]
                    k = len(ystoks) % 3
                    t4 = dma(sp, dys[k], ysc[:, f0:f0 + 3, P * i:P * i + P], v3(b2.ap[:, 0:384], 3), t3)
                    b2.busy = [t4]
                    ystoks[(gname, i)] = t4
                return back

            units = [(i, hd) for i in range(8) for hd in range(6)]

            def scores(i, hd):
                t_, hh = hd // 2, hd % 2
                ps_ = slice(64 * hh, 64 * hh + 64)
                w = P * (i + 1)
                sl = pring.take()
                pe.wait(tproj, *sl.busy)
                for hf in range(-(-w // 512)):
                    n = min(512, w - 512 * hf)
                    diag = hf == (P * i) // 512
                    pe.go(lambda e, hf=hf, n=n, diag=diag: e.matmul(sl.ap[:, 512 * hf:512 * hf + n], QA[ps_, t_, P * i:P * i + P], KA[ps_, t_, 512 * hf:512 * hf + n], start=True, stop=not diag))
                t = pe.op(lambda e: e.matmul(sl.ap[:, P * i:P * i + P], identb[:], negm[:, 0, :], start=False, stop=True))
                return sl, t

            def soft(i, hd, sl, t):
                w = P * (i + 1)
                s_, p_ = sring.take(), prng.take()
                l_ = lzs[i % 2]
                mx = stat.take()
                t = dve.op(lambda e: e.tensor_tensor_reduce(out=s_.ap[:, 0:w], in0=sl.ap[:, 0:w], in1=CN[:, hd, 0:w], scale=-1.0, scalar=3.0e38, op0=ADD, op1=MIN, accum_out=mx.ap[:, 0:1]), t, tcn, *s_.busy, *mx.busy)
                sl.busy = [t]
                t = A(p_.ap[:, 0:w], s_.ap[:, 0:w], ACT.Exp, t, *p_.busy, *(l_.busy if hd == 0 else []), scale=-1.0, bias=mx.ap[:, 0:1], accum=l_.ap[:, hd:hd + 1])
                s_.busy = [t]
                mx.busy = [t]
                return p_, t

            def turn(blocks, p_, t, n):
                sl = pring.take()
                pe.wait(t, *sl.busy)
                for j in range(blocks):
                    f = lambda e, j=j: e.transpose(sl.ap[:, P * j:P * j + P], p_.ap[:, P * j:P * j + P], ident[:])
                    t = pe.op(f) if j == blocks - 1 else pe.go(f)
                p_.busy = [t]
                q_ = ptring.take()
                t = pt_copy(n, q_.ap[:, 0:P * blocks], sl.ap[:, 0:P * blocks], t, *q_.busy)
                sl.busy = [t]
                return q_, t

            def fox_pv(i, hd, q_, t):
                mh = mhalf[i % 2]
                pe.wait(t, *(mh.busy if hd == 0 else []))
                for j in range(i + 1):
                    f = lambda e, j=j: e.matmul(mh.ap[:, 64 * hd:64 * hd + 64], q_.ap[:, P * j:P * j + P], VA[:, j, 64 * hd:64 * hd + 64], start=(j == 0), stop=(j == i))
                    t = pe.op(f) if j == i else pe.go(f)
                q_.busy = [t]
                return t

            def fox_out(i, t):
                mh, l_ = mhalf[i % 2], lzs[i % 2]
                b = tring.take()
                t2 = dve.op(lambda e: e.reciprocal(l_.ap[:, 0:6], l_.ap[:, 0:6]), act.last)
                t2 = TT(v3(b.ap[:, 0:384], 6), v3(mh.ap[:, 0:384], 6), l_.ap[:, 0:6].unsqueeze(2).broadcast_to([P, 6, 64]), MUL, t2, t, *b.busy)
                mh.busy = [t2]
                l_.busy = [t2]
                return rms_rows(b, i, "fox", 0, t2)

            stage = {}
            backs = []
            n = len(units)
            for s_i in range(n + 3):
                if s_i < n:
                    stage[s_i] = scores(*units[s_i])
                if s_i >= 1 and s_i - 1 < n:
                    stage[s_i - 1] = soft(*units[s_i - 1], *stage[s_i - 1])
                if s_i >= 2 and s_i - 2 < n:
                    u = units[s_i - 2]
                    stage[s_i - 2] = turn(u[0] + 1, *stage[s_i - 2], s_i)
                if s_i >= 3:
                    u = units[s_i - 3]
                    t = fox_pv(*u, *stage.pop(s_i - 3))
                    if backs and u[1] == 2:
                        backs.pop()()
                    if u[1] == 5:
                        backs.append(fox_out(u[0], t))
            while backs:
                backs.pop()()

            dsc = nc.dram_tensor("dsc", (3, S, 396), F, kind="Internal").ap()
            ddo = [Dsem(f"do{i}") for i in range(3)]

            def dtok(ap, br, u, prev):
                if br == 0:
                    return ap[:, P * (u - prev):P * u + P]
                if br == 1:
                    n_, r_ = u // 4, u % 4
                    return ap.rearrange("p (j r) -> p r j", r=4)[:, r_, P * (n_ - prev):P * n_ + P]
                return ap.rearrange("p (j u) -> p u j", u=8)[:, u, :]

            dun = [(br, u, t_) for br in range(3) for u in range(8) for t_ in range(3)]

            def has_prev(br, u):
                return int((br == 0 and u > 0) or (br == 1 and u >= 4))

            def dscores(br, u, t_):
                pv_ = has_prev(br, u)
                w = P * (1 + pv_)
                sl = pring.take()
                pe.wait(tproj, *sl.busy)
                for hh in range(2):
                    ps_ = slice(64 * hh, 64 * hh + 64)
                    q_ = dtok(QB[ps_, t_, :], br, u, 0)
                    k_ = dtok(KB[ps_, t_, :], br, u, pv_)
                    o_ = sl.ap[:, 512 * hh:512 * hh + w]
                    pe.go(lambda e, o_=o_, q_=q_, k_=k_: e.matmul(o_, q_, k_, start=True, stop=False))
                for hh in range(2):
                    if pv_:
                        pe.go(lambda e, hh=hh: e.matmul(sl.ap[:, 512 * hh:512 * hh + P], identb[:], negm[:, 1, :], start=False, stop=False))
                    mk = 2 if br == 2 else 0
                    f = lambda e, hh=hh, mk=mk: e.matmul(sl.ap[:, 512 * hh + w - P:512 * hh + w], identb[:], negm[:, mk, :], start=False, stop=True)
                    t = pe.op(f) if hh == 1 else pe.go(f)
                return sl, t

            dcur = {}

            def dsoft(br, u, t_, sl, t):
                w = P * (1 + has_prev(br, u))
                if t_ == 0:
                    dcur[(br, u)] = tring.take()
                    act.wait(*dcur[(br, u)].busy)
                    dve.wait(*dcur[(br, u)].busy)
                o_ = dcur[(br, u)]
                p_ = prng.take()
                sv = v3(sl.ap[:], 2)[:, :, 0:w]
                t = dve.op(lambda e: e.tensor_reduce(o_.ap[:, 384 + 2 * t_:386 + 2 * t_], sv, AX.X, MAX, negate=True), t)
                for hh in range(2):
                    c_ = 2 * t_ + hh
                    t2 = A(p_.ap[:, w * hh:w * hh + w], sl.ap[:, 512 * hh:512 * hh + w], ACT.Exp, t, *p_.busy, bias=o_.ap[:, 384 + c_:385 + c_], accum=o_.ap[:, 390 + c_:391 + c_])
                sl.busy = [t2]
                return p_, t2

            def dpv(br, u, t_, q_, t, cnt):
                nb = 1 + has_prev(br, u)
                mh = mhalf[cnt % 2]
                pe.wait(t, tv4, tv16, *(mh.busy if t_ == 0 else []))
                for hh in range(2):
                    hd = 2 * t_ + hh
                    for j in range(nb):
                        if br == 0:
                            v_ = VB[:, u - nb + 1 + j, :]
                        elif br == 1:
                            v_ = V4[:, 4 * (u // 4 - nb + 1 + j) + u % 4, :]
                        else:
                            v_ = V16[:, u, :]
                        f = lambda e, hd=hd, j=j, hh=hh, v_=v_: e.matmul(mh.ap[:, 64 * hd:64 * hd + 64], q_.ap[:, P * (nb * hh + j):P * (nb * hh + j) + P], v_[:, 64 * hd:64 * hd + 64], start=(j == 0), stop=(j == nb - 1))
                        t = pe.op(f) if hh == 1 and j == nb - 1 else pe.go(f)
                q_.busy = [t]
                return t

            def dout_(br, u, t, cnt):
                mh = mhalf[cnt % 2]
                o_ = dcur.pop((br, u))
                t = CP(o_.ap[:, 0:384], mh.ap[:, 0:384], t)
                mh.busy = [t]
                ds = ddo[cnt % 3]
                if br == 0:
                    t = dma(sp, ds, dsc[0, P * u:P * u + P, :], o_.ap[:, 0:396], t, act.last)
                elif br == 1:
                    n_, r_ = u // 4, u % 4
                    t = dma(sp, ds, dsc[1, 512 * n_:512 * n_ + 512, :].rearrange("(j r) c -> r j c", r=4)[r_], o_.ap[:, 0:396], t, act.last)
                else:
                    t = dma(sp, ds, dsc[2].rearrange("(j u) c -> u j c", u=8)[u], o_.ap[:, 0:396], t, act.last)
                o_.busy = [t]
                return t

            n = len(dun)
            dall = {}
            for s_i in range(n + 3):
                if s_i < n:
                    stage[s_i] = dscores(*dun[s_i])
                if s_i >= 1 and s_i - 1 < n:
                    stage[s_i - 1] = dsoft(*dun[s_i - 1], *stage[s_i - 1])
                if s_i >= 2 and s_i - 2 < n:
                    u = dun[s_i - 2]
                    stage[s_i - 2] = turn(2 * (1 + has_prev(u[0], u[1])), *stage[s_i - 2], s_i)
                if s_i >= 3:
                    u = dun[s_i - 3]
                    cnt = u[0] * 8 + u[1]
                    t = dpv(*u, *stage.pop(s_i - 3), cnt)
                    if u[2] == 2:
                        dall[cnt % 3] = dout_(u[0], u[1], t, cnt)

            cm = [Slot(Hu(6, [P, 3, S])), Slot(Hu(9, [P, 3, S]))]
            dcm = [Dsem("cm0"), Dsem("cm1")]
            cfree = [dve.last]
            loaded = []
            for i, c_ in enumerate(cm):
                if True:
                    loaded.append((c_, dma(sp, dcm[i], c_.ap[:, :, 0:396], dsc[:, P * i:P * i + P, :].rearrange("a p c -> p a c"), *dall.values(), *cfree)))
            pend = None
            for i in range(8):
                c_, tl_ = loaded[i]
                C = c_.ap
                mm_, ll_ = C[:, :, 384:390], C[:, :, 390:396]
                t = TT(C[:, 0, 400:406], mm_[:, 0, :], mm_[:, 1, :], MIN, tl_)
                t = TT(C[:, 0, 400:406], C[:, 0, 400:406], mm_[:, 2, :], MIN, t)
                t = TT(C[:, :, 410:416], C[:, 0:1, 400:406].broadcast_to([P, 3, 6]), mm_, SUB, t)
                t = A(C[:, :, 410:416], C[:, :, 410:416], ACT.Exp, t)
                t1 = TT(C[:, :, 420:426], C[:, :, 410:416], ll_, MUL, t)
                t1 = TT(C[:, 0, 420:426], C[:, 0, 420:426], C[:, 1, 420:426], ADD, t1)
                t1 = TT(C[:, 0, 420:426], C[:, 0, 420:426], C[:, 2, 420:426], ADD, t1)
                t1 = dve.op(lambda e, C=C: e.reciprocal(C[:, 0, 430:436], C[:, 0, 420:426]), t1)
                for br in range(3):
                    v_ = v3(C[:, br, 0:384], 6)
                    t2 = TT(v_, v_, C[:, br, 410:416].unsqueeze(2).broadcast_to([P, 6, 64]), MUL, t)
                t2 = TT(C[:, 0, 0:384], C[:, 0, 0:384], C[:, 1, 0:384], ADD, t2)
                t2 = TT(C[:, 0, 0:384], C[:, 0, 0:384], C[:, 2, 0:384], ADD, t2)
                b = tring.take()
                t2 = TT(v3(b.ap[:, 0:384], 6), v3(C[:, 0, 0:384], 6), C[:, 0, 430:436].unsqueeze(2).broadcast_to([P, 6, 64]), MUL, t2, t1, *b.busy)
                if i + 2 < 8:
                    loaded.append((c_, dma(sp, dcm[i % 2], c_.ap[:, :, 0:396], dsc[:, P * (i + 2):P * (i + 3), :].rearrange("a p c -> p a c"), t2)))
                nxt = rms_rows(b, i, "dil", 3, t2)
                if pend:
                    pend()
                pend = nxt
            pend()

            Y2 = Hu(0, [P, 6, S])
            dl3 = Dsem("y2l")
            tyl = dma(sp, dl3, Y2[:], ysc[:, 0:6, :], *ystoks.values(), pe.last, act.last, dve.last)
            toks = []
            gfree = [pe.last, *ystoks.values()]
            t67 = [split(YC[:, k, :], GH[:, 6 + k, :], GL[:, 6 + k, :], ctok[k], *gfree) for k in range(2)]
            toks = [split(Y2[:, k, :], GH[:, k, :], GL[:, k, :], tyl, *gfree) for k in range(6)] + t67
            xfree = [pe.last, *t67, tv16]
            xt = [dma(sp, dx[k], X[:, k, :], xsc[:, k, :], *xfree) for k in range(8)]
            misc.busy = [dve.last, act.last]
            xt = add_to_x("w2o", Rhs(GH, GL, toks), xt)
            hidden["free"] = [[pe.last], [pe.last]]
            tR = norm_R(xs, xt, 1024)
            h = normed(xs, lambda k: col("ln2", k), tR, HH, HL, *toks)
            SC = const([P, 8])
            tsc = A(SC[:], col("c", 0, 8), ACT.Silu)

            def gated(m):
                def conv(name, f, tok_w=()):
                    sl, tok = job(name, h, 8)
                    b = tring.take()
                    t = A(b.ap[:], sl.ap[:], ACT.Identity, tok, *b.busy, scale=col("ffn_w", 3 * f + 2), bias=col("ffn_b", f))
                    t = STT(b.ap[:, 1:], sl.ap[:, 0:S - 1], col("ffn_w", 3 * f + 1), b.ap[:, 1:], MUL, ADD, t)
                    t = STT(b.ap[:, 2:], sl.ap[:, 0:S - 2], col("ffn_w", 3 * f), b.ap[:, 2:], MUL, ADD, t)
                    sl.busy = [t]
                    return b, t
                a_, ta = conv(f"fupa{m}", m)
                ta = A(a_.ap[:], a_.ap[:], ACT.Silu, ta)
                b_, tb2 = conv(f"fupb{m}", NPAIR + m)
                t = TT(a_.ap[:], a_.ap[:], b_.ap[:], MUL, ta, tb2)
                b_.busy = [t]
                if m < 16 and upto >= 3:
                    for q in range(3):
                        f = 3 * m + q
                        i = ws.take(f"ada{f}")
                        pe.wait(ws.landed[i], tsc, *(misc.busy if f == 0 else []))
                        for k in range(8):
                            g_ = lambda e, i=i, k=k, f=f: e.matmul(misc.ap[:, f:f + 1], raw[i % 3][:, P * k:P * k + P], SC[:, k:k + 1], start=(k == 0), stop=(k == 7))
                            tm_ = pe.op(g_) if k == 7 else pe.go(g_)
                        ws.done(i, tm_)
                    if m == 15:
                        stt["mod"] = TT(mod[:], misc.ap[:, 0:48], col("b_ada", 0, 48), ADD, tm_)
                        misc.busy = [stt["mod"]]
                return a_, t

            xt = mlp("fup", "fdn", h, 6, 8, gated, X, [[t] for t in xt], sizes=[4] * 5 + [2])
            tR = norm_R(xs, xt, 1024)
            xt = normed_in_place(xs, lambda k: col("g_final", k), tR)
        if upto >= 3:
            gains = const([P, 32])
            for j, (m0, name, one) in enumerate(((8, "n1pre", 1.0), (16, "n1post", 0.0), (32, "n2pre", 1.0), (40, "n2post", 0.0))):
                tg = STT(gains[:, 8 * j:8 * j + 8], mod[:, m0:m0 + 8], one, col(name, 0, 8), ADD, MUL, stt["mod"])

            def gain(j):
                return lambda k: gains[:, 8 * j + k:8 * j + k + 1]

            hfree, gfree = [pe.last], [pe.last, tg]
            UU, VT, YB, MIX = G(0, [P, 4, S]), G(4, [P, 8, 512]), G(8, [P, 4, S]), G(8, [P, 8, S])
            so = GO + 12 * 4096
            WSP, BSP, GNB, BNB, WPL = (at(so + 2048 * i, [P, 512]) for i in range(5))
            TRI = at(so + 10240, [P, P])
            BST = at(so + 10752, [P, 8, 6])
            MV = at(so + 10752 + 192, [P, 8, 2])
            RV = at(so + 10752 + 256, [P, 8])
            PBI = at(so + 10752 + 288, [P, 4])
            ds3 = Dsem("b3")
            dma(sp, ds3, v3(WSP[:], 4), d["w_sp"], *gfree)
            dma(sp, ds3, v3(WPL[:], 4), d["w_pool"], *gfree)
            dma(sp, ds3, TRI[:], d["tri"], *gfree)
            dma(sp, ds3, v3(BSP[:], 4), d["b_sp"].unsqueeze(0).broadcast_to([P, 4, P]), *gfree)
            dma(sp, ds3, GNB[:], d["lnv_g"].unsqueeze(0).broadcast_to([P, 512]), *gfree)
            t3 = dma(sp, ds3, BNB[:], d["lnv_b"].unsqueeze(0).broadcast_to([P, 512]), *gfree)
            tR = norm_R(xs, xt, 1024)
            h = normed(xs, gain(0), tR, HH, HL, *hfree, shift=lambda k: mod[:, k:k + 1])
            twsp = TT(v3(WSP[:], 4), v3(WSP[:], 4), TRI[:].unsqueeze(1).broadcast_to([P, 4, P]), MUL, t3)
            tpb = TT(PBI[:], col("b_pool", 0, 4), col("pscale", 0, 4), MUL, t3)

            for m in range(4):
                sl, tok = job_tm(f"zv{m}", h, 8)
                tv = A(VT[:, :, P * m:P * m + P], v3(sl.ap[:], 8), ACT.Gelu_apprx_tanh, tok, *gfree)
                sl.busy = [tv]

            def ln_rows():
                for c in range(8):
                    t = dve.op(lambda e, c=c: e.bn_stats(BST[:, c, :], VT[:, c, :]), tv, t3)
                for c in range(8):
                    t2 = dve.op(lambda e, c=c: e.bn_aggr(MV[:, c, :], BST[:, c, :]), t)
                t2 = A(RV[:], MV[:, :, 1], ACT.Sqrt, t2, bias=epsc[:])
                t2 = dve.op(lambda e: e.reciprocal(RV[:], RV[:]), t2)
                for c in range(8):
                    t2 = TS(VT[:, c, :], VT[:, c, :], MV[:, c, 0:1], RV[:, c:c + 1], SUB, MUL, t2)
                for hf in range(2):
                    v_ = VT[:, 4 * hf:4 * hf + 4, :]
                    t2 = TT(v_, v_, GNB[:].unsqueeze(1).broadcast_to([P, 4, 512]), MUL, t2)
                    stt["vt"] = TT(v_, v_, BNB[:].unsqueeze(1).broadcast_to([P, 4, 512]), ADD, t2, q=pool)

            utok = {}

            def spatial(m):
                sl = pring.take()
                pe.wait(stt["vt"], twsp, *sl.busy)
                for c in range(8):
                    f = lambda e, c=c: e.matmul(sl.ap[:, P * c:P * c + P], VT[:, c, P * m:P * m + P], WSP[:, P * m:P * m + P], start=True, stop=True)
                    t = pe.op(f) if c == 7 else pe.go(f)
                b = tring.take()
                t = TT(v3(b.ap[:], 8), v3(sl.ap[:], 8), BSP[:, P * m:P * m + P].unsqueeze(1).broadcast_to([P, 8, P]), ADD, t, *b.busy)
                sl.busy = [t]
                utok[m] = TT(UU[:, m, :], UU[:, m, :], b.ap[:], MUL, t, utok[m])
                b.busy = [utok[m]]

            ln_rows()
            for m in range(4):
                sl, tok = job(f"zu{m}", h, 8)
                utok[m] = A(UU[:, m, :], sl.ap[:], ACT.Gelu_apprx_tanh, tok, *gfree)
                sl.busy = [utok[m]]
            ybt = {}
            pend = None

            def pool_out(m, z, t):
                sl = pring.take()
                pe.wait(t, t3, *sl.busy)
                for hf in range(2):
                    cs = slice(512 * hf, 512 * hf + 512)
                    f = lambda e, cs=cs: e.matmul(sl.ap[:, cs], WPL[:, P * m:P * m + P], z.ap[:, cs], start=True, stop=True)
                    t = pe.op(f) if hf else pe.go(f)
                z.busy = [t]
                ybt[m] = A(YB[:, m, :], sl.ap[:], ACT.Identity, t, tpb, *gfree, scale=col("pscale", m), bias=PBI[:, m:m + 1])
                sl.busy = [ybt[m]]

            for m in range(4):
                sl, tok = job(f"zb{m}", h, 8)
                spatial(m)
                z = tring.take()
                t = A(z.ap[:], sl.ap[:], ACT.Copy, tok, *z.busy)
                sl.busy = [t]
                a_ = tring.take()
                b_ = tring.take() if m else None
                src = z
                bufs = [a_, b_]
                dve.wait(*a_.busy, *(b_.busy if b_ else []))
                for j in range(m + 1):
                    s_ = 1 << j
                    o_ = bufs[j % 2]
                    t1 = CP(o_.ap[:, 0:s_], src.ap[:, 0:s_], t)
                    t = TT(o_.ap[:, s_:], src.ap[:, s_:], src.ap[:, 0:S - s_], ADD, t, t1)
                    src = o_
                w_ = 2 << m
                t1 = TT(src.ap[:, 0:16], src.ap[:, 0:16], col("rcnt", 16 * m, 16), MUL, t)
                t1 = TT(z.ap[:, 0:16], src.ap[:, 0:16], z.ap[:, 0:16], SUB, t1)
                t = STT(z.ap[:, 16:], src.ap[:, 16:], 1.0 / w_, z.ap[:, 16:], MUL, SUB, t, t1)
                a_.busy = [t]
                if b_:
                    b_.busy = [t]
                pool_out(m, z, t)
            hfree = [pe.last]
            toks = [split(UU[:, k, :], HH[:, k, :], HL[:, k, :], utok[k], *hfree) for k in range(4)]
            toks += [split(YB[:, k, :], HH[:, 4 + k, :], HL[:, 4 + k, :], ybt[k], *hfree) for k in range(4)]
            yr = Rhs(HH, HL, toks)
            mt = []
            for m in range(8):
                sl, tok = job(f"wo3{m}", yr, 8)
                t = A(MIX[:, m, :], sl.ap[:], ACT.Copy, tok, pool.last)
                sl.busy = [t]
                mt.append(t)
            tR = norm_R([MIX[:, k, :] for k in range(8)], mt, 1024)
            xt2 = []
            for k in range(8):
                b = tring.take()
                t = STT(b.ap[:], MIX[:, k, :], gain(1)(k), misc.ap[:], MUL, MUL, tR, *b.busy)
                t = TT(X[:, k, :], X[:, k, :], b.ap[:], ADD, t)
                b.busy = [t]
                xt2.append(t)
            misc.busy = [t]
            hidden["free"] = [[pe.last, t], [pe.last, t]]
            tR = norm_R(xs, xt2, 1024)
            h = normed(xs, gain(2), tR, HH, HL, pe.last, shift=lambda k: mod[:, 24 + k:25 + k])
            tsp = [[dma(sp, dx[k], xsc[:, k, :], X[:, k, :], xt2[k]), dve.last, act.last] for k in range(8)]
            ft = mlp("fa1_", "fa2_", h, 8, 8, relu_up("fa1_", h), X, tsp, first_copy=True)
            XR = unit(HO, 0, [P, 8, S])
            dxr = [Dsem(f"xr{k}") for k in range(8)]
            xr = [dma(sp, dxr[k], XR[:, k, :], xsc[:, k, :], pe.last, *tsp[k]) for k in range(8)]
            tR = norm_R(xs, ft, 1024)
            dout = Dsem("out")
            for k in range(8):
                t = STT(X[:, k, :], X[:, k, :], gain(3)(k), misc.ap[:], MUL, MUL, tR)
                t = TT(XR[:, k, :], XR[:, k, :], X[:, k, :], ADD, t, xr[k])
                t = dma(sp, dout, out[:, k, :], XR[:, k, :], t)
            sp.wait(t)
        else:
            dout = Dsem("out")
            for k in range(8):
                t = dma(sp, dout, out[:, k, :], X[:, k, :], xt[k])
            sp.wait(t)
        assert ws.cur == len(wl), (ws.cur, len(wl))

        block = ctx.enter_context(nc.Block())

        @block.sync
        def _(e):
            sp.run(e)

        @block.scalar
        def _(e):
            act.run(e)

        @block.vector
        def _(e):
            dve.run(e)

        @block.gpsimd
        def _(e):
            pool.run(e)

        @block.tensor
        def _(e):
            pe.run(e)



def layout(inputs):
    g = {k: np.asarray(v) for k, v in inputs.items()}

    def tiles(w):
        k, m = w.shape
        return np.ascontiguousarray(w.reshape(k // P, P, m // P, P).transpose(2, 1, 0, 3)).reshape(m // P, P, k)

    def colv(v):
        return v.reshape(-1, P).T

    a = {}
    a["xT"] = np.ascontiguousarray(g["x"][0].T.reshape(8, P, S).transpose(1, 0, 2))
    a["metaT"] = np.ascontiguousarray(g["meta_tokens"].T.reshape(8, P, NMETA).transpose(1, 0, 2))
    w = g["w_in"][0]
    a["w_in"] = tiles(np.concatenate([w[:, :1536], w[:, 1552:]], axis=1))
    a["w_gr"] = np.ascontiguousarray(w[:, 1536:1552].reshape(8, P, 16).transpose(1, 0, 2)).reshape(P, 128)
    a["w_gate_up"] = g["w_gate_up"][0]
    a["w_out"], a["w_up"], a["w_down"] = tiles(g["w_out"][0]), tiles(g["w_up"][0]), tiles(g["w_down"][0])
    w = g["w_in_2"][0]
    a["w_in2"] = tiles(np.concatenate([w[:, :1152], w[:, 1158:]], axis=1))
    a["w_fa"] = np.ascontiguousarray(w[:, 1152:1158].reshape(8, P, W2).transpose(1, 0, 2)).reshape(P, 8 * W2)
    a["w_o2"], a["w_up2"], a["w_down2"] = tiles(g["w_o_2"][0]), tiles(g["w_up_2"][0]), tiles(g["w_down_2"][0])
    a["w_ada"] = tiles(g["w_ada_3"])
    a["w_in3"], a["w_out3"], a["w_fc1"], a["w_fc2"] = tiles(g["w_in_3"]), tiles(g["w_out_3"]), tiles(g["w_fc1_3"]), tiles(g["w_fc2_3"])
    a["w_sp"] = np.ascontiguousarray(g["w_spatial_3"].transpose(2, 0, 1))
    a["b_sp"] = g["b_spatial_3"]
    a["lnv_g"], a["lnv_b"] = g["ln_v_gain_3"], g["ln_v_bias_3"]
    a["w_pool"] = np.ascontiguousarray(g["w_pool_3"].transpose(1, 0, 2))
    cols = np.zeros((P, NCOL), np.float32)

    def put(name, v):
        s, n = COLS[name]
        cols[:v.shape[0], s:s + n] = v

    put("norm_mix", colv(g["norm_mix_w"][0]))
    put("norm_mlp", colv(g["norm_mlp_w"][0]))
    put("norm_final", colv(g["norm_final_w"]))
    put("b_gate", colv(g["b_gate"][0]))
    put("gla_norm", colv(g["gla_norm_w"][0]))
    put("conv1", g["conv_w"][0].reshape(3, 4, P).transpose(2, 1, 0).reshape(P, 12))
    put("ln1", colv(g["ln1_g_2"][0]))
    put("ln2", colv(g["ln2_g_2"][0]))
    put("g_final", colv(g["g_final_2"]))
    put("fox", colv(g["g_out_fox_2"][0]))
    put("dil", colv(g["g_out_dil_2"][0]))
    put("conv2", g["conv_w_2"][0].reshape(31, 2, P).transpose(2, 1, 0).reshape(P, 62))
    put("conv2_b", colv(g["conv_b_2"][0]))
    put("cn_g", colv(g["cnorm_g_2"][0]))
    put("cn_b", colv(g["cnorm_b_2"][0]))
    put("ffn_w", g["ffn_conv_w_2"][0].reshape(3, 44, P).transpose(2, 1, 0).reshape(P, 132))
    put("ffn_b", colv(g["ffn_conv_b_2"][0]))
    put("b_ada", colv(g["b_ada_3"]))
    put("n1pre", colv(g["norm1_pre_3"]))
    put("n1post", colv(g["norm1_post_3"]))
    put("n2pre", colv(g["norm2_pre_3"]))
    put("n2post", colv(g["norm2_post_3"]))
    put("pscale", colv(g["pool_scale_3"]))
    put("b_pool", g["b_pool_3"].T)
    put("b_forget", g["b_forget_2"][0][:, None])
    put("c", colv(g["c_3"][0]))
    rc = np.zeros((4, 16), np.float32)
    for i, w_ in enumerate((2, 4, 8, 16)):
        rc[i] = 1.0 / np.minimum(np.arange(16) + 1.0, w_)
    put("rcnt", np.broadcast_to(rc.reshape(1, 64), (P, 64)))
    a["cols"] = cols
    a["ident"] = np.eye(P, dtype=np.float32)
    j, i = np.meshgrid(np.arange(P), np.arange(P), indexing="ij")
    m = [(j // (2 * h) == i // (2 * h)) & (j % (2 * h) < h) & (i % (2 * h) >= h) for h in LEVELS] + [j == i]
    a["masks"] = np.ascontiguousarray(np.stack(m, 1).astype(np.float32)).reshape(P, 1024)
    q, k = j, i
    ok = [k <= q, k >= q, (k % 2 == q % 2) & (k <= q)]
    a["negm"] = np.ascontiguousarray(np.stack([np.where(o, 0.0, NEG) for o in ok], 1).astype(np.float32)).reshape(P, 384)
    sl = np.zeros((6, 6, P), np.float32)
    for h in range(6):
        sl[h, h] = 1.0
    a["sel"] = sl
    a["tri"] = (i >= j).astype(np.float32)
    return a


def plan_block2(plan, plan_mlp, d, upto):
    w = d["w_in2"]
    for n, m in (("gg0", 20), ("gv0", 18), ("gg1", 21), ("gv1", 19)):
        plan(n, w[m])
    plan("fa", d["w_fa"])
    for n, m in (("vb", 15), ("qa", 0), ("ka", 3), ("va", 6), ("qb", 9), ("kb", 12)):
        for j in range(3):
            plan(f"{n}{j}", w[m + j])
    for m in range(8):
        plan(f"w2o{m}", d["w_o2"][m])
    plan_mlp("w_up2", "w_down2", "fup", "fdn", 6, 8, sizes=[4] * 5 + [2], pairs=True)


def plan_block3(plan, plan_mlp, d):
    for n, m in (("zv", 4), ("zu", 0), ("zb", 8)):
        for j in range(4):
            plan(f"{n}{j}", d["w_in3"][m + j])
    for m in range(8):
        plan(f"wo3{m}", d["w_out3"][m])
    plan_mlp("w_fc1", "w_fc2", "fa1_", "fa2_", 8, 8)


def kernel(**inputs):
    import concourse.bacc as _bacc
    from concourse.bass_utils import run_bass_kernel_spmd as _run

    nc = _bacc.Bacc("TRN2", target_bir_lowering=False, num_devices=1)
    arrays = layout(inputs)
    d = {n: nc.dram_tensor("in_" + n, a.shape, mybir.dt.from_np(a.dtype), kind="ExternalInput").ap()
         for n, a in arrays.items()}
    out = nc.dram_tensor("out_0", (P, 8, S), F, kind="ExternalOutput").ap()
    build(nc, d, out)
    r = _run(nc, [{"in_" + n: a for n, a in arrays.items()}], core_ids=[0])
    o = r.results[0]["out_0"]
    return np.ascontiguousarray(o.transpose(2, 1, 0)).reshape(1, S, 1024)
```

```python
from contextlib import ExitStack

import numpy as np

import concourse.bass as bass
from concourse import mybir

F = mybir.dt.float32
R = mybir.dt.float32r
BF = mybir.dt.bfloat16
U8 = mybir.dt.uint8
ALU = mybir.AluOpType
ACT = mybir.ActivationFunctionType
AX = mybir.AxisListType
MUL, ADD, SUB, MAX, MIN = ALU.mult, ALU.add, ALU.subtract, ALU.max, ALU.min

P = 128
S = 1024
NMETA = 16
EPS = 1e-6
FF2 = 2816
NPAIR = FF2 // 128
LEVELS = (64, 32, 16, 8, 4, 2, 1)
NEG = -1e30
W2 = 6

COLS = {}


def _columns():
    at = 0
    for name, n in (("norm_mix", 8), ("norm_mlp", 8), ("norm_final", 8), ("b_gate", 2), ("gla_norm", 1),
                    ("conv1", 12), ("ln1", 8), ("ln2", 8), ("g_final", 8), ("fox", 3), ("dil", 3),
                    ("conv2", 62), ("conv2_b", 2), ("cn_g", 2), ("cn_b", 2), ("ffn_w", 132), ("ffn_b", 44),
                    ("b_ada", 48), ("n1pre", 8), ("n1post", 8), ("n2pre", 8), ("n2post", 8),
                    ("pscale", 4), ("b_pool", 4), ("b_forget", 1), ("c", 8), ("rcnt", 64)):
        COLS[name] = (at, n)
        at += n
    return at


NCOL = _columns()


class Engine:

    def __init__(self, name, sem):
        self.name, self.sem, self.count, self.todo, self.seen = name, sem, 0, [], {}

    def wait(self, *tokens):
        for sem, value in tokens:
            if self.seen.get(sem.name, 0) < value:
                self.seen[sem.name] = value
                self.todo.append(lambda e, s=sem, v=value: e.wait_ge(s, v))

    def go(self, fn, *tokens):
        self.wait(*tokens)
        self.todo.append(fn)

    def op(self, fn, *tokens):
        self.wait(*tokens)
        self.count += 1
        self.todo.append(lambda e: fn(e).then_inc(self.sem, 1))
        return (self.sem, self.count)

    @property
    def last(self):
        return (self.sem, self.count)

    def run(self, e):
        for fn in self.todo:
            fn(e)


class Slot:

    def __init__(self, ap):
        self.ap, self._busy, self.held = ap, [], False

    @property
    def busy(self):
        return self._busy

    @busy.setter
    def busy(self, tokens):
        self._busy, self.held = tokens, False


class Ring:
    def __init__(self, slots):
        self.slots, self.at = slots, 0

    def take(self):
        for _ in self.slots:
            s = self.slots[self.at % len(self.slots)]
            self.at += 1
            if not s.held:
                s.held = True
                return s
        raise AssertionError("every buffer is held")


def build(nc, d, out, upto=3):
    ctx = ExitStack()
    with ctx:
        def sem(name):
            return ctx.enter_context(nc.semaphore(name))

        pe, act, dve, pool, sp = (Engine(n, sem("s_" + n)) for n in ("pe", "act", "dve", "pool", "sp"))

        class Dsem:
            def __init__(self, name):
                self.sem, self.count = sem("d_" + name), 0

        def dma(q, ds, o, i, *tokens):
            q.wait(*tokens)
            ds.count += 16
            q.todo.append(lambda e: e.dma_start(o, i).then_inc(ds.sem, 16))
            return (ds.sem, ds.count)

        base = -(-nc.sbuf_base // 64) * 64
        XO, HO = base, base + 32768
        GO = HO + 65536
        WO = GO + 65536
        RO = WO + 24576
        TO = RO + 4096
        CO = TO + 12288
        names = [0]

        def at(off, shape, dt=F, name=None):
            names[0] += 1
            return nc.alloc_sbuf_tensor_at(name or f"b{names[0]}", list(shape), dt, offset=off)

        catch = [CO]

        def const(shape, dt=F):
            n = int(np.prod(shape[1:])) * {F: 4, R: 4, BF: 2, U8: 1}[dt]
            t = at(catch[0], shape, dt)
            catch[0] += -(-n // 32) * 32
            assert catch[0] <= nc.sbuf_usable_end, catch[0]
            return t

        def unit(region, n, shape, dt=F):
            return at(region + 4096 * n, shape, dt)

        X = at(XO, [P, 8, S])
        HH, HL = at(HO, [P, 8, S], R), at(HO + 32768, [P, 8, S], R)
        HHs, HLs = [HH[:, k, :] for k in range(8)], [HL[:, k, :] for k in range(8)]
        GH, GL = at(GO, [P, 8, S], R), at(GO + 32768, [P, 8, S], R)
        GHs, GLs = [GH[:, k, :] for k in range(8)], [GL[:, k, :] for k in range(8)]
        raw = [at(WO + 4096 * i, [P, 1024]) for i in range(4)]
        wlo = [at(WO + 4096 * i, [P, 1024], R) for i in range(4)]
        whi = [at(WO + 16384 + 4096 * i, [P, 1024], R) for i in range(2)]
        RT = at(RO, [P, S])
        T = [Slot(at(TO + 4096 * i, [P, S])) for i in range(3)]
        tring = Ring(T)

        psl = [Slot(ctx.enter_context(nc.psum_tensor(f"ps{i}", [P, 1024], F))) for i in range(3)]
        pring = Ring(psl)
        misc = Slot(ctx.enter_context(nc.psum_tensor("ps3", [P, 1024], F)))

        ident = const([P, P])
        ones = const([P, P])
        identb = const([P, P], BF)
        rmt = const([P, NMETA])
        rms = const([P, 40])
        gprod = const([P, 16])
        adat = const([P, 2, P])
        cols = const([P, NCOL])
        masks = const([P, 8, P], U8)
        negm = const([P, 3, P], BF)
        st = const([P, 8])
        rr = const([P, 8])
        HMH, HML = const([P, 8, NMETA], R), const([P, 8, NMETA], R)
        mod = const([P, 48])
        SC = const([P, 8])
        gx = const([P, 16])
        epsc = const([P, 1])
        onec = const([P, 1])

        def col(name, i=0, n=1):
            a, m = COLS[name]
            return cols[:, a + i:a + i + n]

        dc = Dsem("const")
        for o, i in ((cols[:], "cols"), (ident[:], "ident")):
            tc = dma(sp, dc, o, d[i])
        tones = dve.op(lambda e: e.memset(ones[:], 1.0))
        dve.op(lambda e: e.memset(epsc[:], EPS))
        dve.op(lambda e: e.memset(onec[:], 1.0))
        dve.op(lambda e: e.tensor_copy(identb[:], ident[:]), tc)
        consts = [tc, dve.last]
        for q in (pe, act, dve, pool):
            q.wait(*consts)


        def A(o, i, func, *w, scale=1.0, bias=None, accum=None):
            kw = {"scale": scale}
            if bias is not None:
                kw["bias"] = bias
            if accum is not None:
                kw["accum_out"] = accum
            return act.op(lambda e: e.activation(o, i, func, **kw), *w)

        def TT(o, a, b, op, *w, q=dve):
            return q.op(lambda e: e.tensor_tensor(o, a, b, op), *w)

        def TS(o, a, s1, s2, o1, o2, *w, q=dve):
            if o2 is None:
                return q.op(lambda e: e.tensor_scalar(o, a, s1, None, o1), *w)
            return q.op(lambda e: e.tensor_scalar(o, a, s1, s2, o1, o2), *w)

        def STT(o, a, s, b, o1, o2, *w):
            return dve.op(lambda e: e.scalar_tensor_tensor(out=o, in0=a, scalar=s, in1=b, op0=o1, op1=o2), *w)

        def CP(o, a, *w, q=dve):
            return q.op(lambda e: e.tensor_copy(o, a), *w)

        def split(src, hi, lo, *w, q=pool):
            t = A(hi, src, ACT.Copy, *w)
            return TT(lo, src, hi.bitcast(F), SUB, t, *w, q=q)


        wl = []

        def plan(name, ap, split=True):
            wl.append((name, ap, split))

        class Stream:
            def __init__(self):
                self.cur = self.dma = self.spl = 0
                self.ds = [Dsem(f"w{i}") for i in range(4)]
                self.landed, self.free, self.ready, self.slot = {}, {}, {}, {}
                self.nspl = 0
                self.used = {}

            def pump(self, i):
                while True:
                    moved = False
                    if self.dma < len(wl) and self.dma <= i + 4 and (self.dma < 4 or self.dma - 4 in self.free):
                        j = self.dma
                        ap = wl[j][1]
                        n = int(np.prod(ap.shape[1:]))
                        w = [self.free[j - 4]] if j >= 4 else []
                        dst = raw[j % 4][:, 0:n]
                        if len(ap.shape) == 3:
                            dst = dst.rearrange("p (k m) -> p k m", k=ap.shape[1])
                        self.landed[j] = dma(sp, self.ds[j % 4], dst, ap, *w)
                        self.dma += 1
                        moved = True
                    if self.spl < len(wl) and self.spl <= i + 1 and self.spl in self.landed:
                        j = self.spl
                        if wl[j][2]:
                            s = self.nspl % 2
                            if self.nspl < 2 or (self.nspl - 2) in self.used:
                                n = int(np.prod(wl[j][1].shape[1:]))
                                w = [self.used[self.nspl - 2]] if self.nspl >= 2 else []
                                t = split(raw[j % 4][:, 0:n], whi[s][:, 0:n], wlo[j % 4][:, 0:n], self.landed[j], *w)
                                self.ready[j] = t
                                self.slot[j] = (s, self.nspl)
                                self.nspl += 1
                                self.spl += 1
                                moved = True
                        else:
                            self.spl += 1
                            moved = True
                    if not moved:
                        return

            def take(self, name):
                i = self.cur
                assert wl[i][0] == name, (wl[i][0], name)
                self.cur += 1
                self.pump(i)
                return i

            def done(self, i, tok):
                self.free[i] = tok
                if wl[i][2]:
                    self.used[self.slot[i][1]] = tok

        ws = Stream()

        class Rhs:

            def __init__(self, hi, lo, toks, order=None):
                self.hi, self.lo, self.toks, self.order = hi, lo, toks, order

        def job(name, rhs, nk, k0=0, m=P, meta=False, into=None):
            i = ws.take(name)
            s, _ = ws.slot[i]
            hi = whi[s][:, 0:nk * m].rearrange("p (k m) -> p k m", k=nk)
            lo = wlo[i % 4][:, 0:nk * m].rearrange("p (k m) -> p k m", k=nk)
            sl = pring.take()
            pe.wait(ws.ready[i], *sl.busy)
            if meta:
                pe.wait(*misc.busy)
            order = rhs.order or list(range(nk))
            for k in order:
                pe.wait(rhs.toks[k0 + k])
                first, last = k == order[0], k == order[-1]
                for hf in range(2):
                    cs = slice(512 * hf, 512 * hf + 512)
                    o = sl.ap[0:m, cs]
                    pe.go(lambda e, o=o, k=k, cs=cs, first=first: e.matmul(o, hi[:, k, :], rhs.hi[k0 + k][:, cs], start=first, stop=False))
                    pe.go(lambda e, o=o, k=k, cs=cs: e.matmul(o, hi[:, k, :], rhs.lo[k0 + k][:, cs], start=False, stop=False))
                if meta:
                    o = misc.ap[0:m, 0:NMETA]
                    pe.go(lambda e, o=o, k=k, first=first: e.matmul(o, hi[:, k, :], HMH[:, k, :], start=first, stop=False))
                    pe.go(lambda e, o=o, k=k: e.matmul(o, hi[:, k, :], HML[:, k, :], start=False, stop=False))
                    pe.go(lambda e, o=o, k=k, last=last: e.matmul(o, lo[:, k, :], HMH[:, k, :], start=False, stop=last))
                for hf in range(2):
                    cs = slice(512 * hf, 512 * hf + 512)
                    o = sl.ap[0:m, cs]
                    f = lambda e, o=o, k=k, cs=cs, last=last: e.matmul(o, lo[:, k, :], rhs.hi[k0 + k][:, cs], start=False, stop=last)
                    if last and hf == 1:
                        tok = pe.op(f)
                    else:
                        pe.go(f)
            ws.done(i, tok)
            ws.pump(i + 1)
            return sl, tok

        turns_due = []

        def turned(b, t, dst, *w):
            def later():
                sl = pring.take()
                pe.wait(t, *sl.busy)
                for c in range(8):
                    f = lambda e, c=c: e.transpose(sl.ap[:, P * c:P * c + P], b.ap[:, P * c:P * c + P], ident[:])
                    t2 = pe.op(f) if c == 7 else pe.go(f)
                b.busy = [t2]
                t2 = A(dst, v3(sl.ap[:], 8), ACT.Copy, t2, *w)
                sl.busy = [t2]
                return t2
            turns_due.append(later)

        def turn_now():
            t = None
            while turns_due:
                t = turns_due.pop(0)()
            return t

        def v3(ap, n):
            return ap.rearrange("p (a b) -> p a b", a=n)

        class Norm:

            def __init__(self, width, g=None):
                self.D, self.g, self.k = width, g, 0
                self.acc, self.acc2 = T[2], T[1]
                self.prev = self.prev2 = None

            def feed(self, x, *tok):
                k = self.k
                if k == 0:
                    self.prev = A(self.acc.ap[:], x, ACT.Square, *tok, *self.acc.busy)
                    if self.g is not None:
                        self.prev2 = A(self.acc2.ap[:], x, ACT.Square, *tok, *self.acc2.busy, scale=self.g(0))
                else:
                    b = T[(k - 1) % 2] if self.g is None else T[0]
                    t = A(b.ap[:], x, ACT.Square, *tok, *b.busy)
                    self.prev = TT(self.acc.ap[:], self.acc.ap[:], b.ap[:], ADD, t, self.prev)
                    b.busy = [self.prev]
                    if self.g is not None:
                        t = A(b.ap[:], x, ACT.Square, *tok, *b.busy, scale=self.g(k))
                        self.prev2 = TT(self.acc2.ap[:], self.acc2.ap[:], b.ap[:], ADD, t, self.prev2, q=pool)
                        b.busy = [self.prev2]
                self.k += 1

            def stats(self):
                sl = pring.take()
                pe.wait(self.prev, *sl.busy)
                for b in range(8):
                    t = pe.op(lambda e, b=b: e.matmul(sl.ap[:, b:b + 1], self.acc.ap[:, P * b:P * b + P], ones[:, 0:1], start=(b == 0), stop=True, skip_group_check=True))
                self.acc.busy = [t]
                s1, r1, s2, r2, r12 = (rms[:, 8 * i:8 * i + 8] for i in range(5))
                if self.g is not None:
                    pe.wait(self.prev2)
                    for b in range(8):
                        t = pe.op(lambda e, b=b: e.matmul(sl.ap[:, 512 + b:513 + b], self.acc2.ap[:, P * b:P * b + P], ones[:, 0:1], start=(b == 0), stop=True, skip_group_check=True))
                    self.acc2.busy = [t]
                t = A(s1, sl.ap[:, 0:8], ACT.Sqrt, t, scale=1.0 / self.D, bias=epsc[:])
                self.t = dve.op(lambda e: e.reciprocal(r1, s1), t)
                self.r1 = self.r = r1
                if self.g is not None:
                    t = TT(s2, r1, r1, MUL, self.t)
                    t = TT(s2, s2, sl.ap[:, 512:520], MUL, t)
                    sl.busy = [t]
                    t = A(s2, s2, ACT.Sqrt, t, scale=1.0 / self.D, bias=epsc[:])
                    t = dve.op(lambda e: e.reciprocal(r2, s2), t)
                    self.t = TT(r12, r1, r2, MUL, t)
                    self.r = r12
                else:
                    sl.busy = [t]
                self.dg = T[0]
                self.tdg = TT(v3(self.dg.ap[:], 8), ident[:].unsqueeze(1).broadcast_to([P, 8, P]),
                              self.r.unsqueeze(2).broadcast_to([P, 8, P]), MUL, self.t, *self.dg.busy)

            def spread(self):
                sl = pring.take()
                pe.wait(self.tdg, *sl.busy)
                for hf in range(2):
                    t = pe.op(lambda e, hf=hf: e.matmul(sl.ap[:, 512 * hf:512 * hf + 512], ones[:], self.dg.ap[:, 512 * hf:512 * hf + 512], start=True, stop=True))
                self.dg.busy = [t]
                return sl, t

            def to_rt(self):
                sl, t = self.spread()
                t = A(RT[:], sl.ap[:], ACT.Copy, t, *stt.get("rtfree", []))
                sl.busy = [t]
                self.rt = t
                return t

            def first(self):
                self.tdg = TT(v3(self.dg.ap[:], 8), ident[:].unsqueeze(1).broadcast_to([P, 8, P]),
                              self.r1.unsqueeze(2).broadcast_to([P, 8, P]), MUL, *self.dg.busy)
                return self.spread()

        def weigh(k, x, g, hi, lo, *w):
            t = A(hi[:, k, :], x, ACT.Copy, *w, scale=g)
            return STT(lo[:, k, :], x, g, hi[:, k, :].bitcast(F), MUL, SUB, t, *w)

        def normed(xs, g, sl, tR, hi, lo, *w, shift=None):
            toks = []
            for k, x in enumerate(xs):
                b = tring.take()
                t = STT(b.ap[:], x, g(k), sl.ap[:], MUL, MUL, tR, *b.busy, *w)
                if shift is not None:
                    t2 = A(hi[:, k, :], b.ap[:], ACT.Identity, t, *w, bias=shift(k))
                    if True:
                        t2 = STT(lo[:, k, :], b.ap[:], shift(k), hi[:, k, :].bitcast(F), ADD, SUB, t2, *w)
                else:
                    t2 = split(b.ap[:], hi[:, k, :], lo[:, k, :], t, *w, q=(pool, dve)[k % 2])
                b.busy = [t2]
                toks.append(t2)
            sl.busy = [dve.last]
            return Rhs([hi[:, k, :] for k in range(8)], [lo[:, k, :] for k in range(8)], toks)

        stt = {}

        def relu_up(name, h, rt):
            def up_job(j, mid):
                return job(f"{name}{j}", h, 8)

            def up_drain(j, got):
                sl, tok = got
                b = tring.take()
                if rt is None:
                    t = A(b.ap[:], sl.ap[:], ACT.Relu, tok, *b.busy)
                else:
                    t = STT(b.ap[:], sl.ap[:], 0.0, RT[:], MAX, MUL, tok, rt.rt, *b.busy)
                sl.busy = [t]
                return b, TT(b.ap[:], b.ap[:], b.ap[:], MUL, t)
            return up_job, up_drain

        hidden = {"free": [[], []], "toks": [None] * 8}

        def mlp(name_down, up_job, up_drain, ngroups, acc, acc_toks, first_copy=False, sizes=None, norm=None, on_last=None, step=None):
            sizes = sizes or [4] * ngroups
            gh = Rhs(GHs, GLs, hidden["toks"])
            jobs = [0]

            def stepped(got):
                if step:
                    step(jobs[0])
                jobs[0] += 1
                return got

            def drain(g, j, got):
                slot = 4 * (g % 2) + j
                b, t = up_drain(4 * g + j, got)
                t = split(b.ap[:], GH[:, slot, :], GL[:, slot, :], t, *hidden["free"][g % 2])
                b.busy = [t]
                hidden["toks"][slot] = t

            def ups(g):
                j0 = 0
                if g == 0 and norm is not None:
                    if name_down == "fdn":
                        got = stepped(up_job(0, norm.stats))
                        norm.to_rt()
                        drain(0, 0, got)
                        j0 = 1
                    else:
                        got = stepped(up_job(0, None))
                        norm.stats()
                        got1 = stepped(up_job(1, None))
                        norm.to_rt()
                        drain(0, 0, got)
                        drain(0, 1, got1)
                        j0 = 2
                for j in range(j0, sizes[g]):
                    drain(g, j, stepped(up_job(4 * g + j, None)))

            ups(0)
            for g in range(ngroups):
                if g + 1 < ngroups:
                    ups(g + 1)
                    if g + 1 == ngroups - 1:
                        stt["ups"] = pe.last
                        stt["rtfree"] = [dve.last]
                for m in range(8):
                    sl, tok = stepped(job(f"{name_down}{g}_{m}", gh, sizes[g], k0=4 * (g % 2)))
                    if g == 0 and first_copy:
                        t = A(acc[:, m, :], sl.ap[:], ACT.Copy, tok, *acc_toks[m])
                    else:
                        t = TT(acc[:, m, :], sl.ap[:], acc[:, m, :], ADD, tok, *acc_toks[m])
                    acc_toks[m] = [t]
                    sl.busy = [t]
                    if g == ngroups - 1 and on_last:
                        on_last(m, t)
                hidden["free"][g % 2] = [pe.last]
            return [a[0] for a in acc_toks]

        def plan_mlp(up, dn, name_up, name_down, ng, nk, sizes=None, pairs=False, ada=False):
            sizes = sizes or [4] * ng
            done = [0]

            def extra():
                n, done[0] = done[0], done[0] + 1
                if ada and n % 2:
                    plan(f"ada{n // 2}", d["w_ada"][n // 2], split=False)

            def ups(g):
                for j in range(sizes[g]):
                    m = 4 * g + j
                    if pairs:
                        plan(f"{name_up}a{m}", d[up][m])
                        plan(f"{name_up}b{m}", d[up][NPAIR + m])
                    else:
                        plan(f"{name_up}{m}", d[up][m])
                        extra()
            ups(0)
            for g in range(ng):
                if g + 1 < ng:
                    ups(g + 1)
                for m in range(8):
                    plan(f"{name_down}{g}_{m}", d[dn][m, :, 4 * g * P:(4 * g + sizes[g]) * P])
                    extra()

        plan("gr", d["w_gr"])
        for n, m0 in (("k0", 2), ("k1", 3), ("q0", 0), ("q1", 1), ("v0", 4), ("v1", 5), ("v2", 6), ("v3", 7),
                      ("g0", 8), ("g1", 9), ("g2", 10), ("g3", 11)):
            plan(n, d["w_in"][m0])
        for m in range(4):
            plan(f"cc{m}", d["w_in"][16 + m])
            plan(f"cx{m}", d["w_in"][20 + m])
            plan(f"cb{m}", d["w_in"][12 + m])
        for m in range(8):
            plan(f"wo{m}", d["w_out"][m])
        plan_mlp("w_up", "w_down", "up", "dn", 8, 8, ada=upto >= 3)
        if upto >= 2:
            plan_block2(plan, plan_mlp, d, upto)
        if upto >= 3:
            plan_block3(plan, plan_mlp, d)

        ysc = nc.dram_tensor("ysc", (P, 8, S), F, kind="Internal").ap()
        sgsc = nc.dram_tensor("sgsc", (P, 4, S), F, kind="Internal").ap()
        xsc = nc.dram_tensor("xsc", (P, 8, S), F, kind="Internal").ap()

        dx = [Dsem(f"x{k}") for k in range(8)]
        dm = Dsem("meta")
        XM = unit(GO, 0, [P, 8, NMETA])
        SQM = at(GO + 1024, [P, 8, NMETA])
        DGM = at(GO + 2048, [NMETA, NMETA])
        TM = at(GO + 4096, [P, 8, NMETA])
        tm = dma(sp, dm, XM[:], d["metaT"])
        ws.pump(-3)
        xt = [dma(sp, dx[k], X[:, k, :], d["xT"][:, k, :]) for k in range(8)]
        dmk = Dsem("mask")
        mf = unit(GO, 2, [P, S])
        nf_ = unit(GO, 3, [P, 384])
        dma(sp, dmk, mf[:], d["masks"])
        tmk = dma(sp, dmk, nf_[:], d["negm"])
        ws.pump(-1)

        tgp = TT(gprod[:, 0:8], col("norm_final", 0, 8), col("ln1", 0, 8), MUL)
        for k in range(8):
            tw = TS(TM[:, k, :], XM[:, k, :], col("norm_mix", k), None, MUL, None, tm)
        tmeta = split(TM[:], HMH[:], HML[:], tw)
        t = A(SQM[:], XM[:], ACT.Square, tm)
        pe.wait(t)
        for k in range(8):
            f = lambda e, k=k: e.matmul(misc.ap[0:NMETA, 0:1], SQM[:, k, :], ones[:, 0:1], start=(k == 0), stop=(k == 7))
            t = pe.op(f) if k == 7 else pe.go(f)
        t = A(st[0:NMETA, 0:1], misc.ap[0:NMETA, 0:1], ACT.Sqrt, t, scale=1.0 / 1024, bias=epsc[0:NMETA, :])
        t = dve.op(lambda e: e.reciprocal(rr[0:NMETA, 0:1], st[0:NMETA, 0:1]), t)
        t = TS(DGM[:], ident[0:NMETA, 0:NMETA], rr[0:NMETA, 0:1], None, MUL, None, t)
        t = pe.op(lambda e: e.matmul(misc.ap[:, 0:NMETA], ones[0:NMETA, :], DGM[:], start=True, stop=True), t)
        trm = CP(rmt[:], misc.ap[:, 0:NMETA], t)
        misc.busy = [trm]

        xs = [X[:, k, :] for k in range(8)]
        norm = Norm(1024)
        toks = []
        for k in range(8):
            toks.append(weigh(k, xs[k], col("norm_mix", k), HH, HL, xt[k]))
            norm.feed(xs[k], xt[k])
        h = Rhs(HHs, HLs, toks)
        CP(masks[:].rearrange("p a b -> p (a b)"), mf[:], tmk)
        CP(negm[:].rearrange("p a b -> p (a b)"), nf_[:])
        pe.wait(tmeta)
        xfree = [dve.last, act.last]
        gfree = [tmeta, dve.last]

        def G(n, shape, dt=F):
            return unit(GO, n, shape, dt)

        Q, K, B, V, D, AT = (G(0, [P, 2, S]), G(2, [P, 2, S]), G(4, [P, 2, S]), G(6, [P, 8, 512]), G(10, [P, 2, S]),
                             G(12, [P, 4, S]))
        XL = [Slot(unit(XO, 0, [P, 2, S])), Slot(unit(XO, 2, [P, 2, S]))]
        QI = unit(XO, 4, [P, 2, S])
        U = unit(XO, 6, [P, 1026])
        mo = XO + 7 * 4096 + 64
        KM, BM, VM, KDM, EM = (at(mo, [P, 2, NMETA]), at(mo + 128, [P, 2, NMETA]), at(mo + 256, [NMETA, 512]),
                               at(mo + 2304, [NMETA, 256]), at(mo + 3328, [P, 2, NMETA]))
        EV = at(mo + 3584, [P, NMETA])
        KDT, SA = unit(XO, 0, [P, 8, 256]), unit(XO, 2, [P, 8, 256])

        tz = pool.op(lambda e: e.memset(AT[:], 0.0), *gfree)

        def meta_out(dst, c0, n, *w):
            t = TT(dst, misc.ap[:, c0:c0 + n], rmt[:, c0:c0 + n], MUL, *w)
            misc.busy = [t]
            return t

        sl, tok = job("gr", h, 8, m=16, meta=True)
        norm.stats()
        grm = at(mo + 3456, [16, NMETA])
        t2 = TT(grm[:], misc.ap[0:16, 0:NMETA], rmt[0:16, :], MUL, tok, *xfree)
        misc.busy = [t2]
        tk, tq = [], []
        slk, tokk = job("k0", h, 8, meta=True)
        norm.to_rt()
        gr = T[0]
        t1 = TT(gr.ap[0:16, :], sl.ap[0:16, :], RT[0:16, :], MUL, tok, norm.rt, *gr.busy)
        sl.busy = [t1]

        def k_out(m, sl, tok):
            t = TT(K[:, m, :], sl.ap[:], RT[:], MUL, tok, *gfree)
            sl.busy = [t]
            tk.append(t)
            tk.append(meta_out(KM[:, m, :], 0, NMETA, tok, *xfree))

        k_out(0, slk, tokk)
        wg = T[2]
        dg = Dsem("wg")
        tw = dma(sp, dg, wg.ap[0:16, 0:256], d["w_gate_up"], *wg.busy)

        def logsig(zs, bias, o_abs, o_min, o_g, *w):
            t = A(o_abs, zs, ACT.Abs, *w, bias=bias)
            tmn = TS(o_min, zs, bias, 0.0, ADD, MIN, t, *w)
            t2 = A(o_abs, o_abs, ACT.Exp, t, scale=-1.0)
            t2 = A(o_abs, o_abs, ACT.Ln, t2, bias=onec[0:o_abs.shape[0], :])
            return TT(o_g, o_min, o_abs, SUB, t2, tmn), t, tmn

        sl, tok = job("k1", h, 8, meta=True)
        k_out(1, sl, tok)
        zt = []
        for m in range(2):
            sz = pring.take()
            pe.wait(t1, tw, *sz.busy)
            for hf in range(2):
                f = lambda e, hf=hf, m=m, sz=sz: e.matmul(sz.ap[:, 512 * hf:512 * hf + 512], wg.ap[0:16, P * m:P * m + P], gr.ap[0:16, 512 * hf:512 * hf + 512], start=True, stop=True)
                t = pe.op(f)
            g_, ta, tb = logsig(sz.ap[:], col("b_gate", m), D[:, m, :], B[:, m, :], D[:, m, :], t, *gfree)
            sz.busy = [ta, tb]
            zt.append(g_)
        gr.busy = [pe.last]
        pe.wait(t2, *misc.busy)
        for m in range(2):
            t = pe.op(lambda e, m=m: e.matmul(misc.ap[:, 32 * m:32 * m + NMETA], wg.ap[0:16, P * m:P * m + P], grm[:], start=True, stop=True))
        wg.busy = [t]
        zm = []
        for m in range(2):
            g_, ta, tb = logsig(misc.ap[:, 32 * m:32 * m + NMETA], col("b_gate", m), EM[:, m, :], BM[:, m, :], EM[:, m, :], t, *xfree, *zm)
            zm.append(g_)
        misc.busy = [ta, tb]
        keep = T[2]
        ta = pool.op(lambda e: e.memset(keep.ap[:], 1.0), *keep.busy)
        ta = pool.op(lambda e: e.memset(v3(keep.ap[:], 8)[:, :, 0:1], 0.0), ta)
        tb = []
        for m in range(2):
            tb.append(dve.op(lambda e, m=m: e.tensor_tensor_scan(B[:, m, :], keep.ap[:], D[:, m, :], 0.0, MUL, ADD), ta, zt[m]))
            tbm = dve.op(lambda e, m=m: e.tensor_tensor_scan(BM[:, m, :], keep.ap[:, 1:1 + NMETA], EM[:, m, :], 0.0, MUL, ADD), ta, zm[m])
        keep.busy = [tbm]
        tb.append(tbm)

        for m in range(2):
            sl, tok = job(f"q{m}", h, 8)
            t = STT(Q[:, m, :], sl.ap[:], 0.125, RT[:], MUL, MUL, tok, *gfree)
            sl.busy = [t]
            tq.append(t)

        fill = []

        def level(li):
            hsz = LEVELS[li]
            nb = S // (2 * hsz)
            bv = B[:].rearrange("p t (n w) -> p (t n) w", w=2 * hsz)
            dv = D[:].rearrange("p t (n w) -> p (t n) w", w=2 * hsz)
            ref = bv[:, :, hsz - 1:hsz].broadcast_to([P, 2 * nb, 2 * hsz])
            t = TT(dv, bv, ref, SUB, *tb, *stt.get("dfree", []))
            t = A(D[:], D[:], ACT.Abs, t)
            t = A(D[:], D[:], ACT.Exp, t, scale=-1.0 / 16)
            x = XL[li % 2]
            xv = x.ap[:].rearrange("p t (n w) -> p (t n) w", w=2 * hsz)
            qv = Q[:].rearrange("p t (n w) -> p (t n) w", w=2 * hsz)
            kv = K[:].rearrange("p t (n w) -> p (t n) w", w=2 * hsz)
            TT(xv[:, :, hsz:], dv[:, :, hsz:], qv[:, :, hsz:], MUL, t, *tq, *x.busy, *xfree)
            t = TT(xv[:, :, :hsz], dv[:, :, :hsz], kv[:, :, :hsz], MUL, *tk)
            stt["dfree"] = [t]
            stt[f"x{li}"] = (x, t)

        def level_head(li, hd):
            t_, hh = hd // 2, hd % 2
            sl = pring.take()
            pe.wait(*sl.busy)
            if li == 7:
                a, b = K, Q
                pe.wait(*tq, *tk)
            else:
                x, tx = stt[f"x{li}"]
                a = b = x.ap
                pe.wait(tx)
            for c in range(8):
                cs = slice(P * c, P * c + P)
                f = lambda e, c=c, cs=cs, a=a, b=b: e.matmul(sl.ap[:, cs], a[64 * hh:64 * hh + 64, t_, cs], b[64 * hh:64 * hh + 64, t_, cs], start=True, stop=True)
                t = pe.op(f) if c == 7 else pe.go(f)
            if li < 7:
                x.busy = [t]
            t = dve.op(lambda e: e.copy_predicated(v3(AT[:, hd, :], 8), masks[:, li, :].unsqueeze(1).broadcast_to([P, 8, P]), v3(sl.ap[:], 8)), t, tz)
            sl.busy = [t]
            stt["at"] = t

        level(0)
        for li in range(8):
            for hd in range(4):
                fill.append(lambda li=li, hd=hd: level_head(li, hd))
                if hd == 0 and li < 6:
                    fill.append(lambda li=li: level(li + 1))

        bl = B[:].rearrange("p t (n w) -> p (t n) w", w=P)[:, :, P - 1:P]

        def decays():
            dv = D[:].rearrange("p t (n w) -> p (t n) w", w=P)
            bv = B[:].rearrange("p t (n w) -> p (t n) w", w=P)
            t = A(gx[:].unsqueeze(2), bl, ACT.Exp, *tb, scale=1.0 / 16)
            stt["dec"] = t
            t = A(QI[:], B[:], ACT.Exp, *tb, *xfree, scale=1.0 / 16)
            stt["qi"] = TT(QI[:], QI[:], Q[:], MUL, t, *tq)
            t = TT(dv, bv, bl.broadcast_to([P, 16, P]), SUB, *stt["dfree"])
            t = A(D[:], D[:], ACT.Exp, t, scale=-1.0 / 16)
            stt["kd"] = TT(D[:], D[:], K[:], MUL, t)
            t = TT(EM[:], BM[:], BM[:, :, NMETA - 1:NMETA].broadcast_to([P, 2, NMETA]), SUB, tb[-1])
            t = A(EM[:], EM[:], ACT.Exp, t, scale=-1.0 / 16)
            stt["kdm"] = TT(EM[:], EM[:], KM[:], MUL, t, *tk)
            stt["xl"] = [pe.last]

        def kd_turn(m):
            sl = pring.take()
            pe.wait(stt["kd"], *sl.busy)
            for c in range(8):
                f = lambda e, c=c: e.transpose(sl.ap[:, P * c:P * c + P], D[:, m, P * c:P * c + P], ident[:])
                t = pe.op(f) if c == 7 else pe.go(f)
            t = A(KDT[:, :, P * m:P * m + P], v3(sl.ap[:], 8), ACT.Copy, t, *stt["xl"])
            sl.busy = [t]
            stt[f"kdt{m}"] = t

        def meta_state():
            sl = pring.take()
            pe.wait(stt["kdm"], *sl.busy)
            for m in range(2):
                t = pe.op(lambda e, m=m: e.transpose(sl.ap[0:NMETA, P * m:P * m + P], EM[:, m, :], ident[:]))
            t = CP(KDM[:], sl.ap[0:NMETA, 0:256], t)
            sl.busy = [t]
            kv_mm(0, lambda h: KDM[0:NMETA, 64 * h:64 * h + 64], lambda h: VM[0:NMETA, P * h:P * h + P], t, stt["vm"])

        def kv_mm(c, lhs, rhs, *w):
            sl = pring.take()
            pe.wait(*w, *sl.busy)
            for hd in range(4):
                t_, hh = hd // 2, hd % 2
                f = lambda e, hd=hd, t_=t_, hh=hh: e.matmul(sl.ap[64 * hh:64 * hh + 64, P * t_:P * t_ + P], lhs(hd), rhs(hd), start=True, stop=True)
                t = pe.op(f) if hd == 3 else pe.go(f)
            if c == 0:
                t = CP(SA[:, 0, :], sl.ap[:, 0:256], t, *stt["xl"])
            else:
                for m in range(2):
                    tt = STT(SA[:, c, P * m:P * m + P], SA[:, c - 1, P * m:P * m + P], gx[:, 8 * m + c - 1:8 * m + c],
                             sl.ap[:, P * m:P * m + P], MUL, ADD, t, stt["dec"], stt["s"])
                t = tt
            sl.busy = [t]
            stt["s"] = t

        fill.append(decays)
        fill.append(lambda: kd_turn(0))
        fill.append(lambda: kd_turn(1))
        fill.append(meta_state)
        for c in range(1, 8):
            fill.append(lambda c=c: kv_mm(c, lambda h: KDT[:, c - 1, 64 * h:64 * h + 64],
                                          lambda h: V[:, c - 1, P * h:P * h + P], stt["kdt0"], stt["kdt1"], stt["v"]))

        def fills(n):
            for _ in range(n):
                if fill:
                    fill.pop(0)()

        for m in range(4):
            sl, tok = job(f"v{m}", h, 8, meta=True)
            tt_ = turn_now()
            if tt_:
                stt["v"] = tt_
            b = tring.take()
            t = TT(b.ap[:], sl.ap[:], RT[:], MUL, tok, *b.busy)
            sl.busy = [t]
            turned(b, t, V[:, :, P * m:P * m + P], *gfree)
            t = TT(EV[:], misc.ap[:, 0:NMETA], rmt[:], MUL, tok, *stt.get("evfree", xfree))
            te = pe.op(lambda e: e.transpose(misc.ap[0:NMETA, 512:512 + P], EV[:], ident[:]), t)
            stt["evfree"] = [te]
            stt["vm"] = CP(VM[:, P * m:P * m + P], misc.ap[0:NMETA, 512:512 + P], te, *xfree)
            misc.busy = [stt["vm"]]
            fills(3)
        dsg = [Dsem(f"sg{m}") for m in range(4)]
        tsg = []
        for m in range(4):
            sl, tok = job(f"g{m}", h, 8)
            if m == 0:
                stt["v"] = turn_now()
            b = tring.take()
            t = TT(b.ap[:], sl.ap[:], RT[:], MUL, tok, *b.busy)
            sl.busy = [t]
            t = A(b.ap[:], b.ap[:], ACT.Silu, t)
            t = dma(sp, dsg[m], sgsc[:, m, :], b.ap[:], t)
            b.busy = [t]
            tsg.append(t)
            fills(3)
        dyc = [Dsem(f"yc{m}") for m in range(4)]
        tyc = []
        ufree = list(xfree)
        for m in range(4):
            def cw(k, m=m):
                return col("conv1", 3 * m + k)
            sl, tok = job(f"cc{m}", h, 8, meta=True)
            t = TT(U[:, 2:], sl.ap[:], RT[:], MUL, tok, *ufree)
            sl.busy = [t]
            tc2 = meta_out(U[:, 0:2], NMETA - 2, 2, tok, *ufree)
            fills(2)
            sl, tok = job(f"cx{m}", h, 8, meta=True)
            b = tring.take()
            tb1 = TT(b.ap[:], sl.ap[:], RT[:], MUL, tok, *b.busy)
            sl.busy = [tb1]
            t = TT(U[:, 2:], U[:, 2:], b.ap[:], MUL, tb1, t)
            tb1 = meta_out(EV[:, 0:2], NMETA - 2, 2, tok, *stt["evfree"])
            t2 = TT(U[:, 0:2], U[:, 0:2], EV[:, 0:2], MUL, tb1, tc2)
            t3 = A(b.ap[:], U[:, 2:], ACT.Copy, t, *b.busy, scale=cw(2))
            t4 = STT(b.ap[:], U[:, 1:1025], cw(1), b.ap[:], MUL, ADD, t3, t2)
            t5 = STT(b.ap[:], U[:, 0:1024], cw(0), b.ap[:], MUL, ADD, t4)
            ufree = [t5, t3]
            fills(2)
            sl, tok = job(f"cb{m}", h, 8)
            t = TT(b.ap[:], b.ap[:], sl.ap[:], MUL, tok, t5)
            sl.busy = [t]
            t = TT(b.ap[:], b.ap[:], RT[:], MUL, t)
            t = dma(sp, dyc[m], ysc[:, 4 + m, :], b.ap[:], t)
            b.busy = [t]
            tyc.append(t)
            fills(3)
        fills(len(fill))
        stt["rtfree"] = [dve.last]
        hfree = [pe.last]
        SG, Y = unit(HO, 0, [P, 4, S]), unit(HO, 4, [P, 8, S])
        dl = Dsem("sgl")
        tl = dma(sp, dl, SG[:], sgsc, *tsg, *hfree)
        dl2 = [Dsem(f"yl{m}") for m in range(4)]
        tyl = [dma(sp, dl2[m], Y[:, 4 + m, :], ysc[:, 4 + m, :], tyc[m], *hfree) for m in range(4)]
        st4 = Ring([Slot(st[:, 0:4]), Slot(st[:, 4:8])])
        yt = []

        def o_front(c):
            sl = pring.take()
            pe.wait(stt["at"], stt["qi"], stt["v"], stt["s"], *sl.busy)
            cs = slice(P * c, P * c + P)
            for hd in range(4):
                t_, hh = hd // 2, hd % 2
                oc = 512 * hh + P * t_
                pe.go(lambda e, hd=hd, oc=oc: e.matmul(sl.ap[:, oc:oc + P], AT[:, hd, cs], V[:, c, P * hd:P * hd + P], start=True, stop=False))
                f = lambda e, oc=oc, t_=t_, hh=hh: e.matmul(sl.ap[:, oc:oc + P], QI[64 * hh:64 * hh + 64, t_, cs], SA[64 * hh:64 * hh + 64, c, P * t_:P * t_ + P], start=False, stop=True)
                t = pe.op(f) if hd == 3 else pe.go(f)
            b = tring.take()
            s4 = st4.take()
            act.wait(*b.busy, *s4.busy)
            for hd in range(4):
                oc = 512 * (hd // 2) + P * (hd % 2)
                t5 = A(b.ap[:, 512 + P * hd:512 + P * hd + P], sl.ap[:, oc:oc + P], ACT.Square, t, accum=s4.ap[:, hd:hd + 1])
            t5 = A(s4.ap, s4.ap, ACT.Sqrt, t5, scale=1.0 / P, bias=epsc[:])
            t5 = dve.op(lambda e: e.reciprocal(s4.ap, s4.ap), t5)
            t5 = TT(b.ap[:, 0:512].rearrange("p (a b c) -> p a b c", a=2, b=2),
                    sl.ap[:].rearrange("p (a b c) -> p a b c", a=2, b=4)[:, :, 0:2, :],
                    s4.ap.rearrange("p (a b) -> p a b", a=2).unsqueeze(3).broadcast_to([P, 2, 2, P]), MUL, t5, *b.busy)
            sl.busy = [t5]
            s4.busy = [t5]
            return b, t5

        def o_back(c, b, t5):
            cs = slice(P * c, P * c + P)
            s2 = pring.take()
            pe.wait(t5, *s2.busy)
            for hd in range(4):
                at_ = P * (2 * (hd % 2) + hd // 2)
                f = lambda e, hd=hd, at_=at_: e.transpose(s2.ap[:, P * hd:P * hd + P], b.ap[:, at_:at_ + P], ident[:])
                t = pe.op(f) if hd == 3 else pe.go(f)
            b.busy = [t]
            t = STT(Y[:, 0:4, cs], v3(s2.ap[:, 0:512], 4), col("gla_norm"), SG[:, :, cs], MUL, MUL, t, tl)
            s2.busy = [t]
            return t

        def conv_rows(k):
            yh = GHs[k - 4]
            yl = [GHs[4], GHs[5], GLs[2], GLs[3]][k - 4]
            tyc4.append(split(Y[:, k, :], yh, yl, tyl[k - 4], *hfree, dve.last))

        tyc4 = []
        prev = None
        for c in range(8):
            if c in (2, 3, 4, 5):
                conv_rows(c + 2)
            cur = (c, *o_front(c))
            if prev:
                ty = o_back(*prev)
            prev = cur
        ty = o_back(*prev)
        gfree = [pe.last, ty]
        yh, yl = [GHs[k] for k in (4, 5, 6, 7, 0, 1, 2, 3)], [GLs[k] for k in (4, 5, 6, 7, 0, 1, 2, 3)]
        yl[4:8] = [GHs[4], GHs[5], GLs[2], GLs[3]]
        yh[0:4] = [GHs[6], GHs[7], GLs[0], GLs[1]]
        yl[0:4] = [GLs[k] for k in (4, 5, 6, 7)]
        toks = [split(Y[:, k, :], yh[k], yl[k], *gfree, q=(pool, dve)[k % 2]) for k in range(4)] + tyc4
        xfree = [pe.last, dve.last, act.last]
        xt = [dma(sp, dx[k], X[:, k, :], d["xT"][:, k, :], *xfree) for k in range(8)]
        yr = Rhs(yh, yl, toks, order=[4, 5, 6, 7, 0, 1, 2, 3])

        def add_to_x(name, r, toks, on_last):
            res = []
            for m in range(8):
                sl, tok = job(f"{name}{m}", r, 8)
                t = TT(X[:, m, :], sl.ap[:], X[:, m, :], ADD, tok, toks[m])
                sl.busy = [t]
                res.append(t)
                on_last(m, t)
            return res

        def feeder(norm, g, toks, *w):
            def on_last(m, t):
                if g is not None:
                    toks.append(weigh(m, X[:, m, :], g(m), HH, HL, t, *w))
                norm.feed(X[:, m, :], t)
            return on_last

        tsc = A(SC[:], col("c", 0, 8), ACT.Silu)

        ada = Ring([Slot(adat[:, 0, :]), Slot(adat[:, 1, :])])
        ada_due = []

        def ada_tile(f):
            i = ws.take(f"ada{f}")
            w_ = raw[i % 4][:].rearrange("p (k m) -> p k m", k=8)
            t = TT(w_, w_, SC[:].unsqueeze(2).broadcast_to([P, 8, P]), MUL, ws.landed[i], tsc, q=pool)
            a_ = ada.take()
            t = dve.op(lambda e: e.tensor_reduce(a_.ap, raw[i % 4][:].rearrange("p (k m) -> p m k", k=8), AX.X, ADD), t, *a_.busy)
            ws.done(i, t)

            def later():
                stt["ada"] = pe.op(lambda e: e.matmul(misc.ap[:, f:f + 1], a_.ap, ones[:, 0:1], start=True, stop=True), t, *(misc.busy if f == 0 else []))
                a_.busy = [stt["ada"]]
            ada_due.append(later)

        def ada_step(n):
            while ada_due:
                ada_due.pop(0)()
            if n % 2 and n < 96 and upto >= 3:
                ada_tile(n // 2)

        norm, htoks = Norm(1024), []
        xt = add_to_x("wo", yr, xt, feeder(norm, lambda k: col("norm_mlp", k), htoks, ty, *toks))
        hidden["free"] = [[pe.last], [pe.last]]
        h = Rhs(HHs, HLs, htoks)
        n2, htoks2 = Norm(1024, lambda k: col("norm_final", k)), []

        def on_last(m, t):
            feeder(n2, lambda k: gprod[:, k:k + 1], htoks2, stt["ups"])(m, t)

        xt = mlp("dn", *relu_up("up", h, norm), 8, X, [[t] for t in xt], norm=norm, on_last=on_last, step=ada_step)
        if upto >= 3:
            while ada_due:
                ada_due.pop(0)()
            stt["mod"] = TT(mod[:], misc.ap[:, 0:48], col("b_ada", 0, 48), ADD, stt["ada"])
            misc.busy = [stt["mod"]]

        if upto >= 2:
            h = Rhs(HHs, HLs, htoks2)
            gfree = [pe.last]
            sg0, tg0 = job("gg0", h, 8)
            n2.stats()
            sv0, tv0 = job("gv0", h, 8)
            n2.to_rt()
            s1, t1 = n2.first()
            for k in range(8):
                xt[k] = STT(X[:, k, :], X[:, k, :], col("norm_final", k), s1.ap[:], MUL, MUL, t1)
            s1.busy = [xt[-1]]
            tspill = [dma(sp, dx[k], xsc[:, k, :], X[:, k, :], xt[k]) for k in range(8)]
            xfree = [*tspill, dve.last, act.last]
            QA, KA, QB, KB = G(0, [P, 3, S]), G(3, [P, 3, S]), G(6, [P, 3, S]), G(9, [P, 3, S])
            VA, CF = G(12, [P, 8, 384]), G(15, [P, S])
            UC, YC, VB = unit(XO, 0, [P, 2, 1054]), unit(XO, 3, [P, 2, S]), unit(XO, 5, [P, 8, 384])
            ctok = [None, None]

            def gate_out(m, sg, tg, sv, tv):
                b = tring.take()
                t = TT(b.ap[:], sg.ap[:], RT[:], MUL, tg, n2.rt, *b.busy)
                sg.busy = [t]
                t = A(b.ap[:], b.ap[:], ACT.Sigmoid, t)
                t = TT(b.ap[:], b.ap[:], sv.ap[:], MUL, tv, t)
                sv.busy = [t]
                t = TT(UC[:, m, 30:], b.ap[:], RT[:], MUL, t, *xfree)
                b.busy = [t]
                ctok[m] = A(YC[:, m, :], UC[:, m, 30:], ACT.Identity, t, *xfree, scale=col("conv2", 31 * m + 30), bias=col("conv2_b", m))

            gate_out(0, sg0, tg0, sv0, tv0)
            tpad = pool.op(lambda e: e.memset(UC[:, :, 0:30], 0.0), *xfree)
            sg0, tg0 = job("gg1", h, 8)
            sv0, tv0 = job("gv1", h, 8)
            gate_out(1, sg0, tg0, sv0, tv0)
            dve.wait(tpad)

            def taps(m, k0, k1):
                for k in range(k0, k1):
                    ctok[m] = STT(YC[:, m, :], UC[:, m, k:k + S], col("conv2", 31 * m + k), YC[:, m, :], MUL, ADD, ctok[m])

            def ln_mean():
                pe.wait(*ctok, *misc.busy)
                for hf in range(2):
                    cs = slice(512 * hf, 512 * hf + 512)
                    for m in range(2):
                        t = pe.op(lambda e, m=m, cs=cs: e.matmul(misc.ap[:, cs], ones[:], YC[:, m, cs], start=(m == 0), stop=(m == 1)))
                for m in range(2):
                    ctok[m] = STT(YC[:, m, :], misc.ap[:], -1.0 / 256, YC[:, m, :], MUL, ADD, t)
                misc.busy = [dve.last]

            def ln_rest():
                nl = Norm(256)
                for m in range(2):
                    nl.feed(YC[:, m, :], ctok[m])
                nl.stats()
                sl, tR = nl.spread()
                for m in range(2):
                    t = STT(YC[:, m, :], YC[:, m, :], col("cn_g", m), sl.ap[:], MUL, MUL, tR)
                    ctok[m] = A(YC[:, m, :], YC[:, m, :], ACT.Silu, t, bias=col("cn_b", m))
                sl.busy = [dve.last]

            fill = []
            for m in range(2):
                for k in range(0, 30, 5):
                    fill.append(lambda m=m, k=k: taps(m, k, k + 5))
            fill += [ln_mean, ln_rest]

            sl, tok = job("fa", h, 8, m=W2)
            a6, b6, o6 = T[0], T[1], T[2]
            for s_ in (a6, b6, o6):
                act.wait(*s_.busy)
                dve.wait(*s_.busy)
            t = TT(o6.ap[0:6, :], sl.ap[0:6, :], RT[0:6, :], MUL, tok)
            sl.busy = [t]
            g_, ta, tb_ = logsig(o6.ap[0:6, :], cols[0:6, COLS["b_forget"][0]:COLS["b_forget"][0] + 1], a6.ap[0:6, :], b6.ap[0:6, :], a6.ap[0:6, :], t)
            t1 = dve.op(lambda e: e.memset(o6.ap[0:6, :], 1.0), ta, tb_)
            tcf = dve.op(lambda e: e.tensor_tensor_scan(CF[0:6, :], o6.ap[0:6, :], a6.ap[0:6, :], 0.0, MUL, ADD), t1, g_, *gfree)
            for s_ in (a6, b6, o6):
                s_.busy = [tcf]
            tq2 = []

            def proj(n, dst, scale=1.0):
                for m in range(3):
                    sl, tok = job(f"{n}{m}", h, 8)
                    turn_now()
                    t = STT(dst[:, m, :], sl.ap[:], scale, RT[:], MUL, MUL, tok, *gfree)
                    sl.busy = [t]
                    fills(1)
                return t

            def projv(n, dst, *w):
                for m in range(3):
                    sl, tok = job(f"{n}{m}", h, 8)
                    turn_now()
                    b = tring.take()
                    t = TT(b.ap[:], sl.ap[:], RT[:], MUL, tok, *b.busy)
                    sl.busy = [t]
                    turned(b, t, dst[:, :, P * m:P * m + P], *w)
                    fills(1)

            projv("vb", VB, *xfree)
            turn_now()
            tvb = act.last
            vsc = nc.dram_tensor("vsc", (S, 384), F, kind="Internal").ap()
            dv_ = Dsem("vs")
            tvs = dma(sp, dv_, vsc.rearrange("(b p) c -> p b c", p=P), VB[:], tvb)
            proj("qb", QB, 0.125)
            proj("kb", KB)
            projv("va", VA, *gfree)
            proj("qa", QA, 0.125)
            proj("ka", KA)
            turn_now()
            fills(len(fill))
            stt["rtfree"] = [dve.last]
            tproj = dve.last
            tva = act.last
            hfree = [pe.last]

            def Hu(n, shape, dt=F):
                return unit(HO, n, shape, dt)

            sring = Ring([Slot(Hu(0, [P, S])), Slot(Hu(1, [P, S]))])
            prng = Ring([Slot(Hu(2, [P, S])), Slot(Hu(3, [P, S]))])
            ptring = Ring([Slot(Hu(4, [P, S])), Slot(Hu(5, [P, S]))])
            CN = Hu(6, [P, 6, S])
            SEL = Hu(12, [6, 6, P])
            V4, V16 = Hu(13, [P, 8, 384]), unit(XO, 0, [P, 8, 384])
            dsel, dv4, dv16 = Dsem("sel"), Dsem("v4"), Dsem("v16")
            tsel = dma(sp, dsel, SEL[:], d["sel"], *hfree)
            for n in range(2):
                tv4 = dma(sp, dv4, V4[:, 4 * n:4 * n + 4, :], vsc[512 * n:512 * n + 512, :].rearrange("(j r) c -> j r c", r=4), tvs, *hfree)
            tv16 = dma(sp, dv16, V16[:], vsc.rearrange("(j u) c -> j u c", u=8), tvs, *ctok)
            gate_toks = []

            def gate_sums(hd):
                sl = pring.take()
                pe.wait(tsel, tcf, *sl.busy)
                for hf in range(2):
                    t = pe.op(lambda e, hf=hf, hd=hd: e.matmul(sl.ap[:, 512 * hf:512 * hf + 512], SEL[0:6, hd, :], CF[0:6, 512 * hf:512 * hf + 512], start=True, stop=True))
                gate_toks.append(A(CN[:, hd, :], sl.ap[:], ACT.Copy, t, *hfree, scale=-1.0))
                sl.busy = [gate_toks[-1]]

            stat = Ring([Slot(st), Slot(rr)])
            mhalf = [Slot(misc.ap[:, 0:512]), Slot(misc.ap[:, 512:1024])]
            lz = const([P, 16])
            lzs = [Slot(lz[:, 0:8]), Slot(lz[:, 8:16])]
            ystoks = []
            YF, YD = unit(XO, 0, [P, 3, S]), unit(XO, 5, [P, 3, S])
            yring = Ring([Slot(CF[:, 0:512]), Slot(CF[:, 512:1024])])

            def pt_copy(n, dst, src, *w):
                if n % 2:
                    return A(dst, src, ACT.Copy, *w)
                return CP(dst, src, *w)

            def rms_rows(b, i, gname, dst, t):
                s_ = stat.take()
                b2 = yring.take()
                t2 = A(b2.ap[:, 0:384], b.ap[:, 0:384], ACT.Square, t, *b2.busy, *s_.busy, accum=s_.ap[:, 0:1])
                t2 = A(s_.ap[:, 1:2], s_.ap[:, 0:1], ACT.Sqrt, t2, scale=1.0 / 384, bias=epsc[:])
                t2 = dve.op(lambda e: e.reciprocal(s_.ap[:, 2:3], s_.ap[:, 1:2]), t2)
                t2 = TS(b.ap[:, 0:384], b.ap[:, 0:384], s_.ap[:, 2:3], None, MUL, None, t2)
                s_.busy = [t2]

                def back():
                    sl = pring.take()
                    pe.wait(t2, *sl.busy)
                    for m in range(3):
                        f = lambda e, m=m: e.transpose(sl.ap[:, P * m:P * m + P], b.ap[:, P * m:P * m + P], ident[:])
                        t = pe.op(f) if m == 2 else pe.go(f)
                    b.busy = [t]
                    for m in range(3):
                        t3 = TS(dst[:, m, P * i:P * i + P], sl.ap[:, P * m:P * m + P], col(gname, m), None, MUL, None, t, *ydfree)
                    sl.busy = [t3]
                    ystoks.append(t3)
                    b2.busy = [t3]
                return back

            units = [(i, hd) for i in range(7, -1, -1) for hd in range(6)]

            def scores(i, hd):
                t_, hh = hd // 2, hd % 2
                ps_ = slice(64 * hh, 64 * hh + 64)
                w = P * (i + 1)
                sl = pring.take()
                pe.wait(tproj, *sl.busy)
                for hf in range(-(-w // 512)):
                    n = min(512, w - 512 * hf)
                    diag = hf == (P * i) // 512
                    pe.go(lambda e, hf=hf, n=n, diag=diag: e.matmul(sl.ap[:, 512 * hf:512 * hf + n], QA[ps_, t_, P * i:P * i + P], KA[ps_, t_, 512 * hf:512 * hf + n], start=True, stop=not diag))
                t = pe.op(lambda e: e.matmul(sl.ap[:, P * i:P * i + P], identb[:], negm[:, 1, :], start=False, stop=True))
                return sl, t

            def soft(i, hd, sl, t):
                w = P * (i + 1)
                s_, p_ = sring.take(), prng.take()
                l_ = lzs[i % 2]
                mx = stat.take()
                t = dve.op(lambda e: e.tensor_tensor_reduce(out=s_.ap[:, 0:w], in0=sl.ap[:, 0:w], in1=CN[:, hd, 0:w], scale=-1.0, scalar=3.0e38, op0=ADD, op1=MIN, accum_out=mx.ap[:, 0:1]), t, gate_toks[hd], *s_.busy, *mx.busy)
                sl.busy = [t]
                t = A(p_.ap[:, 0:w], s_.ap[:, 0:w], ACT.Exp, t, *p_.busy, *(l_.busy if hd == 0 else []), scale=-1.0, bias=mx.ap[:, 0:1], accum=l_.ap[:, hd:hd + 1])
                s_.busy = [t]
                mx.busy = [t]
                return p_, t

            def turn(blocks, p_, t, n):
                sl = pring.take()
                pe.wait(t, *sl.busy)
                for j in range(blocks):
                    f = lambda e, j=j: e.transpose(sl.ap[:, P * j:P * j + P], p_.ap[:, P * j:P * j + P], ident[:])
                    t = pe.op(f) if j == blocks - 1 else pe.go(f)
                p_.busy = [t]
                q_ = ptring.take()
                t = pt_copy(n, q_.ap[:, 0:P * blocks], sl.ap[:, 0:P * blocks], t, *q_.busy)
                sl.busy = [t]
                return q_, t

            def fox_pv(i, hd, q_, t):
                mh = mhalf[i % 2]
                pe.wait(t, tva, *(mh.busy if hd == 0 else []))
                for j in range(i + 1):
                    f = lambda e, j=j: e.matmul(mh.ap[:, 64 * hd:64 * hd + 64], q_.ap[:, P * j:P * j + P], VA[:, j, 64 * hd:64 * hd + 64], start=(j == 0), stop=(j == i))
                    t = pe.op(f) if j == i else pe.go(f)
                q_.busy = [t]
                return t

            def fox_out(i, t):
                mh, l_ = mhalf[i % 2], lzs[i % 2]
                b = tring.take()
                t2 = dve.op(lambda e: e.reciprocal(l_.ap[:, 0:6], l_.ap[:, 0:6]), act.last)
                t2 = TT(v3(b.ap[:, 0:384], 6), v3(mh.ap[:, 0:384], 6), l_.ap[:, 0:6].unsqueeze(2).broadcast_to([P, 6, 64]), MUL, t2, t, *b.busy)
                mh.busy = [t2]
                l_.busy = [t2]
                return rms_rows(b, i, "fox", YF, t2)

            dsc = nc.dram_tensor("dsc", (3, S, 396), F, kind="Internal").ap()
            ddo = [Dsem(f"do{i}") for i in range(3)]

            def dtok(ap, br, u, prev):
                if br == 0:
                    return ap[:, P * (u - prev):P * u + P]
                if br == 1:
                    return ap.rearrange("p (j r) -> p r j", r=4)[:, u % 4, P * (u // 4 - prev):P * (u // 4) + P]
                return ap.rearrange("p (j u) -> p u j", u=8)[:, u, :]

            dun = [(br, u, t_) for br in range(3) for u in range(8) for t_ in range(3)]

            def has_prev(br, u):
                return int((br == 0 and u > 0) or (br == 1 and u >= 4))

            def dscores(br, u, t_):
                pv_ = has_prev(br, u)
                w = P * (1 + pv_)
                sl = pring.take()
                pe.wait(tproj, *sl.busy)
                for hh in range(2):
                    ps_ = slice(64 * hh, 64 * hh + 64)
                    q_ = dtok(QB[ps_, t_, :], br, u, 0)
                    k_ = dtok(KB[ps_, t_, :], br, u, pv_)
                    o_ = sl.ap[:, 512 * hh:512 * hh + w]
                    pe.go(lambda e, o_=o_, q_=q_, k_=k_: e.matmul(o_, q_, k_, start=True, stop=False))
                for hh in range(2):
                    mk = 2 if br == 2 else 1 - pv_
                    f = lambda e, hh=hh, mk=mk: e.matmul(sl.ap[:, 512 * hh:512 * hh + w], identb[:], negm[:, mk:mk + 1 + pv_, :].rearrange("p a b -> p (a b)"), start=False, stop=True)
                    t = pe.op(f) if hh == 1 else pe.go(f)
                return sl, t

            dcur = {}

            def dsoft(br, u, t_, sl, t):
                w = P * (1 + has_prev(br, u))
                if t_ == 0:
                    dcur[(br, u)] = tring.take()
                    act.wait(*dcur[(br, u)].busy)
                    dve.wait(*dcur[(br, u)].busy)
                o_ = dcur[(br, u)]
                p_ = prng.take()
                sv = v3(sl.ap[:], 2)[:, :, 0:w]
                t = dve.op(lambda e: e.tensor_reduce(o_.ap[:, 384 + 2 * t_:386 + 2 * t_], sv, AX.X, MAX, negate=True), t)
                for hh in range(2):
                    c_ = 2 * t_ + hh
                    t2 = A(p_.ap[:, w * hh:w * hh + w], sl.ap[:, 512 * hh:512 * hh + w], ACT.Exp, t, *p_.busy, bias=o_.ap[:, 384 + c_:385 + c_], accum=o_.ap[:, 390 + c_:391 + c_])
                sl.busy = [t2]
                return p_, t2

            def dpv(br, u, t_, q_, t, cnt):
                nb = 1 + has_prev(br, u)
                mh = mhalf[cnt % 2]
                pe.wait(t, tv4, tv16, *(mh.busy if t_ == 0 else []))
                for hh in range(2):
                    hd = 2 * t_ + hh
                    for j in range(nb):
                        if br == 0:
                            v_ = VB[:, u - nb + 1 + j, :]
                        elif br == 1:
                            v_ = V4[:, 4 * (u // 4 - nb + 1 + j) + u % 4, :]
                        else:
                            v_ = V16[:, u, :]
                        f = lambda e, hd=hd, j=j, hh=hh, v_=v_: e.matmul(mh.ap[:, 64 * hd:64 * hd + 64], q_.ap[:, P * (nb * hh + j):P * (nb * hh + j) + P], v_[:, 64 * hd:64 * hd + 64], start=(j == 0), stop=(j == nb - 1))
                        t = pe.op(f) if hh == 1 and j == nb - 1 else pe.go(f)
                q_.busy = [t]
                return t

            def dout_(br, u, t, cnt):
                mh = mhalf[cnt % 2]
                o_ = dcur.pop((br, u))
                t = CP(o_.ap[:, 0:384], mh.ap[:, 0:384], t)
                mh.busy = [t]
                ds = ddo[cnt % 3]
                if br == 0:
                    t = dma(sp, ds, dsc[0, P * u:P * u + P, :], o_.ap[:, 0:396], t, act.last)
                elif br == 1:
                    n_, r_ = u // 4, u % 4
                    t = dma(sp, ds, dsc[1, 512 * n_:512 * n_ + 512, :].rearrange("(j r) c -> r j c", r=4)[r_], o_.ap[:, 0:396], t, act.last)
                else:
                    t = dma(sp, ds, dsc[2].rearrange("(j u) c -> u j c", u=8)[u], o_.ap[:, 0:396], t, act.last)
                o_.busy = [t]
                return t

            stage = {}
            n = len(dun)
            dall = {}
            for s_i in range(n + 3):
                if s_i < n:
                    stage[s_i] = dscores(*dun[s_i])
                if s_i >= 1 and s_i - 1 < n:
                    stage[s_i - 1] = dsoft(*dun[s_i - 1], *stage[s_i - 1])
                if s_i >= 2 and s_i - 2 < n:
                    u = dun[s_i - 2]
                    stage[s_i - 2] = turn(2 * (1 + has_prev(u[0], u[1])), *stage[s_i - 2], s_i)
                if s_i >= 3:
                    u = dun[s_i - 3]
                    cnt = u[0] * 8 + u[1]
                    t = dpv(*u, *stage.pop(s_i - 3), cnt)
                    if u[2] == 2:
                        dall[cnt % 3] = dout_(u[0], u[1], t, cnt)
                    if s_i % 10 == 5 and s_i < 60:
                        gate_sums(s_i // 10)

            ydfree = [pe.last]
            for s_ in yring.slots:
                s_.busy = [gate_toks[-1]]
            cm = [at(GO + 6 * 4096 + 5376 * i, [P, 3, 448]) for i in range(2)]
            dcm = [Dsem("cm0"), Dsem("cm1")]
            loaded = {}

            def join_load(i, *w):
                loaded[i] = dma(sp, dcm[i % 2], cm[i % 2][:, :, 0:396], dsc[:, P * i:P * i + P, :].rearrange("a p c -> p a c"), *w)

            for i in range(2):
                join_load(i, *dall.values(), pe.last)

            def join(i):
                C = cm[i % 2]
                tl_ = loaded[i]
                mm_, ll_ = C[:, :, 384:390], C[:, :, 390:396]
                t = TT(C[:, 0, 400:406], mm_[:, 0, :], mm_[:, 1, :], MIN, tl_)
                t = TT(C[:, 0, 400:406], C[:, 0, 400:406], mm_[:, 2, :], MIN, t)
                t = TT(C[:, :, 410:416], C[:, 0:1, 400:406].broadcast_to([P, 3, 6]), mm_, SUB, t)
                t = A(C[:, :, 410:416], C[:, :, 410:416], ACT.Exp, t)
                t1 = TT(C[:, :, 420:426], C[:, :, 410:416], ll_, MUL, t)
                t1 = TT(C[:, 0, 420:426], C[:, 0, 420:426], C[:, 1, 420:426], ADD, t1)
                t1 = TT(C[:, 0, 420:426], C[:, 0, 420:426], C[:, 2, 420:426], ADD, t1)
                t1 = dve.op(lambda e, C=C: e.reciprocal(C[:, 0, 430:436], C[:, 0, 420:426]), t1)
                for br in range(3):
                    v_ = v3(C[:, br, 0:384], 6)
                    t2 = TT(v_, v_, C[:, br, 410:416].unsqueeze(2).broadcast_to([P, 6, 64]), MUL, t)
                t2 = TT(C[:, 0, 0:384], C[:, 0, 0:384], C[:, 1, 0:384], ADD, t2)
                t2 = TT(C[:, 0, 0:384], C[:, 0, 0:384], C[:, 2, 0:384], ADD, t2)
                b = tring.take()
                t2 = TT(v3(b.ap[:, 0:384], 6), v3(C[:, 0, 0:384], 6), C[:, 0, 430:436].unsqueeze(2).broadcast_to([P, 6, 64]), MUL, t2, t1, *b.busy)
                if i + 2 < 8:
                    join_load(i + 2, t2)
                return rms_rows(b, i, "dil", YD, t2)

            backs = []
            n = len(units)
            for s_i in range(n + 3):
                if s_i < n:
                    stage[s_i] = scores(*units[s_i])
                if s_i >= 1 and s_i - 1 < n:
                    stage[s_i - 1] = soft(*units[s_i - 1], *stage[s_i - 1])
                if s_i >= 2 and s_i - 2 < n:
                    u = units[s_i - 2]
                    stage[s_i - 2] = turn(u[0] + 1, *stage[s_i - 2], s_i)
                if s_i % 6 == 5 and s_i < 48:
                    joined = join(s_i // 6)
                elif s_i % 6 == 2 and s_i > 5:
                    joined()
                if s_i >= 3:
                    u = units[s_i - 3]
                    t = fox_pv(*u, *stage.pop(s_i - 3))
                    if backs and u[1] == 2:
                        backs.pop()()
                    if u[1] == 5:
                        backs.append(fox_out(u[0], t))
            while backs:
                backs.pop()()

            gfree = [pe.last, dve.last, act.last]
            ys = [YF[:, 0, :], YF[:, 1, :], YF[:, 2, :], YD[:, 0, :], YD[:, 1, :], YD[:, 2, :], YC[:, 0, :], YC[:, 1, :]]
            toks = [None] * 8
            for j, k in enumerate((3, 4, 5, 6, 7, 0, 1, 2)):
                toks[k] = split(ys[k], GHs[k], GLs[k], *gfree, q=(pool, dve)[j % 2])
            xfree = [pool.last, dve.last]
            xt = [dma(sp, dx[k], X[:, k, :], xsc[:, k, :], *xfree) for k in range(8)]
            misc.busy = [dve.last, act.last]
            norm, htoks = Norm(1024), []
            xt = add_to_x("w2o", Rhs(GHs, GLs, toks, order=[3, 4, 5, 6, 7, 0, 1, 2]), xt, feeder(norm, lambda k: col("ln2", k), htoks, *toks))
            hidden["free"] = [[pe.last], [pe.last]]
            h = Rhs(HHs, HLs, htoks)
            def up_job(m, mid):
                got = job(f"fupa{m}", h, 8)
                if mid:
                    mid()
                got = (*got, *job(f"fupb{m}", h, 8))
                return got

            def conv_drain(sl, tok, f):
                b0 = tring.take()
                t0 = TT(b0.ap[:], sl.ap[:], RT[:], MUL, tok, norm.rt, *b0.busy)
                sl.busy = [t0]
                b = tring.take()
                t = A(b.ap[:], b0.ap[:], ACT.Identity, t0, *b.busy, scale=col("ffn_w", 3 * f + 2), bias=col("ffn_b", f))
                t = STT(b.ap[:, 1:], b0.ap[:, 0:S - 1], col("ffn_w", 3 * f + 1), b.ap[:, 1:], MUL, ADD, t)
                t = STT(b.ap[:, 2:], b0.ap[:, 0:S - 2], col("ffn_w", 3 * f), b.ap[:, 2:], MUL, ADD, t)
                b0.busy = [t]
                return b, t

            def up_drain(m, got):
                sa, ta, sb_, tb_ = got
                a_, ta = conv_drain(sa, ta, m)
                ta = A(a_.ap[:], a_.ap[:], ACT.Silu, ta)
                b_, tb2 = conv_drain(sb_, tb_, NPAIR + m)
                t = TT(a_.ap[:], a_.ap[:], b_.ap[:], MUL, ta, tb2)
                b_.busy = [t]
                return a_, t

            n3 = Norm(1024, lambda k: col("g_final", k))
            xt = mlp("fdn", up_job, up_drain, 6, X, [[t] for t in xt], sizes=[4] * 5 + [2], norm=norm,
                     on_last=lambda m, t: n3.feed(X[:, m, :], t))
        if upto >= 3:
            gains = const([P, 32])
            for j, (m0, name, one) in enumerate(((8, "n1pre", 1.0), (16, "n1post", 0.0), (32, "n2pre", 1.0), (40, "n2post", 0.0))):
                tg = STT(gains[:, 8 * j:8 * j + 8], mod[:, m0:m0 + 8], one, col(name, 0, 8), ADD, MUL, stt["mod"])

            tg = TT(gprod[:, 8:16], gains[:, 0:8], col("g_final", 0, 8), MUL, tg)
            dve.wait(tg)

            def gain(j):
                return lambda k: gains[:, 8 * j + k:8 * j + k + 1]

            hfree, gfree = [pe.last], [pe.last, tg]
            UU, VT, YB, MIX = G(0, [P, 4, S]), G(4, [P, 8, 512]), G(8, [P, 4, S]), G(8, [P, 8, S])
            so = GO + 12 * 4096
            WSP, BSP, GNB, BNB, WPL = (at(so + 2048 * i, [P, 512]) for i in range(5))
            TRI = at(so + 10240, [P, P])
            BST = at(so + 10752, [P, 8, 6])
            MV = at(so + 10752 + 192, [P, 8, 2])
            RV = at(so + 10752 + 256, [P, 8])
            PBI = at(so + 10752 + 288, [P, 4])
            ds3 = Dsem("b3")
            dma(sp, ds3, v3(WSP[:], 4), d["w_sp"], *gfree)
            dma(sp, ds3, v3(WPL[:], 4), d["w_pool"], *gfree)
            dma(sp, ds3, TRI[:], d["tri"], *gfree)
            dma(sp, ds3, v3(BSP[:], 4), d["b_sp"].unsqueeze(0).broadcast_to([P, 4, P]), *gfree)
            dma(sp, ds3, GNB[:], d["lnv_g"].unsqueeze(0).broadcast_to([P, 512]), *gfree)
            t3 = dma(sp, ds3, BNB[:], d["lnv_b"].unsqueeze(0).broadcast_to([P, 512]), *gfree)
            n3.stats()
            sR, tR = n3.spread()
            h = normed(xs, lambda k: gprod[:, 8 + k:9 + k], sR, tR, HH, HL, *hfree, shift=lambda k: mod[:, k:k + 1])
            s1, t1 = n3.first()
            for k in range(8):
                xt[k] = STT(X[:, k, :], X[:, k, :], col("g_final", k), s1.ap[:], MUL, MUL, t1, act.last)
            s1.busy = [xt[-1]]
            twsp = TT(v3(WSP[:], 4), v3(WSP[:], 4), TRI[:].unsqueeze(1).broadcast_to([P, 4, P]), MUL, t3)
            tpb = TT(PBI[:], col("b_pool", 0, 4), col("pscale", 0, 4), MUL, t3)

            for m in range(4):
                sl, tok = job(f"zv{m}", h, 8)
                turn_now()
                b = tring.take()
                tv = A(b.ap[:], sl.ap[:], ACT.Gelu_apprx_tanh, tok, *b.busy)
                sl.busy = [tv]
                turned(b, tv, VT[:, :, P * m:P * m + P], *gfree)

            def ln_rows(tv):
                for c in range(8):
                    t = dve.op(lambda e, c=c: e.bn_stats(BST[:, c, :], VT[:, c, :]), tv, t3)
                for c in range(8):
                    t2 = dve.op(lambda e, c=c: e.bn_aggr(MV[:, c, :], BST[:, c, :]), t)
                t2 = A(RV[:], MV[:, :, 1], ACT.Sqrt, t2, bias=epsc[:])
                t2 = dve.op(lambda e: e.reciprocal(RV[:], RV[:]), t2)
                for c in range(8):
                    t2 = TS(VT[:, c, :], VT[:, c, :], MV[:, c, 0:1], RV[:, c:c + 1], SUB, MUL, t2)
                for hf in range(2):
                    v_ = VT[:, 4 * hf:4 * hf + 4, :]
                    t2 = TT(v_, v_, GNB[:].unsqueeze(1).broadcast_to([P, 4, 512]), MUL, t2)
                    stt["vt"] = TT(v_, v_, BNB[:].unsqueeze(1).broadcast_to([P, 4, 512]), ADD, t2, q=pool)

            utok = {}

            def spatial(m):
                sl = pring.take()
                pe.wait(stt["vt"], twsp, *sl.busy)
                for c in range(8):
                    f = lambda e, c=c: e.matmul(sl.ap[:, P * c:P * c + P], VT[:, c, P * m:P * m + P], WSP[:, P * m:P * m + P], start=True, stop=True)
                    t = pe.op(f) if c == 7 else pe.go(f)
                b = tring.take()
                t = TT(v3(b.ap[:], 8), v3(sl.ap[:], 8), BSP[:, P * m:P * m + P].unsqueeze(1).broadcast_to([P, 8, P]), ADD, t, *b.busy)
                sl.busy = [t]
                utok[m] = TT(UU[:, m, :], UU[:, m, :], b.ap[:], MUL, t, utok[m])
                b.busy = [utok[m]]

            for m in range(4):
                sl, tok = job(f"zu{m}", h, 8)
                if m == 0:
                    ln_rows(turn_now())
                utok[m] = A(UU[:, m, :], sl.ap[:], ACT.Gelu_apprx_tanh, tok, *gfree)
                sl.busy = [utok[m]]
            ybt = {}
            pend = None

            def pool_out(m, z, t):
                sl = pring.take()
                pe.wait(t, t3, *sl.busy)
                for hf in range(2):
                    cs = slice(512 * hf, 512 * hf + 512)
                    f = lambda e, cs=cs: e.matmul(sl.ap[:, cs], WPL[:, P * m:P * m + P], z.ap[:, cs], start=True, stop=True)
                    t = pe.op(f) if hf else pe.go(f)
                z.busy = [t]
                ybt[m] = A(YB[:, m, :], sl.ap[:], ACT.Identity, t, tpb, *gfree, scale=col("pscale", m), bias=PBI[:, m:m + 1])
                sl.busy = [ybt[m]]

            for m in range(4):
                sl, tok = job(f"zb{m}", h, 8)
                spatial(m)
                z = tring.take()
                t = A(z.ap[:], sl.ap[:], ACT.Copy, tok, *z.busy)
                sl.busy = [t]
                a_ = tring.take()
                b_ = tring.take() if m else None
                src = z
                bufs = [a_, b_]
                dve.wait(*a_.busy, *(b_.busy if b_ else []))
                for j in range(m + 1):
                    s_ = 1 << j
                    o_ = bufs[j % 2]
                    t1 = CP(o_.ap[:, 0:s_], src.ap[:, 0:s_], t)
                    t = TT(o_.ap[:, s_:], src.ap[:, s_:], src.ap[:, 0:S - s_], ADD, t, t1)
                    src = o_
                w_ = 2 << m
                t1 = TT(src.ap[:, 0:16], src.ap[:, 0:16], col("rcnt", 16 * m, 16), MUL, t)
                t1 = TT(z.ap[:, 0:16], src.ap[:, 0:16], z.ap[:, 0:16], SUB, t1)
                t = STT(z.ap[:, 16:], src.ap[:, 16:], 1.0 / w_, z.ap[:, 16:], MUL, SUB, t, t1)
                a_.busy = [t]
                if b_:
                    b_.busy = [t]
                pool_out(m, z, t)
            hfree = [pe.last]
            toks = [split(UU[:, k, :], HH[:, k, :], HL[:, k, :], utok[k], *hfree) for k in range(4)]
            toks += [split(YB[:, k, :], HH[:, 4 + k, :], HL[:, 4 + k, :], ybt[k], *hfree) for k in range(4)]
            yr = Rhs(HHs, HLs, toks)
            nm = Norm(1024)
            for m in range(8):
                sl, tok = job(f"wo3{m}", yr, 8)
                t = A(MIX[:, m, :], sl.ap[:], ACT.Copy, tok, *toks)
                sl.busy = [t]
                nm.feed(MIX[:, m, :], t)
            nm.stats()
            sR, tR = nm.spread()
            xt2 = []
            nx = Norm(1024)
            for k in range(8):
                t = STT(MIX[:, k, :], MIX[:, k, :], gain(1)(k), sR.ap[:], MUL, MUL, tR, nm.t)
                t = TT(X[:, k, :], X[:, k, :], MIX[:, k, :], ADD, t)
                nx.feed(X[:, k, :], t)
                xt2.append(t)
            sR.busy = [t]
            hidden["free"] = [[pe.last, t], [pe.last, t]]
            nx.stats()
            sR, tR = nx.spread()
            h = normed(xs, gain(2), sR, tR, HH, HL, pe.last, shift=lambda k: mod[:, 24 + k:25 + k])
            tsp = [[dma(sp, dx[k], xsc[:, k, :], X[:, k, :], xt2[k]), dve.last, act.last] for k in range(8)]
            nf = Norm(1024)
            XR = unit(HO, 0, [P, 8, S])
            dxr = [Dsem(f"xr{k}") for k in range(8)]
            xr = []

            def on_last(m, t):
                if m == 0:
                    xr.extend(dma(sp, dxr[k], XR[:, k, :], xsc[:, k, :], stt["ups"], *tsp[k]) for k in range(8))
                nf.feed(X[:, m, :], t)

            ft = mlp("fa2_", *relu_up("fa1_", h, None), 8, X, [list(t) for t in tsp], first_copy=True, on_last=on_last)
            nf.stats()
            sR, tR = nf.spread()
            dout = Dsem("out")
            for k in range(8):
                t = STT(X[:, k, :], X[:, k, :], gain(3)(k), sR.ap[:], MUL, MUL, tR, act.last)
                t = TT(XR[:, k, :], XR[:, k, :], X[:, k, :], ADD, t, xr[k])
                t = dma(sp, dout, out[:, k, :], XR[:, k, :], t)
            sp.wait(t)
        else:
            dout = Dsem("out")
            for k in range(8):
                t = dma(sp, dout, out[:, k, :], X[:, k, :], xt[k])
            sp.wait(t)
        assert ws.cur == len(wl), (ws.cur, len(wl))

        block = ctx.enter_context(nc.Block())

        @block.sync
        def _(e):
            sp.run(e)

        @block.scalar
        def _(e):
            act.run(e)

        @block.vector
        def _(e):
            dve.run(e)

        @block.gpsimd
        def _(e):
            pool.run(e)

        @block.tensor
        def _(e):
            pe.run(e)



def layout(inputs):
    g = {k: np.asarray(v) for k, v in inputs.items()}

    def tiles(w):
        k, m = w.shape
        return np.ascontiguousarray(w.reshape(k // P, P, m // P, P).transpose(2, 1, 0, 3)).reshape(m // P, P, k)

    def colv(v):
        return v.reshape(-1, P).T

    a = {}
    a["xT"] = np.ascontiguousarray(g["x"][0].T.reshape(8, P, S).transpose(1, 0, 2))
    a["metaT"] = np.ascontiguousarray(g["meta_tokens"].T.reshape(8, P, NMETA).transpose(1, 0, 2))
    w = g["w_in"][0]
    a["w_in"] = tiles(np.concatenate([w[:, :1536], w[:, 1552:]], axis=1))
    a["w_gr"] = np.ascontiguousarray(w[:, 1536:1552].reshape(8, P, 16).transpose(1, 0, 2)).reshape(P, 128)
    a["w_gate_up"] = g["w_gate_up"][0]
    a["w_out"], a["w_up"], a["w_down"] = tiles(g["w_out"][0]), tiles(g["w_up"][0]), tiles(g["w_down"][0])
    w = g["w_in_2"][0]
    a["w_in2"] = tiles(np.concatenate([w[:, :1152], w[:, 1158:]], axis=1))
    a["w_fa"] = np.ascontiguousarray(w[:, 1152:1158].reshape(8, P, W2).transpose(1, 0, 2)).reshape(P, 8 * W2)
    a["w_o2"], a["w_up2"], a["w_down2"] = tiles(g["w_o_2"][0]), tiles(g["w_up_2"][0]), tiles(g["w_down_2"][0])
    a["w_ada"] = tiles(g["w_ada_3"])
    a["w_in3"], a["w_out3"], a["w_fc1"], a["w_fc2"] = tiles(g["w_in_3"]), tiles(g["w_out_3"]), tiles(g["w_fc1_3"]), tiles(g["w_fc2_3"])
    a["w_sp"] = np.ascontiguousarray(g["w_spatial_3"].transpose(2, 0, 1))
    a["b_sp"] = g["b_spatial_3"]
    a["lnv_g"], a["lnv_b"] = g["ln_v_gain_3"], g["ln_v_bias_3"]
    a["w_pool"] = np.ascontiguousarray(g["w_pool_3"].transpose(1, 0, 2))
    cols = np.zeros((P, NCOL), np.float32)

    def put(name, v):
        s, n = COLS[name]
        cols[:v.shape[0], s:s + n] = v

    put("norm_mix", colv(g["norm_mix_w"][0]))
    put("norm_mlp", colv(g["norm_mlp_w"][0]))
    put("norm_final", colv(g["norm_final_w"]))
    put("b_gate", colv(g["b_gate"][0]))
    put("gla_norm", colv(g["gla_norm_w"][0]))
    put("conv1", g["conv_w"][0].reshape(3, 4, P).transpose(2, 1, 0).reshape(P, 12))
    put("ln1", colv(g["ln1_g_2"][0]))
    put("ln2", colv(g["ln2_g_2"][0]))
    put("g_final", colv(g["g_final_2"]))
    put("fox", colv(g["g_out_fox_2"][0]))
    put("dil", colv(g["g_out_dil_2"][0]))
    put("conv2", g["conv_w_2"][0].reshape(31, 2, P).transpose(2, 1, 0).reshape(P, 62))
    put("conv2_b", colv(g["conv_b_2"][0]))
    put("cn_g", colv(g["cnorm_g_2"][0]))
    put("cn_b", colv(g["cnorm_b_2"][0]))
    put("ffn_w", g["ffn_conv_w_2"][0].reshape(3, 44, P).transpose(2, 1, 0).reshape(P, 132))
    put("ffn_b", colv(g["ffn_conv_b_2"][0]))
    put("b_ada", colv(g["b_ada_3"]))
    put("n1pre", colv(g["norm1_pre_3"]))
    put("n1post", colv(g["norm1_post_3"]))
    put("n2pre", colv(g["norm2_pre_3"]))
    put("n2post", colv(g["norm2_post_3"]))
    put("pscale", colv(g["pool_scale_3"]))
    put("b_pool", g["b_pool_3"].T)
    put("b_forget", g["b_forget_2"][0][:, None])
    put("c", colv(g["c_3"][0]))
    rc = np.zeros((4, 16), np.float32)
    for i, w_ in enumerate((2, 4, 8, 16)):
        rc[i] = 1.0 / np.minimum(np.arange(16) + 1.0, w_)
    put("rcnt", np.broadcast_to(rc.reshape(1, 64), (P, 64)))
    a["cols"] = cols
    a["ident"] = np.eye(P, dtype=np.float32)
    j, i = np.meshgrid(np.arange(P), np.arange(P), indexing="ij")
    m = [(j // (2 * h) == i // (2 * h)) & (j % (2 * h) < h) & (i % (2 * h) >= h) for h in LEVELS] + [j == i]
    a["masks"] = np.ascontiguousarray(np.stack(m, 1).astype(np.float32)).reshape(P, 1024)
    q, k = j, i
    ok = [k >= q, k <= q, (k % 2 == q % 2) & (k <= q)]
    a["negm"] = np.ascontiguousarray(np.stack([np.where(o, 0.0, NEG) for o in ok], 1).astype(np.float32)).reshape(P, 384)
    sl = np.zeros((6, 6, P), np.float32)
    for h in range(6):
        sl[h, h] = 1.0
    a["sel"] = sl
    a["tri"] = (i >= j).astype(np.float32)
    return a


def plan_block2(plan, plan_mlp, d, upto):
    w = d["w_in2"]
    for n, m in (("gg0", 20), ("gv0", 18), ("gg1", 21), ("gv1", 19)):
        plan(n, w[m])
    plan("fa", d["w_fa"])
    for n, m in (("vb", 15), ("qb", 9), ("kb", 12), ("va", 6), ("qa", 0), ("ka", 3)):
        for j in range(3):
            plan(f"{n}{j}", w[m + j])
    for m in range(8):
        plan(f"w2o{m}", d["w_o2"][m])
    plan_mlp("w_up2", "w_down2", "fup", "fdn", 6, 8, sizes=[4] * 5 + [2], pairs=True)


def plan_block3(plan, plan_mlp, d):
    for n, m in (("zv", 4), ("zu", 0), ("zb", 8)):
        for j in range(4):
            plan(f"{n}{j}", d["w_in3"][m + j])
    for m in range(8):
        plan(f"wo3{m}", d["w_out3"][m])
    plan_mlp("w_fc1", "w_fc2", "fa1_", "fa2_", 8, 8)


def kernel(**inputs):
    import concourse.bacc as _bacc
    from concourse.bass_utils import run_bass_kernel_spmd as _run

    nc = _bacc.Bacc("TRN2", target_bir_lowering=False, num_devices=1)
    arrays = layout(inputs)
    d = {n: nc.dram_tensor("in_" + n, a.shape, mybir.dt.from_np(a.dtype), kind="ExternalInput").ap()
         for n, a in arrays.items()}
    out = nc.dram_tensor("out_0", (P, 8, S), F, kind="ExternalOutput").ap()
    build(nc, d, out)
    r = _run(nc, [{"in_" + n: a for n, a in arrays.items()}], core_ids=[0])
    o = r.results[0]["out_0"]
    return np.ascontiguousarray(o.transpose(2, 1, 0)).reshape(1, S, 1024)
```

```python
from contextlib import ExitStack

import numpy as np

import concourse.bass as bass
from concourse import mybir

F = mybir.dt.float32
R = mybir.dt.float32r
BF = mybir.dt.bfloat16
U8 = mybir.dt.uint8
ALU = mybir.AluOpType
ACT = mybir.ActivationFunctionType
AX = mybir.AxisListType
MUL, ADD, SUB, MAX, MIN = ALU.mult, ALU.add, ALU.subtract, ALU.max, ALU.min

P = 128
S = 1024
NMETA = 16
EPS = 1e-6
FF2 = 2816
NPAIR = FF2 // 128
ADA_AT = sorted([0, 1, 2] + [n for n in range(4, 88) if (n - 4) % 12 in (0, 1, 2, 5, 7, 9)] + [15, 27, 39])
LEVELS = (64, 32, 16, 8, 4, 2, 1)
NEG = -1e30
W2 = 6

COLS = {}


def _columns():
    at = 0
    for name, n in (("norm_mix", 8), ("norm_mlp", 8), ("norm_final", 8), ("b_gate", 2), ("gla_norm", 1),
                    ("conv1", 12), ("ln1", 8), ("ln2", 8), ("g_final", 8), ("fox", 3), ("dil", 3),
                    ("conv2", 62), ("conv2_b", 2), ("cn_g", 2), ("cn_b", 2), ("ffn_w", 132), ("ffn_b", 44),
                    ("b_ada", 48), ("n1pre", 8), ("n1post", 8), ("n2pre", 8), ("n2post", 8),
                    ("pscale", 4), ("b_pool", 4), ("b_forget", 1), ("c", 8), ("rcnt", 64)):
        COLS[name] = (at, n)
        at += n
    return at


NCOL = _columns()


class Engine:

    def __init__(self, name, sem):
        self.name, self.sem, self.count, self.todo, self.seen = name, sem, 0, [], {}

    def wait(self, *tokens):
        for sem, value in tokens:
            if self.seen.get(sem.name, 0) < value:
                self.seen[sem.name] = value
                self.todo.append(lambda e, s=sem, v=value: e.wait_ge(s, v))

    def go(self, fn, *tokens):
        self.wait(*tokens)
        self.todo.append(fn)

    def op(self, fn, *tokens):
        self.wait(*tokens)
        self.count += 1
        self.todo.append(lambda e: fn(e).then_inc(self.sem, 1))
        return (self.sem, self.count)

    @property
    def last(self):
        return (self.sem, self.count)

    def run(self, e):
        for fn in self.todo:
            fn(e)


class Slot:

    def __init__(self, ap):
        self.ap, self._busy, self.held = ap, [], False

    @property
    def busy(self):
        return self._busy

    @busy.setter
    def busy(self, tokens):
        self._busy, self.held = tokens, False


class Ring:
    def __init__(self, slots):
        self.slots, self.at = slots, 0

    def take(self):
        for _ in self.slots:
            s = self.slots[self.at % len(self.slots)]
            self.at += 1
            if not s.held:
                s.held = True
                return s
        raise AssertionError("every buffer is held")


def build(nc, d, out, upto=3):
    ctx = ExitStack()
    with ctx:
        def sem(name):
            return ctx.enter_context(nc.semaphore(name))

        pe, act, dve, pool, sp = (Engine(n, sem("s_" + n)) for n in ("pe", "act", "dve", "pool", "sp"))

        class Dsem:
            def __init__(self, name):
                self.sem, self.count = sem("d_" + name), 0

        def dma(q, ds, o, i, *tokens):
            q.wait(*tokens)
            ds.count += 16
            q.todo.append(lambda e: e.dma_start(o, i).then_inc(ds.sem, 16))
            return (ds.sem, ds.count)

        base = -(-nc.sbuf_base // 64) * 64
        XO, HO = base, base + 32768
        GO = HO + 65536
        WO = GO + 65536
        RO = WO + 24576
        TO = RO + 4096
        CO = TO + 12288
        names = [0]

        def at(off, shape, dt=F, name=None):
            names[0] += 1
            return nc.alloc_sbuf_tensor_at(name or f"b{names[0]}", list(shape), dt, offset=off)

        catch = [CO]

        def const(shape, dt=F):
            n = int(np.prod(shape[1:])) * {F: 4, R: 4, BF: 2, U8: 1}[dt]
            t = at(catch[0], shape, dt)
            catch[0] += -(-n // 32) * 32
            assert catch[0] <= nc.sbuf_usable_end, catch[0]
            return t

        def unit(region, n, shape, dt=F):
            return at(region + 4096 * n, shape, dt)

        X = at(XO, [P, 8, S])
        HH, HL = at(HO, [P, 8, S], R), at(HO + 32768, [P, 8, S], R)
        HHs, HLs = [HH[:, k, :] for k in range(8)], [HL[:, k, :] for k in range(8)]
        GH, GL = at(GO, [P, 8, S], R), at(GO + 32768, [P, 8, S], R)
        GHs, GLs = [GH[:, k, :] for k in range(8)], [GL[:, k, :] for k in range(8)]
        raw = [at(WO + 4096 * i, [P, 1024]) for i in range(4)]
        wlo = [at(WO + 4096 * i, [P, 1024], R) for i in range(4)]
        whi = [at(WO + 16384 + 4096 * i, [P, 1024], R) for i in range(2)]
        RT = at(RO, [P, S])
        T = [Slot(at(TO + 4096 * i, [P, S])) for i in range(3)]
        tring = Ring(T)

        psl = [Slot(ctx.enter_context(nc.psum_tensor(f"ps{i}", [P, 1024], F))) for i in range(3)]
        pring = Ring(psl)
        misc = Slot(ctx.enter_context(nc.psum_tensor("ps3", [P, 1024], F)))

        ident = const([P, P])
        ones = const([P, P])
        identb = const([P, P], BF)
        rmt = const([P, NMETA])
        rms = const([P, 40])
        gprod = const([P, 16])
        adat = const([P, 2, P])
        cols = const([P, NCOL])
        masks = const([P, 8, P], U8)
        negm = const([P, 3, P], BF)
        st = const([P, 8])
        rr = const([P, 8])
        meta_at = catch[0]
        HM = const([P, 8, 2, NMETA], R)
        HMH, HML = HM[:, :, 0, :], HM[:, :, 1, :]
        mod = const([P, 48])
        SC = const([P, 8])
        gx = const([P, 16])
        epsc = const([P, 1])
        rx = const([P, 8])
        pbias, lz, gains = at(meta_at, [P, 48]), at(meta_at + 192, [P, 16]), at(meta_at + 256, [P, 32])
        onec = const([P, 1])

        def col(name, i=0, n=1):
            a, m = COLS[name]
            return cols[:, a + i:a + i + n]

        dc = Dsem("const")
        for o, i in ((cols[:], "cols"), (ident[:], "ident")):
            tc = dma(sp, dc, o, d[i])
        dve.op(lambda e: e.memset(ones[:], 1.0))
        dve.op(lambda e: e.memset(epsc[:], EPS))
        dve.op(lambda e: e.memset(onec[:], 1.0))
        dve.op(lambda e: e.tensor_copy(identb[:], ident[:]), tc)
        consts = [tc, dve.last]
        for q in (pe, act, dve, pool):
            q.wait(*consts)


        def A(o, i, func, *w, scale=1.0, bias=None, accum=None):
            kw = {"scale": scale}
            if bias is not None:
                kw["bias"] = bias
            if accum is not None:
                kw["accum_out"] = accum
            return act.op(lambda e: e.activation(o, i, func, **kw), *w)

        def TT(o, a, b, op, *w, q=dve):
            return q.op(lambda e: e.tensor_tensor(o, a, b, op), *w)

        def TS(o, a, s1, s2, o1, o2, *w, q=dve):
            if o2 is None:
                return q.op(lambda e: e.tensor_scalar(o, a, s1, None, o1), *w)
            return q.op(lambda e: e.tensor_scalar(o, a, s1, s2, o1, o2), *w)

        def STT(o, a, s, b, o1, o2, *w):
            return dve.op(lambda e: e.scalar_tensor_tensor(out=o, in0=a, scalar=s, in1=b, op0=o1, op1=o2), *w)

        def CP(o, a, *w, q=dve):
            return q.op(lambda e: e.tensor_copy(o, a), *w)

        def split(src, hi, lo, *w, q=pool):
            t = A(hi, src, ACT.Copy, *w)
            return TT(lo, src, hi.bitcast(F), SUB, t, *w, q=q)


        wl = []

        def plan(name, ap, split=True):
            wl.append((name, ap, split))

        class Stream:
            def __init__(self):
                self.cur = self.dma = self.spl = 0
                self.ds = [Dsem(f"w{i}") for i in range(4)]
                self.landed, self.free, self.ready, self.slot = {}, {}, {}, {}
                self.nspl = 0
                self.used = {}

            def pump(self, i):
                while True:
                    moved = False
                    if self.dma < len(wl) and self.dma <= i + 4 and (self.dma < 4 or self.dma - 4 in self.free):
                        j = self.dma
                        ap = wl[j][1]
                        n = int(np.prod(ap.shape[1:]))
                        w = [self.free[j - 4]] if j >= 4 else []
                        dst = raw[j % 4][:, 0:n]
                        if len(ap.shape) == 3:
                            dst = dst.rearrange("p (k m) -> p k m", k=ap.shape[1])
                        self.landed[j] = dma(sp, self.ds[j % 4], dst, ap, *w)
                        self.dma += 1
                        moved = True
                    if self.spl < len(wl) and self.spl <= i + 1 and self.spl in self.landed:
                        j = self.spl
                        if wl[j][2]:
                            s = self.nspl % 2
                            if self.nspl < 2 or (self.nspl - 2) in self.used:
                                n = int(np.prod(wl[j][1].shape[1:]))
                                w = [self.used[self.nspl - 2]] if self.nspl >= 2 else []
                                t = split(raw[j % 4][:, 0:n], whi[s][:, 0:n], wlo[j % 4][:, 0:n], self.landed[j], *w)
                                self.ready[j] = t
                                self.slot[j] = (s, self.nspl)
                                self.nspl += 1
                                self.spl += 1
                                moved = True
                        else:
                            self.spl += 1
                            moved = True
                    if not moved:
                        return

            def take(self, name):
                i = self.cur
                assert wl[i][0] == name, (wl[i][0], name)
                self.cur += 1
                self.pump(i)
                return i

            def done(self, i, tok):
                self.free[i] = tok
                if wl[i][2]:
                    self.used[self.slot[i][1]] = tok

        ws = Stream()

        class Rhs:

            def __init__(self, hi, lo, toks, order=None):
                self.hi, self.lo, self.toks, self.order = hi, lo, toks, order

        def job(name, rhs, nk, k0=0, m=P, meta=False, into=None):
            i = ws.take(name)
            s, _ = ws.slot[i]
            hi = whi[s][:, 0:nk * m].rearrange("p (k m) -> p k m", k=nk)
            lo = wlo[i % 4][:, 0:nk * m].rearrange("p (k m) -> p k m", k=nk)
            sl = pring.take()
            pe.wait(ws.ready[i], *sl.busy)
            if meta:
                pe.wait(*misc.busy)
            order = rhs.order or list(range(nk))
            for k in order:
                pe.wait(rhs.toks[k0 + k])
                first, last = k == order[0], k == order[-1]
                for hf in range(2):
                    cs = slice(512 * hf, 512 * hf + 512)
                    o = sl.ap[0:m, cs]
                    pe.go(lambda e, o=o, k=k, cs=cs, first=first: e.matmul(o, hi[:, k, :], rhs.hi[k0 + k][:, cs], start=first, stop=False))
                    pe.go(lambda e, o=o, k=k, cs=cs: e.matmul(o, hi[:, k, :], rhs.lo[k0 + k][:, cs], start=False, stop=False))
                if meta:
                    o = misc.ap[0:m, 0:2 * NMETA]
                    pe.go(lambda e, o=o, k=k, first=first: e.matmul(o, hi[:, k, :], HM[:, k].rearrange("p a b -> p (a b)"), start=first, stop=False))
                    o = misc.ap[0:m, 0:NMETA]
                    pe.go(lambda e, o=o, k=k, last=last: e.matmul(o, lo[:, k, :], HM[:, k, 0, :], start=False, stop=last))
                for hf in range(2):
                    cs = slice(512 * hf, 512 * hf + 512)
                    o = sl.ap[0:m, cs]
                    f = lambda e, o=o, k=k, cs=cs, last=last: e.matmul(o, lo[:, k, :], rhs.hi[k0 + k][:, cs], start=False, stop=last)
                    if last and hf == 1:
                        tok = pe.op(f)
                    else:
                        pe.go(f)
            ws.done(i, tok)
            ws.pump(i + 1)
            return sl, tok

        stt = {}
        turns_due = []

        def turned(b, t, dst, *w):
            def later():
                sl = pring.take()
                pe.wait(t, *sl.busy)
                for c in range(8):
                    f = lambda e, c=c: e.transpose(sl.ap[:, P * c:P * c + P], b.ap[:, P * c:P * c + P], ident[:])
                    t2 = pe.op(f) if c == 7 else pe.go(f)
                b.busy = [t2]
                t2 = A(dst, v3(sl.ap[:], 8), ACT.Copy, t2, *w)
                sl.busy = [t2]
                return t2
            turns_due.append(later)

        def turn_now():
            t = None
            while turns_due:
                t = turns_due.pop(0)()
            return t

        def v3(ap, n):
            return ap.rearrange("p (a b) -> p a b", a=n)

        class Norm:

            def __init__(self, width, g=None):
                self.D, self.g, self.k = width, g, 0
                self.acc, self.acc2 = T[2], T[1]
                self.prev = self.prev2 = None
                stt.setdefault("rtfree", [])

            def feed(self, x, *tok, q=dve):
                k = self.k
                if k == 0:
                    self.prev = A(self.acc.ap[:], x, ACT.Square, *tok, *self.acc.busy)
                    if self.g is not None:
                        self.prev2 = A(self.acc2.ap[:], x, ACT.Square, *tok, *self.acc2.busy, scale=self.g(0))
                else:
                    b = T[(k - 1) % 2] if self.g is None else T[0]
                    t = A(b.ap[:], x, ACT.Square, *tok, *b.busy)
                    self.prev = TT(self.acc.ap[:], self.acc.ap[:], b.ap[:], ADD, t, self.prev, q=q)
                    b.busy = [self.prev]
                    if self.g is not None:
                        t = A(RT[:], x, ACT.Square, *tok, *stt["rtfree"], scale=self.g(k))
                        self.prev2 = TT(self.acc2.ap[:], self.acc2.ap[:], RT[:], ADD, t, self.prev2, q=pool)
                        stt["rtfree"] = [self.prev2]
                self.k += 1

            def stats(self):
                pe.wait(self.prev, *misc.busy)
                for b in range(8):
                    t = pe.op(lambda e, b=b: e.matmul(misc.ap[:, 512 + b:513 + b], self.acc.ap[:, P * b:P * b + P], ones[:, 0:1], start=(b == 0), stop=True, skip_group_check=True))
                self.acc.busy = [t]
                s1, r1, s2, r2, r12 = (rms[:, 8 * i:8 * i + 8] for i in range(5))
                if self.g is not None:
                    pe.wait(self.prev2)
                    for b in range(8):
                        t = pe.op(lambda e, b=b: e.matmul(misc.ap[:, 520 + b:521 + b], self.acc2.ap[:, P * b:P * b + P], ones[:, 0:1], start=False, stop=True, skip_group_check=True))
                    self.acc2.busy = [t]
                t = A(s1, misc.ap[:, 512:520], ACT.Sqrt, t, scale=1.0 / self.D, bias=epsc[:])
                self.t = dve.op(lambda e: e.reciprocal(r1, s1), t)
                self.r1 = self.r = r1
                if self.g is not None:
                    t = TT(s2, r1, r1, MUL, self.t)
                    t = TT(s2, s2, misc.ap[:, 520:528], MUL, t)
                    t2 = A(s2, s2, ACT.Sqrt, t, scale=1.0 / self.D, bias=epsc[:])
                    t2 = dve.op(lambda e: e.reciprocal(r2, s2), t2)
                    self.t = TT(r12, r1, r2, MUL, t2)
                    self.r = r12
                misc.busy = misc.busy + [t]
                self.dg = T[0]
                self.tdg = TT(v3(self.dg.ap[:], 8), ident[:].unsqueeze(1).broadcast_to([P, 8, P]),
                              self.r.unsqueeze(2).broadcast_to([P, 8, P]), MUL, self.t, *self.dg.busy)

            def spread(self):
                sl = pring.take()
                pe.wait(self.tdg, *sl.busy)
                for hf in range(2):
                    t = pe.op(lambda e, hf=hf: e.matmul(sl.ap[:, 512 * hf:512 * hf + 512], ones[:], self.dg.ap[:, 512 * hf:512 * hf + 512], start=True, stop=True))
                self.dg.busy = [t]
                return sl, t

            def to_rt(self):
                sl, t = self.spread()
                t = A(RT[:], sl.ap[:], ACT.Copy, t, *stt.get("rtfree", []))
                sl.busy = [t]
                self.rt = t
                return t

            def first(self, dg):
                t = TT(v3(dg.ap[:], 8), ident[:].unsqueeze(1).broadcast_to([P, 8, P]),
                       self.r1.unsqueeze(2).broadcast_to([P, 8, P]), MUL, *dg.busy)
                sl = pring.take()
                pe.wait(t, *sl.busy)
                for hf in range(2):
                    t = pe.op(lambda e, hf=hf: e.matmul(sl.ap[:, 512 * hf:512 * hf + 512], ones[:], dg.ap[:, 512 * hf:512 * hf + 512], start=True, stop=True))
                dg.busy = [t]
                return sl, t

        def weigh(k, x, g, hi, lo, *w):
            t = A(hi[:, k, :], x, ACT.Copy, *w, scale=g)
            return STT(lo[:, k, :], x, g, hi[:, k, :].bitcast(F), MUL, SUB, t, *w)

        def relu_up(name, h, rt, bias=None):
            def up_job(j, mid):
                return job(f"{name}{j}", h, 8)

            def up_drain(j, got):
                sl, tok = got
                b = tring.take()
                if bias:
                    t = TT(b.ap[:], sl.ap[:], RT[:], MUL, tok, rt.rt, *b.busy)
                    sl.busy = [t]
                    t = A(b.ap[:], b.ap[:], ACT.Relu, t, bias=bias(j))
                else:
                    t = STT(b.ap[:], sl.ap[:], 0.0, RT[:], MAX, MUL, tok, rt.rt, *b.busy)
                    sl.busy = [t]
                return b, TT(b.ap[:], b.ap[:], b.ap[:], MUL, t)
            return up_job, up_drain

        hidden = {"free": [[], []], "toks": [None] * 8}

        def mlp(name_down, up_job, up_drain, ngroups, acc, acc_toks, first_copy=False, sizes=None, norm=None, on_last=None, step=None):
            sizes = sizes or [4] * ngroups
            first = [sum(sizes[:g]) for g in range(ngroups)]
            gh = Rhs(GHs, GLs, hidden["toks"])
            jobs = [0]

            def stepped(got, pair=False):
                if step and not pair:
                    step(jobs[0])
                    jobs[0] += 1
                return got

            def drain(g, j, got):
                slot = 4 * (g % 2) + j
                b, t = up_drain(first[g] + j, got)
                t = split(b.ap[:], GH[:, slot, :], GL[:, slot, :], t, *hidden["free"][g % 2])
                b.busy = [t]
                hidden["toks"][slot] = t

            def ups(g):
                j0 = 0
                if g == 0 and norm is not None:
                    if name_down == "fdn":
                        got = up_job(0, norm.stats)
                        norm.to_rt()
                        drain(0, 0, got)
                        j0 = 1
                    else:
                        got = stepped(up_job(0, None))
                        norm.stats()
                        got1 = stepped(up_job(1, None))
                        norm.to_rt()
                        drain(0, 0, got)
                        drain(0, 1, got1)
                        j0 = 2
                for j in range(j0, sizes[g]):
                    drain(g, j, stepped(up_job(first[g] + j, None), name_down == "fdn"))

            ups(0)
            for g in range(ngroups):
                if g + 1 < ngroups:
                    ups(g + 1)
                    if g + 1 == ngroups - 1:
                        stt["ups"] = pe.last
                        stt["rtfree"] = [dve.last]
                for m in range(8):
                    sl, tok = stepped(job(f"{name_down}{g}_{m}", gh, sizes[g], k0=4 * (g % 2)))
                    if g == 0 and first_copy:
                        t = A(acc[:, m, :], sl.ap[:], ACT.Copy, tok, *acc_toks[m])
                    else:
                        t = TT(acc[:, m, :], sl.ap[:], acc[:, m, :], ADD, tok, *acc_toks[m])
                    acc_toks[m] = [t]
                    sl.busy = [t]
                    if g == ngroups - 1 and on_last and m:
                        on_last(m - 1, acc_toks[m - 1][0])
                hidden["free"][g % 2] = [pe.last]
            on_last(7, acc_toks[7][0])
            return [a[0] for a in acc_toks]

        def plan_mlp(up, dn, name_up, name_down, ng, nk, sizes=None, pairs=False, aux=()):
            sizes = sizes or [4] * ng
            first = [sum(sizes[:g]) for g in range(ng)]
            done = [0]

            def extra():
                n, done[0] = done[0], done[0] + 1
                if aux and n in ADA_AT:
                    plan(*aux[ADA_AT.index(n)], split=False)

            def ups(g):
                for j in range(sizes[g]):
                    m = first[g] + j
                    if pairs:
                        plan(f"{name_up}a{m}", d[up][m])
                        extra()
                        plan(f"{name_up}b{m}", d[up][NPAIR + m])
                        extra()
                    else:
                        plan(f"{name_up}{m}", d[up][m])
                        extra()
            ups(0)
            for g in range(ng):
                if g + 1 < ng:
                    ups(g + 1)
                for m in range(8):
                    plan(f"{name_down}{g}_{m}", d[dn][m, :, first[g] * P:(first[g] + sizes[g]) * P])
                    extra()

        plan("gr", d["w_gr"])
        for n, m0 in (("k0", 2), ("k1", 3), ("q0", 0), ("q1", 1), ("v0", 4), ("v1", 5), ("v2", 6), ("v3", 7),
                      ("g0", 8), ("g1", 9), ("g2", 10), ("g3", 11)):
            plan(n, d["w_in"][m0])
        for m in range(4):
            plan(f"cc{m}", d["w_in"][16 + m])
            plan(f"cx{m}", d["w_in"][20 + m])
            plan(f"cb{m}", d["w_in"][12 + m])
        for m in range(8):
            plan(f"wo{m}", d["w_out"][m])
        plan_mlp("w_up", "w_down", "up", "dn", 8, 8, aux=[(f"ada{m}", d["w_ada"][m]) for m in range(48)] if upto >= 3 else [])
        if upto >= 2:
            plan_block2(plan, plan_mlp, d, upto)
        if upto >= 3:
            plan_block3(plan, plan_mlp, d)

        ysc = nc.dram_tensor("ysc", (P, 8, S), F, kind="Internal").ap()
        sgsc = nc.dram_tensor("sgsc", (P, 4, S), F, kind="Internal").ap()
        xsc = nc.dram_tensor("xsc", (P, 8, S), F, kind="Internal").ap()

        dx = [Dsem(f"x{k}") for k in range(8)]
        dm = Dsem("meta")
        XM = unit(GO, 0, [P, 8, NMETA])
        SQM = at(GO + 1024, [P, 8, NMETA])
        DGM = at(GO + 2048, [NMETA, NMETA])
        TM = at(GO + 4096, [P, 8, NMETA])
        tm = dma(sp, dm, XM[:], d["metaT"])
        ws.pump(-3)
        xt = [dma(sp, dx[k], X[:, k, :], d["xT"][:, k, :]) for k in range(8)]
        dmk = Dsem("mask")
        mf = unit(GO, 2, [P, S])
        nf_ = unit(GO, 3, [P, 384])
        dma(sp, dmk, mf[:], d["masks"])
        tmk = dma(sp, dmk, nf_[:], d["negm"])
        ws.pump(-1)

        TT(gprod[:, 0:8], col("norm_final", 0, 8), col("ln1", 0, 8), MUL)
        for k in range(8):
            tw = TS(TM[:, k, :], XM[:, k, :], col("norm_mix", k), None, MUL, None, tm)
        tmeta = split(TM[:], HMH, HML, tw)
        t = A(SQM[:], XM[:], ACT.Square, tm)
        pe.wait(t)
        for k in range(8):
            f = lambda e, k=k: e.matmul(misc.ap[0:NMETA, 0:1], SQM[:, k, :], ones[:, 0:1], start=(k == 0), stop=(k == 7))
            t = pe.op(f) if k == 7 else pe.go(f)
        t = A(st[0:NMETA, 0:1], misc.ap[0:NMETA, 0:1], ACT.Sqrt, t, scale=1.0 / 1024, bias=epsc[0:NMETA, :])
        t = dve.op(lambda e: e.reciprocal(rr[0:NMETA, 0:1], st[0:NMETA, 0:1]), t)
        t = TS(DGM[:], ident[0:NMETA, 0:NMETA], rr[0:NMETA, 0:1], None, MUL, None, t)
        t = pe.op(lambda e: e.matmul(misc.ap[:, 0:NMETA], ones[0:NMETA, :], DGM[:], start=True, stop=True), t)
        trm = CP(rmt[:], misc.ap[:, 0:NMETA], t)
        misc.busy = [trm]

        xs = [X[:, k, :] for k in range(8)]
        norm = Norm(1024)
        toks = []
        for k in range(8):
            toks.append(weigh(k, xs[k], col("norm_mix", k), HH, HL, xt[k]))
            norm.feed(xs[k], xt[k], q=(pool, dve)[k % 2])
        h = Rhs(HHs, HLs, toks)
        CP(masks[:].rearrange("p a b -> p (a b)"), mf[:], tmk)
        CP(negm[:].rearrange("p a b -> p (a b)"), nf_[:])
        pe.wait(tmeta)
        xfree = [dve.last, act.last]
        gfree = [tmeta, dve.last]

        def G(n, shape, dt=F):
            return unit(GO, n, shape, dt)

        Q, K, B, V, D, AT = (G(0, [P, 2, S]), G(2, [P, 2, S]), G(4, [P, 2, S]), G(6, [P, 8, 512]), G(10, [P, 2, S]),
                             G(12, [P, 4, S]))
        XL = [Slot(unit(XO, 0, [P, 2, S])), Slot(unit(XO, 2, [P, 2, S]))]
        QI = unit(XO, 4, [P, 2, S])
        U = unit(XO, 6, [P, 1026])
        mo = XO + 7 * 4096 + 64
        KM, BM, VM, KDM, EM = (at(mo, [P, 2, NMETA]), at(mo + 128, [P, 2, NMETA]), at(mo + 256, [NMETA, 512]),
                               at(mo + 2304, [NMETA, 256]), at(mo + 3328, [P, 2, NMETA]))
        EV = at(mo + 3584, [P, NMETA])
        KDT, SA = unit(XO, 0, [P, 8, 256]), unit(XO, 2, [P, 8, 256])

        def meta_out(dst, c0, n, *w, m=P):
            t = A(dst, misc.ap[0:m, c0:c0 + n], ACT.Copy, *w)
            t = TT(dst, misc.ap[0:m, NMETA + c0:NMETA + c0 + n], dst, ADD, t)
            misc.busy = [t]
            return TT(dst, dst, rmt[0:m, c0:c0 + n], MUL, t)

        sl, tok = job("gr", h, 8, m=16, meta=True)
        norm.stats()
        grm = at(mo + 3456, [16, NMETA])
        t2 = meta_out(grm[:], 0, NMETA, tok, *xfree, m=16)
        tk, tq = [], []
        slk, tokk = job("k0", h, 8, meta=True)
        norm.to_rt()
        gr = T[0]
        t1 = TT(gr.ap[0:16, :], sl.ap[0:16, :], RT[0:16, :], MUL, tok, norm.rt, *gr.busy)
        sl.busy = [t1]

        def k_out(m, sl, tok):
            tk.append(meta_out(KM[:, m, :], 0, NMETA, tok, *xfree))
            t = TT(K[:, m, :], sl.ap[:], RT[:], MUL, tok, *gfree)
            sl.busy = [t]
            tk.append(t)

        k_out(0, slk, tokk)
        wg = T[2]
        dg = Dsem("wg")
        tw = dma(sp, dg, wg.ap[0:16, 0:256], d["w_gate_up"], *wg.busy)

        def logsig(zs, bias, o_abs, o_min, o_g, *w):
            t = A(o_abs, zs, ACT.Abs, *w, bias=bias)
            tmn = TS(o_min, zs, bias, 0.0, ADD, MIN, t, *w)
            t2 = A(o_abs, o_abs, ACT.Exp, t, scale=-1.0)
            t2 = A(o_abs, o_abs, ACT.Ln, t2, bias=onec[0:o_abs.shape[0], :])
            return TT(o_g, o_min, o_abs, SUB, t2, tmn), t, tmn

        sl, tok = job("k1", h, 8, meta=True)
        k_out(1, sl, tok)
        zt = []
        for m in range(2):
            sz = pring.take()
            pe.wait(t1, tw, *sz.busy)
            for hf in range(2):
                f = lambda e, hf=hf, m=m, sz=sz: e.matmul(sz.ap[:, 512 * hf:512 * hf + 512], wg.ap[0:16, P * m:P * m + P], gr.ap[0:16, 512 * hf:512 * hf + 512], start=True, stop=True)
                t = pe.op(f)
            g_, ta, tb = logsig(sz.ap[:], col("b_gate", m), D[:, m, :], B[:, m, :], D[:, m, :], t, *gfree)
            sz.busy = [ta, tb]
            zt.append(g_)
        gr.busy = [pe.last]
        pe.wait(t2, *misc.busy)
        for m in range(2):
            t = pe.op(lambda e, m=m: e.matmul(misc.ap[:, 32 * m:32 * m + NMETA], wg.ap[0:16, P * m:P * m + P], grm[:], start=True, stop=True))
        wg.busy = [t]
        zm = []
        for m in range(2):
            g_, ta, tb = logsig(misc.ap[:, 32 * m:32 * m + NMETA], col("b_gate", m), EM[:, m, :], BM[:, m, :], EM[:, m, :], t, *xfree, *zm)
            zm.append(g_)
        misc.busy = [ta, tb]
        keep = T[2]
        ta = pool.op(lambda e: e.memset(keep.ap[:], 1.0), *keep.busy)
        ta = pool.op(lambda e: e.memset(v3(keep.ap[:], 8)[:, :, 0:1], 0.0), ta)
        tb = []
        for m in range(2):
            tb.append(dve.op(lambda e, m=m: e.tensor_tensor_scan(B[:, m, :], keep.ap[:], D[:, m, :], 0.0, MUL, ADD), ta, zt[m]))
            tbm = dve.op(lambda e, m=m: e.tensor_tensor_scan(BM[:, m, :], keep.ap[:, 1:1 + NMETA], EM[:, m, :], 0.0, MUL, ADD), ta, zm[m])
        keep.busy = [tbm]
        tb.append(tbm)

        for m in range(2):
            sl, tok = job(f"q{m}", h, 8)
            t = STT(Q[:, m, :], sl.ap[:], 0.125, RT[:], MUL, MUL, tok, *gfree)
            sl.busy = [t]
            tq.append(t)

        fill = []
        tz = pool.op(lambda e: e.memset(AT[:], 0.0), *gfree)

        def level(li):
            hsz = LEVELS[li]
            nb = S // (2 * hsz)
            bv = B[:].rearrange("p t (n w) -> p (t n) w", w=2 * hsz)
            dv = D[:].rearrange("p t (n w) -> p (t n) w", w=2 * hsz)
            ref = bv[:, :, hsz - 1:hsz].broadcast_to([P, 2 * nb, 2 * hsz])
            t = TT(dv, bv, ref, SUB, *tb, *stt.get("dfree", []))
            t = A(D[:], D[:], ACT.Abs, t)
            t = A(D[:], D[:], ACT.Exp, t, scale=-1.0 / 16)
            x = XL[li % 2]
            xv = x.ap[:].rearrange("p t (n w) -> p (t n) w", w=2 * hsz)
            qv = Q[:].rearrange("p t (n w) -> p (t n) w", w=2 * hsz)
            kv = K[:].rearrange("p t (n w) -> p (t n) w", w=2 * hsz)
            TT(xv[:, :, hsz:], dv[:, :, hsz:], qv[:, :, hsz:], MUL, t, *tq, *x.busy, *xfree)
            t = TT(xv[:, :, :hsz], dv[:, :, :hsz], kv[:, :, :hsz], MUL, *tk)
            stt["dfree"] = [t]
            stt[f"x{li}"] = (x, t)

        def level_head(li, hd):
            t_, hh = hd // 2, hd % 2
            sl = pring.take()
            pe.wait(*sl.busy)
            if li == 7:
                a, b = K, Q
                pe.wait(*tq, *tk)
            else:
                x, tx = stt[f"x{li}"]
                a = b = x.ap
                pe.wait(tx)
            for c in range(8):
                cs = slice(P * c, P * c + P)
                f = lambda e, c=c, cs=cs, a=a, b=b: e.matmul(sl.ap[:, cs], a[64 * hh:64 * hh + 64, t_, cs], b[64 * hh:64 * hh + 64, t_, cs], start=True, stop=True)
                t = pe.op(f) if c == 7 else pe.go(f)
            if li < 7:
                x.busy = [t]
            t = dve.op(lambda e: e.copy_predicated(v3(AT[:, hd, :], 8), masks[:, li, :].unsqueeze(1).broadcast_to([P, 8, P]), v3(sl.ap[:], 8)), t, tz)
            sl.busy = [t]
            stt["at"] = t

        level(0)
        for li in range(8):
            for hd in range(4):
                fill.append(lambda li=li, hd=hd: level_head(li, hd))
                if hd == 0 and li < 6:
                    fill.append(lambda li=li: level(li + 1))
                if hd == 1 and li == 6:
                    fill.append(lambda: decays())
                if hd == 3 and li == 6:
                    fill.append(lambda: stt.update(xl=[pe.last]))

        bl = B[:].rearrange("p t (n w) -> p (t n) w", w=P)[:, :, P - 1:P]

        def decays():
            dv = D[:].rearrange("p t (n w) -> p (t n) w", w=P)
            bv = B[:].rearrange("p t (n w) -> p (t n) w", w=P)
            t = A(gx[:].unsqueeze(2), bl, ACT.Exp, *tb, scale=1.0 / 16)
            stt["dec"] = t
            t = A(QI[:], B[:], ACT.Exp, *tb, *xfree, scale=1.0 / 16)
            stt["qi"] = TT(QI[:], QI[:], Q[:], MUL, t, *tq)
            t = TT(dv, bv, bl.broadcast_to([P, 16, P]), SUB, *stt["dfree"])
            t = A(D[:], D[:], ACT.Exp, t, scale=-1.0 / 16)
            stt["kd"] = TT(D[:], D[:], K[:], MUL, t)
            t = TT(EM[:], BM[:], BM[:, :, NMETA - 1:NMETA].broadcast_to([P, 2, NMETA]), SUB, tb[-1])
            t = A(EM[:], EM[:], ACT.Exp, t, scale=-1.0 / 16)
            stt["kdm"] = TT(EM[:], EM[:], KM[:], MUL, t, *tk)

        def kd_turn(m):
            sl = pring.take()
            pe.wait(stt["kd"], *sl.busy)
            for c in range(8):
                f = lambda e, c=c: e.transpose(sl.ap[:, P * c:P * c + P], D[:, m, P * c:P * c + P], ident[:])
                t = pe.op(f) if c == 7 else pe.go(f)
            t = A(KDT[:, :, P * m:P * m + P], v3(sl.ap[:], 8), ACT.Copy, t, *stt["xl"])
            sl.busy = [t]
            stt[f"kdt{m}"] = t

        def meta_turn():
            sl = pring.take()
            pe.wait(stt["kdm"], *sl.busy)
            for m in range(2):
                t = pe.op(lambda e, m=m: e.transpose(sl.ap[0:NMETA, P * m:P * m + P], EM[:, m, :], ident[:]))
            stt["kdmt"] = CP(KDM[:], sl.ap[0:NMETA, 0:256], t)
            sl.busy = [stt["kdmt"]]

        def kv_mm(c, lhs, rhs, *w):
            sl = pring.take()
            pe.wait(*w, *sl.busy)
            for hd in range(4):
                t_, hh = hd // 2, hd % 2
                f = lambda e, hd=hd, t_=t_, hh=hh: e.matmul(sl.ap[64 * hh:64 * hh + 64, P * t_:P * t_ + P], lhs(hd), rhs(hd), start=True, stop=True)
                t = pe.op(f) if hd == 3 else pe.go(f)
            if c == 0:
                t = CP(SA[:, 0, :], sl.ap[:, 0:256], t, *stt["xl"])
            else:
                for m in range(2):
                    tt = STT(SA[:, c, P * m:P * m + P], SA[:, c - 1, P * m:P * m + P], gx[:, 8 * m + c - 1:8 * m + c],
                             sl.ap[:, P * m:P * m + P], MUL, ADD, t, stt["dec"], stt["s"])
                t = tt
            sl.busy = [t]
            stt["s"] = t

        fill.append(meta_turn)
        fill.append(lambda: kd_turn(0))
        fill.append(lambda: kd_turn(1))
        fill.append(lambda: kv_mm(0, lambda h: KDM[0:NMETA, 64 * h:64 * h + 64], lambda h: VM[0:NMETA, P * h:P * h + P], stt["kdmt"], stt["vm"]))
        for c in range(1, 8):
            fill.append(lambda c=c: kv_mm(c, lambda h: KDT[:, c - 1, 64 * h:64 * h + 64],
                                          lambda h: V[:, c - 1, P * h:P * h + P], stt["kdt0"], stt["kdt1"], stt["v"]))

        def fills(n):
            for _ in range(n):
                if fill:
                    fill.pop(0)()

        vmfree = []
        for m in range(4):
            sl, tok = job(f"v{m}", h, 8, meta=True)
            tt_ = turn_now()
            if tt_:
                stt["v"] = tt_
            tev = meta_out(EV[:], 0, NMETA, tok, *stt.get("evfree", xfree))
            b = tring.take()
            t = TT(b.ap[:], sl.ap[:], RT[:], MUL, tok, *b.busy)
            sl.busy = [t]
            turned(b, t, V[:, :, P * m:P * m + P], *gfree)
            fills(3)
            te = pe.op(lambda e: e.transpose(misc.ap[0:NMETA, 512:512 + P], EV[:], ident[:]), tev, *vmfree)
            stt["evfree"] = [te]
            stt["vm"] = A(VM[:, P * m:P * m + P], misc.ap[0:NMETA, 512:512 + P], ACT.Copy, te, *xfree)
            vmfree = [stt["vm"]]
        misc.busy = misc.busy + vmfree
        dsg = [Dsem(f"sg{m}") for m in range(4)]
        tsg = []
        for m in range(4):
            sl, tok = job(f"g{m}", h, 8)
            if m == 0:
                stt["v"] = turn_now()
            b = tring.take()
            t = TT(b.ap[:], sl.ap[:], RT[:], MUL, tok, *b.busy)
            sl.busy = [t]
            t = A(b.ap[:], b.ap[:], ACT.Silu, t)
            t = dma(sp, dsg[m], sgsc[:, m, :], b.ap[:], t)
            b.busy = [t]
            tsg.append(t)
            fills(3)
        dyc = [Dsem(f"yc{m}") for m in range(4)]
        tyc = []
        ufree = list(xfree)
        for m in range(4):
            def cw(k, m=m):
                return col("conv1", 3 * m + k)
            sl, tok = job(f"cc{m}", h, 8, meta=True)
            tc2 = meta_out(U[:, 0:2], NMETA - 2, 2, tok, *ufree)
            t = TT(U[:, 2:], sl.ap[:], RT[:], MUL, tok, *ufree)
            sl.busy = [t]
            fills(2)
            sl, tok = job(f"cx{m}", h, 8, meta=True)
            b = tring.take()
            tb1 = TT(b.ap[:], sl.ap[:], RT[:], MUL, tok, *b.busy)
            sl.busy = [tb1]
            t = TT(U[:, 2:], U[:, 2:], b.ap[:], MUL, tb1, t)
            tb1 = meta_out(EV[:, 0:2], NMETA - 2, 2, tok, *stt["evfree"])
            t2 = TT(U[:, 0:2], U[:, 0:2], EV[:, 0:2], MUL, tb1, tc2)
            t3 = A(b.ap[:], U[:, 2:], ACT.Copy, t, *b.busy, scale=cw(2))
            t4 = STT(b.ap[:], U[:, 1:1025], cw(1), b.ap[:], MUL, ADD, t3, t2)
            t5 = STT(b.ap[:], U[:, 0:1024], cw(0), b.ap[:], MUL, ADD, t4)
            ufree = [t5, t3]
            fills(2)
            sl, tok = job(f"cb{m}", h, 8)
            t = TT(b.ap[:], b.ap[:], sl.ap[:], MUL, tok, t5)
            sl.busy = [t]
            t = TT(b.ap[:], b.ap[:], RT[:], MUL, t)
            t = dma(sp, dyc[m], ysc[:, 4 + m, :], b.ap[:], t)
            b.busy = [t]
            tyc.append(t)
            fills(3)
        fills(len(fill))
        stt["rtfree"] = [dve.last]
        hfree = [pe.last]
        SG, Y = unit(HO, 0, [P, 4, S]), unit(HO, 4, [P, 8, S])
        dl = Dsem("sgl")
        tl = dma(sp, dl, SG[:], sgsc, *tsg, *hfree)
        dl2 = [Dsem(f"yl{m}") for m in range(4)]
        tyl = [dma(sp, dl2[m], Y[:, 4 + m, :], ysc[:, 4 + m, :], tyc[m], *hfree) for m in range(4)]
        st4 = Ring([Slot(st[:, 0:4]), Slot(st[:, 4:8])])

        def o_front(c):
            sl = pring.take()
            pe.wait(stt["at"], stt["qi"], stt["v"], stt["s"], *sl.busy)
            cs = slice(P * c, P * c + P)
            for hd in range(4):
                t_, hh = hd // 2, hd % 2
                oc = 512 * hh + P * t_
                pe.go(lambda e, hd=hd, oc=oc: e.matmul(sl.ap[:, oc:oc + P], AT[:, hd, cs], V[:, c, P * hd:P * hd + P], start=True, stop=False))
                f = lambda e, oc=oc, t_=t_, hh=hh: e.matmul(sl.ap[:, oc:oc + P], QI[64 * hh:64 * hh + 64, t_, cs], SA[64 * hh:64 * hh + 64, c, P * t_:P * t_ + P], start=False, stop=True)
                t = pe.op(f) if hd == 3 else pe.go(f)
            b = tring.take()
            s4 = st4.take()
            act.wait(*b.busy, *s4.busy)
            for hd in range(4):
                oc = 512 * (hd // 2) + P * (hd % 2)
                t5 = A(b.ap[:, 512 + P * hd:512 + P * hd + P], sl.ap[:, oc:oc + P], ACT.Square, t, accum=s4.ap[:, hd:hd + 1])
            t5 = A(s4.ap, s4.ap, ACT.Sqrt, t5, scale=1.0 / P, bias=epsc[:])
            t5 = dve.op(lambda e: e.reciprocal(s4.ap, s4.ap), t5)
            t5 = TT(b.ap[:, 0:512].rearrange("p (a b c) -> p a b c", a=2, b=2),
                    sl.ap[:].rearrange("p (a b c) -> p a b c", a=2, b=4)[:, :, 0:2, :],
                    s4.ap.rearrange("p (a b) -> p a b", a=2).unsqueeze(3).broadcast_to([P, 2, 2, P]), MUL, t5, *b.busy)
            sl.busy = [t5]
            s4.busy = [t5]
            return b, t5

        def o_back(c, b, t5):
            cs = slice(P * c, P * c + P)
            s2 = pring.take()
            pe.wait(t5, *s2.busy)
            for hd in range(4):
                at_ = P * (2 * (hd % 2) + hd // 2)
                f = lambda e, hd=hd, at_=at_: e.transpose(s2.ap[:, P * hd:P * hd + P], b.ap[:, at_:at_ + P], ident[:])
                t = pe.op(f) if hd == 3 else pe.go(f)
            b.busy = [t]
            t = STT(Y[:, 0:4, cs], v3(s2.ap[:, 0:512], 4), col("gla_norm"), SG[:, :, cs], MUL, MUL, t, tl)
            s2.busy = [t]
            return t

        def conv_rows(k):
            yh = GHs[k - 4]
            yl = [GHs[4], GHs[5], GLs[2], GLs[3]][k - 4]
            tyc4.append(split(Y[:, k, :], yh, yl, tyl[k - 4], *hfree, dve.last))

        tyc4 = []
        prev = None
        for c in range(8):
            if c in (2, 3, 4, 5):
                conv_rows(c + 2)
            cur = (c, *o_front(c))
            if prev:
                ty = o_back(*prev)
            prev = cur
        ty = o_back(*prev)
        gfree = [pe.last, ty]
        yh, yl = [GHs[k] for k in (4, 5, 6, 7, 0, 1, 2, 3)], [GLs[k] for k in (4, 5, 6, 7, 0, 1, 2, 3)]
        yl[4:8] = [GHs[4], GHs[5], GLs[2], GLs[3]]
        yh[0:4] = [GHs[6], GHs[7], GLs[0], GLs[1]]
        yl[0:4] = [GLs[k] for k in (4, 5, 6, 7)]
        toks = [split(Y[:, k, :], yh[k], yl[k], *gfree, q=(pool, dve)[k % 2]) for k in range(4)] + tyc4
        xfree = [pe.last, dve.last, act.last]
        xt = [dma(sp, dx[k], X[:, k, :], d["xT"][:, k, :], *xfree) for k in range(8)]
        yr = Rhs(yh, yl, toks, order=[4, 5, 6, 7, 0, 1, 2, 3])

        def add_to_x(name, r, toks, on_last, prepare=None):
            res = []
            for m in range(8):
                sl, tok = job(f"{name}{m}", r, 8)
                if prepare:
                    toks[m] = prepare(m, toks[m])
                t = TT(X[:, m, :], sl.ap[:], X[:, m, :], ADD, tok, toks[m])
                sl.busy = [t]
                res.append(t)
                if m:
                    on_last(m - 1, res[m - 1])
            on_last(7, t)
            return res

        def feeder(norm, g, toks, *w):
            def on_last(m, t):
                if g is not None:
                    toks.append(weigh(m, X[:, m, :], g(m), HH, HL, t, *w))
                norm.feed(X[:, m, :], t)
            return on_last

        tsc = A(SC[:], col("c", 0, 8), ACT.Silu)

        ada = Ring([Slot(adat[:, 0, :]), Slot(adat[:, 1, :])])
        due = []

        def row_tile(name, f, vec, c0, *tv, on_pool=False):
            i = ws.take(name)
            w_ = raw[i % 4][:].rearrange("p (k m) -> p k m", k=8)
            t = TT(w_, w_, vec.unsqueeze(2).broadcast_to([P, 8, P]), MUL, ws.landed[i], *tv, q=pool)

            def reduce():
                a_ = ada.take()
                t2 = dve.op(lambda e: e.tensor_reduce(a_.ap, raw[i % 4][:].rearrange("p (k m) -> p m k", k=8), AX.X, ADD), t, *a_.busy)
                ws.done(i, t2)

                def last():
                    stt["row"] = pe.op(lambda e: e.matmul(misc.ap[:, c0 + f:c0 + f + 1], a_.ap, ones[:, 0:1], start=True, stop=True), t2, *(misc.busy if f == 0 else []))
                    a_.busy = [stt["row"]]
                return last

            if on_pool:
                for n in (512, 256, 128):
                    t = TT(raw[i % 4][:, 0:n], raw[i % 4][:, 0:n], raw[i % 4][:, n:2 * n], ADD, t, q=pool)

                def reduce():
                    sl = pring.take()
                    pe.wait(*sl.busy)
                    t2 = pe.op(lambda e: e.matmul(sl.ap[:, 0:1], raw[i % 4][:, 0:P], ones[:, 0:1], start=True, stop=True), t)
                    ws.done(i, t2)
                    stt["row"] = CP(pbias[:, f:f + 1], sl.ap[:, 0:1], t2)
                    sl.busy = [stt["row"]]
            due.append(reduce)

        def row_steps(n=1):
            for _ in range(n):
                for _ in range(len(due)):
                    nxt = due.pop(0)()
                    if nxt:
                        due.append(nxt)

        def ada_step(n):
            row_steps()
            if n in ADA_AT and upto >= 3:
                f = ADA_AT.index(n)
                row_tile(f"ada{f}", f, SC[:], 0, tsc)
                row_steps()

        norm, htoks = Norm(1024), []
        xt = add_to_x("wo", yr, xt, feeder(norm, lambda k: col("norm_mlp", k), htoks, ty, *toks))
        hidden["free"] = [[pe.last], [pe.last]]
        h = Rhs(HHs, HLs, htoks)
        n2, htoks2 = Norm(1024, lambda k: col("norm_final", k)), []

        tspill = []

        def on_last(m, t):
            feeder(n2, lambda k: gprod[:, k:k + 1], htoks2, stt["ups"])(m, t)
            if upto >= 2:
                tspill.append(dma(sp, dx[m], xsc[:, m, :], X[:, m, :], t))

        xt = mlp("dn", *relu_up("up", h, norm), 8, X, [[t] for t in xt], norm=norm, on_last=on_last, step=ada_step)
        if upto >= 3:
            row_steps(2)
            stt["mod"] = TT(mod[:], misc.ap[:, 0:48], col("b_ada", 0, 48), ADD, stt["row"])
            misc.busy = [stt["mod"]]

        if upto >= 2:
            h = Rhs(HHs, HLs, htoks2)
            gfree = [pe.last]
            sg0, tg0 = job("gg0", h, 8)
            n2.stats()
            sv0, tv0 = job("gv0", h, 8)
            n2.to_rt()
            tr1 = CP(rx[:], n2.r1, n2.t)
            xfree = [*tspill, dve.last, act.last]
            QA, KA, QB, KB = G(0, [P, 3, S]), G(3, [P, 3, S]), G(6, [P, 3, S]), G(9, [P, 3, S])
            VA, CF = G(12, [P, 8, 384]), G(15, [P, S])
            UC, YC, VB = unit(XO, 0, [P, 2, 1054]), unit(XO, 3, [P, 2, S]), unit(XO, 5, [P, 8, 384])
            ctok = [None, None]

            def gate_out(m, sg, tg, sv, tv):
                b = tring.take()
                t = TT(b.ap[:], sg.ap[:], RT[:], MUL, tg, n2.rt, *b.busy)
                sg.busy = [t]
                t = A(b.ap[:], b.ap[:], ACT.Sigmoid, t)
                t = TT(b.ap[:], b.ap[:], sv.ap[:], MUL, tv, t)
                sv.busy = [t]
                t = TT(UC[:, m, 30:], b.ap[:], RT[:], MUL, t, *xfree)
                b.busy = [t]
                ctok[m] = A(YC[:, m, :], UC[:, m, 30:], ACT.Identity, t, *xfree, scale=col("conv2", 31 * m + 30), bias=col("conv2_b", m))

            gate_out(0, sg0, tg0, sv0, tv0)
            tpad = pool.op(lambda e: e.memset(UC[:, :, 0:30], 0.0), *xfree)
            sg0, tg0 = job("gg1", h, 8)
            sv0, tv0 = job("gv1", h, 8)
            gate_out(1, sg0, tg0, sv0, tv0)
            dve.wait(tpad)

            def taps(m, k0, k1):
                for k in range(k0, k1):
                    ctok[m] = STT(YC[:, m, :], UC[:, m, k:k + S], col("conv2", 31 * m + k), YC[:, m, :], MUL, ADD, ctok[m])

            def ln_mean():
                pe.wait(*ctok, *misc.busy)
                for hf in range(2):
                    cs = slice(512 * hf, 512 * hf + 512)
                    for m in range(2):
                        t = pe.op(lambda e, m=m, cs=cs: e.matmul(misc.ap[:, cs], ones[:], YC[:, m, cs], start=(m == 0), stop=(m == 1)))
                for m in range(2):
                    ctok[m] = STT(YC[:, m, :], misc.ap[:], -1.0 / 256, YC[:, m, :], MUL, ADD, t)
                misc.busy = [dve.last]

            def ln_rest():
                nl = Norm(256)
                for m in range(2):
                    nl.feed(YC[:, m, :], ctok[m])
                nl.stats()
                sl, tR = nl.spread()
                for m in range(2):
                    t = STT(YC[:, m, :], YC[:, m, :], col("cn_g", m), sl.ap[:], MUL, MUL, tR)
                    ctok[m] = A(YC[:, m, :], YC[:, m, :], ACT.Silu, t, bias=col("cn_b", m))
                sl.busy = [dve.last]

            fill = []
            for m in range(2):
                for k in range(0, 30, 5):
                    fill.append(lambda m=m, k=k: taps(m, k, k + 5))
            fill += [ln_mean, ln_rest]

            sl, tok = job("fa", h, 8, m=W2)
            a6, b6, o6 = T[0], T[1], T[2]
            for s_ in (a6, b6, o6):
                act.wait(*s_.busy)
                dve.wait(*s_.busy)
            t = TT(o6.ap[0:6, :], sl.ap[0:6, :], RT[0:6, :], MUL, tok)
            sl.busy = [t]
            g_, ta, tb_ = logsig(o6.ap[0:6, :], cols[0:6, COLS["b_forget"][0]:COLS["b_forget"][0] + 1], a6.ap[0:6, :], b6.ap[0:6, :], a6.ap[0:6, :], t)
            t1 = dve.op(lambda e: e.memset(o6.ap[0:6, :], 1.0), ta, tb_)
            tcf = dve.op(lambda e: e.tensor_tensor_scan(CF[0:6, :], o6.ap[0:6, :], a6.ap[0:6, :], 0.0, MUL, ADD), t1, g_, *gfree)
            for s_ in (a6, b6, o6):
                s_.busy = [tcf]

            def proj(n, dst, scale=1.0):
                for m in range(3):
                    sl, tok = job(f"{n}{m}", h, 8)
                    turn_now()
                    t = STT(dst[:, m, :], sl.ap[:], scale, RT[:], MUL, MUL, tok, *gfree)
                    sl.busy = [t]
                    fills(1)
                return t

            def projv(n, dst, *w):
                for m in range(3):
                    sl, tok = job(f"{n}{m}", h, 8)
                    turn_now()
                    b = tring.take()
                    t = TT(b.ap[:], sl.ap[:], RT[:], MUL, tok, *b.busy)
                    sl.busy = [t]
                    turned(b, t, dst[:, :, P * m:P * m + P], *w)
                    fills(1)

            projv("vb", VB, *xfree)
            turn_now()
            tvb = act.last
            vsc = nc.dram_tensor("vsc", (S, 384), F, kind="Internal").ap()
            dv_ = Dsem("vs")
            tvs = dma(sp, dv_, vsc.rearrange("(b p) c -> p b c", p=P), VB[:], tvb)
            proj("qb", QB, 0.125)
            tdil = proj("kb", KB)
            projv("va", VA, *gfree)
            proj("qa", QA, 0.125)
            tproj = proj("ka", KA)
            turn_now()
            fills(len(fill))
            stt["rtfree"] = [dve.last]
            tva = act.last
            hfree = [pe.last]

            def Hu(n, shape, dt=F):
                return unit(HO, n, shape, dt)

            sring = Ring([Slot(Hu(0, [P, S])), Slot(Hu(1, [P, S]))])
            prng = Ring([Slot(Hu(2, [P, S])), Slot(Hu(3, [P, S]))])
            ptring = Ring([Slot(Hu(4, [P, S])), Slot(Hu(5, [P, S]))])
            CN = Hu(6, [P, 6, S])
            SEL = Hu(12, [6, 6, P])
            V4, V16 = Hu(13, [P, 8, 384]), unit(XO, 0, [P, 8, 384])
            dsel, dv4, dv16 = Dsem("sel"), Dsem("v4"), Dsem("v16")
            tsel = dma(sp, dsel, SEL[:], d["sel"], *hfree)
            for n in range(2):
                tv4 = dma(sp, dv4, V4[:, 4 * n:4 * n + 4, :], vsc[512 * n:512 * n + 512, :].rearrange("(j r) c -> j r c", r=4), tvs, *hfree)
            tv16 = dma(sp, dv16, V16[:], vsc.rearrange("(j u) c -> j u c", u=8), tvs, *ctok)
            gate_toks = []

            def gate_sums(hd):
                sl = pring.take()
                pe.wait(tsel, tcf, *sl.busy)
                for hf in range(2):
                    t = pe.op(lambda e, hf=hf, hd=hd: e.matmul(sl.ap[:, 512 * hf:512 * hf + 512], SEL[0:6, hd, :], CF[0:6, 512 * hf:512 * hf + 512], start=True, stop=True))
                gate_toks.append(A(CN[:, hd, :], sl.ap[:], ACT.Copy, t, *hfree, scale=-1.0))
                sl.busy = [gate_toks[-1]]

            stat = Ring([Slot(st), Slot(rr)])
            mhalf = [Slot(misc.ap[:, 0:512]), Slot(misc.ap[:, 512:1024])]
            lzs = [Slot(lz[:, 0:8]), Slot(lz[:, 8:16])]
            YF, YD = unit(XO, 0, [P, 3, S]), unit(XO, 5, [P, 3, S])
            junk, ssf, ssd, srf, srd = CF[:, 0:384], CF[:, 512:520], CF[:, 520:528], CF[:, 528:536], CF[:, 536:544]

            def pt_copy(n, dst, src, *w):
                if n % 3:
                    return A(dst, src, ACT.Copy, *w)
                return CP(dst, src, *w)

            def rows(b, i, ss, dst, t):
                t2 = A(junk, b.ap[:, 0:384], ACT.Square, t, gate_toks[-1], accum=ss[:, i:i + 1])

                def back():
                    sl = pring.take()
                    pe.wait(t, *sl.busy)
                    for m in range(3):
                        f = lambda e, m=m: e.transpose(sl.ap[:, P * m:P * m + P], b.ap[:, P * m:P * m + P], ident[:])
                        t3 = pe.op(f) if m == 2 else pe.go(f)
                    b.busy = [t2, t3]
                    t3 = CP(dst[:, :, P * i:P * i + P], v3(sl.ap[:, 0:384], 3), t3, *ydfree)
                    sl.busy = [t3]
                return back

            def rows_normed(ss, sr, gname, dst):
                t = A(sr, ss, ACT.Sqrt, act.last, scale=1.0 / 384, bias=epsc[:])
                t = dve.op(lambda e: e.reciprocal(sr, sr), t)
                b = tring.take()
                t = TT(v3(b.ap[:], 8), ident[:].unsqueeze(1).broadcast_to([P, 8, P]), sr.unsqueeze(2).broadcast_to([P, 8, P]), MUL, t, *b.busy)

                def back():
                    sl = pring.take()
                    pe.wait(t, *sl.busy)
                    for hf in range(2):
                        t2 = pe.op(lambda e, hf=hf: e.matmul(sl.ap[:, 512 * hf:512 * hf + 512], ones[:], b.ap[:, 512 * hf:512 * hf + 512], start=True, stop=True))
                    b.busy = [t2]
                    t3 = [STT(dst[:, m, :], dst[:, m, :], col(gname, m), sl.ap[:], MUL, MUL, t2) for m in range(3)]
                    sl.busy = [t3[-1]]
                    return t3
                return back

            units = [(i, hd) for i in range(7, -1, -1) for hd in range(6)]

            def scores(i, hd):
                t_, hh = hd // 2, hd % 2
                ps_ = slice(64 * hh, 64 * hh + 64)
                w = P * (i + 1)
                sl = pring.take()
                pe.wait(tproj, *sl.busy)
                for hf in range(-(-w // 512)):
                    n = min(512, w - 512 * hf)
                    diag = hf == (P * i) // 512
                    pe.go(lambda e, hf=hf, n=n, diag=diag: e.matmul(sl.ap[:, 512 * hf:512 * hf + n], QA[ps_, t_, P * i:P * i + P], KA[ps_, t_, 512 * hf:512 * hf + n], start=True, stop=not diag))
                t = pe.op(lambda e: e.matmul(sl.ap[:, P * i:P * i + P], identb[:], negm[:, 1, :], start=False, stop=True))
                return sl, t

            def soft(i, hd, sl, t):
                w = P * (i + 1)
                s_, p_ = sring.take(), prng.take()
                l_ = lzs[i % 2]
                mx = stat.take()
                t = dve.op(lambda e: e.tensor_tensor_reduce(out=s_.ap[:, 0:w], in0=sl.ap[:, 0:w], in1=CN[:, hd, 0:w], scale=-1.0, scalar=3.0e38, op0=ADD, op1=MIN, accum_out=mx.ap[:, 0:1]), t, gate_toks[hd], *s_.busy, *mx.busy)
                sl.busy = [t]
                t = A(p_.ap[:, 0:w], s_.ap[:, 0:w], ACT.Exp, t, *p_.busy, *(l_.busy if hd == 0 else []), scale=-1.0, bias=mx.ap[:, 0:1], accum=l_.ap[:, hd:hd + 1])
                s_.busy = [t]
                mx.busy = [t]
                return p_, t

            def turn(blocks, p_, t, n):
                sl = pring.take()
                pe.wait(t, *sl.busy)
                for j in range(blocks):
                    f = lambda e, j=j: e.transpose(sl.ap[:, P * j:P * j + P], p_.ap[:, P * j:P * j + P], ident[:])
                    t = pe.op(f) if j == blocks - 1 else pe.go(f)
                p_.busy = [t]
                q_ = ptring.take()
                t = pt_copy(n, q_.ap[:, 0:P * blocks], sl.ap[:, 0:P * blocks], t, *q_.busy)
                sl.busy = [t]
                return q_, t

            def fox_pv(i, hd, q_, t):
                mh = mhalf[i % 2]
                pe.wait(t, tva, *(mh.busy if hd == 0 else []))
                for j in range(i + 1):
                    f = lambda e, j=j: e.matmul(mh.ap[:, 64 * hd:64 * hd + 64], q_.ap[:, P * j:P * j + P], VA[:, j, 64 * hd:64 * hd + 64], start=(j == 0), stop=(j == i))
                    t = pe.op(f) if j == i else pe.go(f)
                q_.busy = [t]
                return t

            def fox_out(i, t):
                mh, l_ = mhalf[i % 2], lzs[i % 2]
                b = tring.take()
                t2 = dve.op(lambda e: e.reciprocal(l_.ap[:, 0:6], l_.ap[:, 0:6]), act.last)
                t2 = TT(v3(b.ap[:, 0:384], 6), v3(mh.ap[:, 0:384], 6), l_.ap[:, 0:6].unsqueeze(2).broadcast_to([P, 6, 64]), MUL, t2, t, *b.busy)
                mh.busy = [t2]
                l_.busy = [t2]
                return rows(b, i, ssf, YF, t2)

            dsc = nc.dram_tensor("dsc", (3, S, 396), F, kind="Internal").ap()
            ddo = [Dsem(f"do{i}") for i in range(3)]

            def dtok(ap, br, u, prev):
                if br == 0:
                    return ap[:, P * (u - prev):P * u + P]
                if br == 1:
                    return ap.rearrange("p (j r) -> p r j", r=4)[:, u % 4, P * (u // 4 - prev):P * (u // 4) + P]
                return ap.rearrange("p (j u) -> p u j", u=8)[:, u, :]

            dun = [(br, u, t_) for br in range(3) for u in range(8) for t_ in range(3)]

            def has_prev(br, u):
                return int((br == 0 and u > 0) or (br == 1 and u >= 4))

            def dscores(br, u, t_):
                pv_ = has_prev(br, u)
                w = P * (1 + pv_)
                sl = pring.take()
                pe.wait(tdil, *sl.busy)
                for hh in range(2):
                    ps_ = slice(64 * hh, 64 * hh + 64)
                    q_ = dtok(QB[ps_, t_, :], br, u, 0)
                    k_ = dtok(KB[ps_, t_, :], br, u, pv_)
                    o_ = sl.ap[:, 512 * hh:512 * hh + w]
                    pe.go(lambda e, o_=o_, q_=q_, k_=k_: e.matmul(o_, q_, k_, start=True, stop=False))
                for hh in range(2):
                    mk = 2 if br == 2 else 1 - pv_
                    f = lambda e, hh=hh, mk=mk: e.matmul(sl.ap[:, 512 * hh:512 * hh + w], identb[:], negm[:, mk:mk + 1 + pv_, :].rearrange("p a b -> p (a b)"), start=False, stop=True)
                    t = pe.op(f) if hh == 1 else pe.go(f)
                return sl, t

            dcur = {}

            def dsoft(br, u, t_, sl, t):
                w = P * (1 + has_prev(br, u))
                if t_ == 0:
                    dcur[(br, u)] = tring.take()
                    act.wait(*dcur[(br, u)].busy)
                    dve.wait(*dcur[(br, u)].busy)
                o_ = dcur[(br, u)]
                p_ = prng.take()
                sv = v3(sl.ap[:], 2)[:, :, 0:w]
                t = dve.op(lambda e: e.tensor_reduce(o_.ap[:, 384 + 2 * t_:386 + 2 * t_], sv, AX.X, MAX, negate=True), t)
                for hh in range(2):
                    c_ = 2 * t_ + hh
                    t2 = A(p_.ap[:, w * hh:w * hh + w], sl.ap[:, 512 * hh:512 * hh + w], ACT.Exp, t, *p_.busy, bias=o_.ap[:, 384 + c_:385 + c_], accum=o_.ap[:, 390 + c_:391 + c_])
                sl.busy = [t2]
                return p_, t2

            def dpv(br, u, t_, q_, t, cnt):
                nb = 1 + has_prev(br, u)
                mh = mhalf[cnt % 2]
                pe.wait(t, (tvb, tv4, tv16)[br], *(mh.busy if t_ == 0 else []))
                for hh in range(2):
                    hd = 2 * t_ + hh
                    for j in range(nb):
                        if br == 0:
                            v_ = VB[:, u - nb + 1 + j, :]
                        elif br == 1:
                            v_ = V4[:, 4 * (u // 4 - nb + 1 + j) + u % 4, :]
                        else:
                            v_ = V16[:, u, :]
                        f = lambda e, hd=hd, j=j, hh=hh, v_=v_: e.matmul(mh.ap[:, 64 * hd:64 * hd + 64], q_.ap[:, P * (nb * hh + j):P * (nb * hh + j) + P], v_[:, 64 * hd:64 * hd + 64], start=(j == 0), stop=(j == nb - 1))
                        t = pe.op(f) if hh == 1 and j == nb - 1 else pe.go(f)
                q_.busy = [t]
                return t

            def dout_(br, u, t, cnt):
                mh = mhalf[cnt % 2]
                o_ = dcur.pop((br, u))
                t = CP(o_.ap[:, 0:384], mh.ap[:, 0:384], t)
                mh.busy = [t]
                ds = ddo[cnt % 3]
                if br == 0:
                    t = dma(sp, ds, dsc[0, P * u:P * u + P, :], o_.ap[:, 0:396], t, act.last)
                elif br == 1:
                    n_, r_ = u // 4, u % 4
                    t = dma(sp, ds, dsc[1, 512 * n_:512 * n_ + 512, :].rearrange("(j r) c -> r j c", r=4)[r_], o_.ap[:, 0:396], t, act.last)
                else:
                    t = dma(sp, ds, dsc[2].rearrange("(j u) c -> u j c", u=8)[u], o_.ap[:, 0:396], t, act.last)
                o_.busy = [t]
                return t

            stage, nrow = {}, 0
            n = len(dun)
            dall = {}
            for s_i in range(n + 3):
                if s_i < n:
                    stage[s_i] = dscores(*dun[s_i])
                if s_i >= 1 and s_i - 1 < n:
                    stage[s_i - 1] = dsoft(*dun[s_i - 1], *stage[s_i - 1])
                if s_i >= 2 and s_i - 2 < n:
                    u = dun[s_i - 2]
                    stage[s_i - 2] = turn(2 * (1 + has_prev(u[0], u[1])), *stage[s_i - 2], s_i)
                if s_i >= 3:
                    u = dun[s_i - 3]
                    cnt = u[0] * 8 + u[1]
                    t = dpv(*u, *stage.pop(s_i - 3), cnt)
                    if u[2] == 2:
                        dall[cnt % 3] = dout_(u[0], u[1], t, cnt)
                    if s_i % 10 == 5 and s_i < 60:
                        gate_sums(s_i // 10)
                if upto >= 3 and s_i >= 8:
                    row_steps()
                    if s_i % 3 and nrow < 44:
                        row_tile(f"b{nrow}", nrow, mod[:, 0:8] if nrow < 12 else mod[:, 24:32], 0, stt["mod"], on_pool=True)
                        nrow += 1

            ydfree = [pe.last]
            cm = [at(GO + 6 * 4096 + 5376 * i, [P, 3, 448]) for i in range(2)]
            dcm = [Dsem("cm0"), Dsem("cm1")]
            loaded = {}

            def join_load(i, *w):
                loaded[i] = dma(sp, dcm[i % 2], cm[i % 2][:, :, 0:396], dsc[:, P * i:P * i + P, :].rearrange("a p c -> p a c"), *w)

            for i in range(2):
                join_load(i, *dall.values(), pe.last)

            def join(i):
                C = cm[i % 2]
                tl_ = loaded[i]
                mm_ = C[:, :, 384:390]
                t = TT(C[:, 0, 400:406], mm_[:, 0, :], mm_[:, 1, :], MIN, tl_)
                t = TT(C[:, 0, 400:406], C[:, 0, 400:406], mm_[:, 2, :], MIN, t)
                t = TT(C[:, :, 410:416], C[:, 0:1, 400:406].broadcast_to([P, 3, 6]), mm_, SUB, t)
                t = A(C[:, :, 410:416], C[:, :, 410:416], ACT.Exp, t)
                return t

            def join_sum(i, t):
                C = cm[i % 2]
                ll_ = C[:, :, 390:396]
                t1 = TT(C[:, :, 420:426], C[:, :, 410:416], ll_, MUL, t)
                t1 = TT(C[:, 0, 420:426], C[:, 0, 420:426], C[:, 1, 420:426], ADD, t1)
                t1 = TT(C[:, 0, 420:426], C[:, 0, 420:426], C[:, 2, 420:426], ADD, t1)
                t1 = dve.op(lambda e, C=C: e.reciprocal(C[:, 0, 430:436], C[:, 0, 420:426]), t1)
                for br in range(3):
                    v_ = v3(C[:, br, 0:384], 6)
                    t2 = TT(v_, v_, C[:, br, 410:416].unsqueeze(2).broadcast_to([P, 6, 64]), MUL, t, q=pool)
                t2 = TT(C[:, 0, 0:384], C[:, 0, 0:384], C[:, 1, 0:384], ADD, t2, q=pool)
                t2 = TT(C[:, 0, 0:384], C[:, 0, 0:384], C[:, 2, 0:384], ADD, t2, q=pool)
                b = tring.take()
                t2 = TT(v3(b.ap[:, 0:384], 6), v3(C[:, 0, 0:384], 6), C[:, 0, 430:436].unsqueeze(2).broadcast_to([P, 6, 64]), MUL, t2, t1, *b.busy, q=pool)
                if i + 2 < 8:
                    join_load(i + 2, t2)
                return rows(b, i, ssd, YD, t2)

            backs = []
            n = len(units)
            for s_i in range(n + 3):
                if s_i < n:
                    stage[s_i] = scores(*units[s_i])
                if s_i >= 1 and s_i - 1 < n:
                    stage[s_i - 1] = soft(*units[s_i - 1], *stage[s_i - 1])
                if s_i >= 2 and s_i - 2 < n:
                    u = units[s_i - 2]
                    stage[s_i - 2] = turn(u[0] + 1, *stage[s_i - 2], s_i)
                if s_i in (2, 3) and upto >= 3:
                    row_steps()
                    tpb = stt["row"]
                if s_i < 32 and s_i % 4 == 3:
                    tj = join(s_i // 4)
                elif s_i < 36 and s_i % 4 == 0 and s_i:
                    joined = join_sum(s_i // 4 - 1, tj)
                elif s_i < 36 and s_i % 4 == 2 and s_i > 4:
                    joined()
                elif s_i == 36:
                    joined = rows_normed(ssd, srd, "dil", YD)
                elif s_i == 38:
                    joined()
                if s_i >= 3:
                    u = units[s_i - 3]
                    t = fox_pv(*u, *stage.pop(s_i - 3))
                    if backs and u[1] == 2:
                        backs.pop()()
                    if u[1] == 5:
                        backs.append(fox_out(u[0], t))
            gfree = [pe.last, dve.last, act.last, pool.last]
            toks = [None] * 8
            for k in (3, 4, 5):
                toks[k] = split(YD[:, k - 3, :], GHs[k], GLs[k], *gfree, q=(pool, dve)[k % 2])
            while backs:
                backs.pop()()
            tf = rows_normed(ssf, srf, "fox", YF)
            gfree.append(dve.last)
            for k in (6, 7):
                toks[k] = split(YC[:, k - 6, :], GHs[k], GLs[k], *gfree)
            tf()

            for k in range(3):
                toks[k] = split(YF[:, k, :], GHs[k], GLs[k], dve.last, *gfree, q=(dve, pool)[k % 2])
            xfree = [pool.last, dve.last]
            xt = [dma(sp, dx[k], X[:, k, :], xsc[:, k, :], *xfree) for k in range(8)]
            misc.busy = [dve.last, act.last]
            dgx = tring.take()
            t = TT(v3(dgx.ap[:], 8), ident[:].unsqueeze(1).broadcast_to([P, 8, P]), rx[:].unsqueeze(2).broadcast_to([P, 8, P]), MUL, tr1, *dgx.busy)
            xrt = [t]

            def first_norm(m, tx):
                if m == 0:
                    sl = pring.take()
                    pe.wait(*xrt, *sl.busy)
                    for hf in range(2):
                        t = pe.op(lambda e, hf=hf: e.matmul(sl.ap[:, 512 * hf:512 * hf + 512], ones[:], dgx.ap[:, 512 * hf:512 * hf + 512], start=True, stop=True))
                    dgx.busy = [t]
                    xrt[0] = A(RT[:], sl.ap[:], ACT.Copy, t, *stt["rtfree"])
                    sl.busy = [xrt[0]]
                t = STT(X[:, m, :], X[:, m, :], col("norm_final", m), RT[:], MUL, MUL, xrt[0], tx)
                stt["rtfree"] = [t]
                return t

            norm, htoks = Norm(1024), []
            xt = add_to_x("w2o", Rhs(GHs, GLs, toks, order=[3, 4, 5, 6, 7, 0, 1, 2]), xt, feeder(norm, lambda k: col("ln2", k), htoks, *toks), first_norm)
            hidden["free"] = [[pe.last], [pe.last]]
            h = Rhs(HHs, HLs, htoks)
            def up_job(m, mid):
                a_ = job(f"fupa{m}", h, 8)
                if mid:
                    mid()
                else:
                    a_ = gate_drain(m, a_)
                return a_, job(f"fupb{m}", h, 8), mid is None

            def conv_drain(sl, tok, f):
                b0 = tring.take()
                t0 = TT(b0.ap[:], sl.ap[:], RT[:], MUL, tok, norm.rt, *b0.busy)
                sl.busy = [t0]
                b = tring.take()
                t = A(b.ap[:], b0.ap[:], ACT.Identity, t0, *b.busy, scale=col("ffn_w", 3 * f + 2), bias=col("ffn_b", f))
                t = STT(b.ap[:, 1:], b0.ap[:, 0:S - 1], col("ffn_w", 3 * f + 1), b.ap[:, 1:], MUL, ADD, t)
                t = STT(b.ap[:, 2:], b0.ap[:, 0:S - 2], col("ffn_w", 3 * f), b.ap[:, 2:], MUL, ADD, t)
                b0.busy = [t]
                return b, t

            def gate_drain(m, got):
                a_, ta = conv_drain(*got, m)
                return a_, A(a_.ap[:], a_.ap[:], ACT.Silu, ta)

            def up_drain(m, got):
                a_, (sb_, tb_), drained = got
                a_, ta = a_ if drained else gate_drain(m, a_)
                b_, tb2 = conv_drain(sb_, tb_, NPAIR + m)
                t = TT(a_.ap[:], a_.ap[:], b_.ap[:], MUL, ta, tb2)
                b_.busy = [t]
                return a_, t

            if upto >= 3:
                tg = stt["mod"]
                for j, (m0, name, one) in enumerate(((8, "n1pre", 1.0), (16, "n1post", 0.0), (32, "n2pre", 1.0), (40, "n2post", 0.0))):
                    tg = STT(gains[:, 8 * j:8 * j + 8], mod[:, m0:m0 + 8], one, col(name, 0, 8), ADD, MUL, tg)
                tg = TT(gprod[:, 8:16], gains[:, 0:8], col("g_final", 0, 8), MUL, tg)
                dve.wait(tg)
                act.wait(tg)
            n3, htoks3 = Norm(1024, lambda k: col("g_final", k)), []

            def on_last3(m, t):
                feeder(n3, (lambda k: gprod[:, 8 + k:9 + k]) if upto >= 3 else None, htoks3, stt["ups"])(m, t)

            xt = mlp("fdn", up_job, up_drain, 6, X, [[t] for t in xt], sizes=[2] + [4] * 5, norm=norm,
                     on_last=on_last3)

        if upto >= 3:
            def gain(j):
                return lambda k: gains[:, 8 * j + k:8 * j + k + 1]

            hfree, gfree = [pe.last], [pe.last, tg]
            UU, VT, YB, MIX = G(0, [P, 4, S]), G(4, [P, 8, 512]), G(8, [P, 4, S]), G(8, [P, 8, S])
            so = GO + 12 * 4096
            WSP, BSP, GNB, BNB, WPL = (at(so + 2048 * i, [P, 512]) for i in range(5))
            TRI = at(so + 10240, [P, P])
            BST = at(so + 10752, [P, 8, 6])
            MV = at(so + 10752 + 192, [P, 8, 2])
            RV = at(so + 10752 + 256, [P, 8])
            PBI = at(so + 10752 + 288, [P, 4])
            ds3 = Dsem("b3")
            dma(sp, ds3, v3(WSP[:], 4), d["w_sp"], *gfree)
            dma(sp, ds3, v3(WPL[:], 4), d["w_pool"], *gfree)
            dma(sp, ds3, TRI[:], d["tri"], *gfree)
            dma(sp, ds3, v3(BSP[:], 4), d["b_sp"].unsqueeze(0).broadcast_to([P, 4, P]), *gfree)
            dma(sp, ds3, GNB[:], d["lnv_g"].unsqueeze(0).broadcast_to([P, 512]), *gfree)
            t3 = dma(sp, ds3, BNB[:], d["lnv_b"].unsqueeze(0).broadcast_to([P, 512]), *gfree)
            h = Rhs(HHs, HLs, htoks3)
            got0 = job("zv0", h, 8)
            n3.stats()
            got1 = job("zv1", h, 8)
            n3.to_rt()
            for q in (dve, act):
                q.wait(tpb)
            twsp = TT(v3(WSP[:], 4), v3(WSP[:], 4), TRI[:].unsqueeze(1).broadcast_to([P, 4, P]), MUL, t3)
            tpbi = TT(PBI[:], col("b_pool", 0, 4), col("pscale", 0, 4), MUL, t3)

            for m in range(4):
                sl, tok = (got0, got1)[m] if m < 2 else job(f"zv{m}", h, 8)
                if m >= 2:
                    turn_now()
                b = tring.take()
                tv = TT(b.ap[:], sl.ap[:], RT[:], MUL, tok, n3.rt, *b.busy)
                sl.busy = [tv]
                tv = A(b.ap[:], b.ap[:], ACT.Gelu_apprx_tanh, tv, bias=pbias[:, 4 + m:5 + m])
                turned(b, tv, VT[:, :, P * m:P * m + P], *gfree)

            def ln_stats(tv):
                for c in range(8):
                    t = dve.op(lambda e, c=c: e.bn_stats(BST[:, c, :], VT[:, c, :]), tv, t3)
                for c in range(8):
                    t2 = dve.op(lambda e, c=c: e.bn_aggr(MV[:, c, :], BST[:, c, :]), t)
                t2 = A(RV[:], MV[:, :, 1], ACT.Sqrt, t2, bias=epsc[:])
                return t2

            def ln_rows(t2):
                t2 = dve.op(lambda e: e.reciprocal(RV[:], RV[:]), t2)
                for c in range(8):
                    t2 = TS(VT[:, c, :], VT[:, c, :], MV[:, c, 0:1], RV[:, c:c + 1], SUB, MUL, t2)
                stt["ln"] = t2

            def ln_gains(hf):
                v_ = VT[:, 2 * hf:2 * hf + 2, :]
                tg_ = TT(v_, v_, GNB[:].unsqueeze(1).broadcast_to([P, 2, 512]), MUL, stt["ln"], q=pool)
                stt["vt"] = TT(v_, v_, BNB[:].unsqueeze(1).broadcast_to([P, 2, 512]), ADD, tg_, q=pool)

            utok = {}

            def spatial(m):
                sl = pring.take()
                pe.wait(stt["vt"], twsp, *sl.busy)
                for c in range(8):
                    f = lambda e, c=c: e.matmul(sl.ap[:, P * c:P * c + P], VT[:, c, P * m:P * m + P], WSP[:, P * m:P * m + P], start=True, stop=True)
                    t = pe.op(f) if c == 7 else pe.go(f)
                b = tring.take()
                t = TT(v3(b.ap[:], 8), v3(sl.ap[:], 8), BSP[:, P * m:P * m + P].unsqueeze(1).broadcast_to([P, 8, P]), ADD, t, *b.busy)
                sl.busy = [t]
                utok[m] = TT(UU[:, m, :], UU[:, m, :], b.ap[:], MUL, t, utok[m])
                b.busy = [utok[m]]

            ybt = {}
            def pool_out(m, z, t):
                sl = pring.take()
                pe.wait(t, t3, *sl.busy)
                for hf in range(2):
                    cs = slice(512 * hf, 512 * hf + 512)
                    f = lambda e, cs=cs: e.matmul(sl.ap[:, cs], WPL[:, P * m:P * m + P], z.ap[:, cs], start=True, stop=True)
                    t = pe.op(f) if hf else pe.go(f)
                z.busy = [t]
                ybt[m] = A(YB[:, m, :], sl.ap[:], ACT.Identity, t, tpbi, *gfree, scale=col("pscale", m), bias=PBI[:, m:m + 1])
                sl.busy = [ybt[m]]

            for m in range(4):
                sl, tok = job(f"zb{m}", h, 8)
                if m == 0:
                    tvt = turn_now()
                else:
                    pool_out(*pend)
                z = tring.take()
                t = TT(z.ap[:], sl.ap[:], RT[:], MUL, tok, *z.busy)
                sl.busy = [t]
                t = A(z.ap[:], z.ap[:], ACT.Identity, t, bias=pbias[:, 8 + m:9 + m])
                a_ = tring.take()
                b_ = tring.take() if m else None
                src = z
                bufs = [a_, b_]
                dve.wait(*a_.busy, *(b_.busy if b_ else []))
                for j in range(m + 1):
                    s_ = 1 << j
                    o_ = bufs[j % 2]
                    t1 = CP(o_.ap[:, 0:s_], src.ap[:, 0:s_], t)
                    t = TT(o_.ap[:, s_:], src.ap[:, s_:], src.ap[:, 0:S - s_], ADD, t, t1)
                    src = o_
                w_ = 2 << m
                t1 = TT(src.ap[:, 0:16], src.ap[:, 0:16], col("rcnt", 16 * m, 16), MUL, t)
                t1 = TT(z.ap[:, 0:16], src.ap[:, 0:16], z.ap[:, 0:16], SUB, t1)
                t = STT(z.ap[:, 16:], src.ap[:, 16:], 1.0 / w_, z.ap[:, 16:], MUL, SUB, t, t1)
                a_.busy = [t]
                if b_:
                    b_.busy = [t]
                pend = (m, z, t)
                if m == 0:
                    tvt = ln_stats(tvt)
                else:
                    if m == 1:
                        ln_rows(tvt)
                    ln_gains(m - 1)
            toks = [None] * 8
            for m in range(4):
                sl, tok = job(f"zu{m}", h, 8)
                if m == 0:
                    pool_out(*pend)
                t = TT(UU[:, m, :], sl.ap[:], RT[:], MUL, tok, *gfree)
                sl.busy = [t]
                utok[m] = A(UU[:, m, :], UU[:, m, :], ACT.Gelu_apprx_tanh, t, bias=pbias[:, m:m + 1])
                hlast = [pe.last]
                if m == 0:
                    ln_gains(3)
                elif m == 1:
                    spatial(0)
                if m:
                    spatial(m)
            stt["rtfree"] = [dve.last]
            for k in range(4, 8):
                toks[k] = split(YB[:, k - 4, :], HH[:, k, :], HL[:, k, :], ybt[k - 4], *hlast, q=(dve, pool)[k % 2])
            for k in range(4):
                toks[k] = split(UU[:, k, :], HH[:, k, :], HL[:, k, :], utok[k], *hlast, q=(dve, pool)[k % 2])
            mfree = [dve.last, pool.last]
            yr = Rhs(HHs, HLs, toks, order=[4, 5, 6, 7, 0, 1, 2, 3])
            nm = Norm(1024)
            for m in range(8):
                sl, tok = job(f"wo3{m}", yr, 8)
                t = A(MIX[:, m, :], sl.ap[:], ACT.Copy, tok, *mfree)
                sl.busy = [t]
                nm.feed(MIX[:, m, :], t)
                if m == 0:
                    dg = Slot(unit(GO, 4, [P, S]))
                    dg.busy = [pe.last]
                    s1, t1 = n3.first(dg)
                    for k in range(8):
                        xt[k] = STT(X[:, k, :], X[:, k, :], col("g_final", k), s1.ap[:], MUL, MUL, t1, act.last)
                    s1.busy = [xt[-1]]
            nm.stats()
            sR, tR = nm.spread()
            xt2 = []
            nx, htoks, hl = Norm(1024), [], [pe.last]

            def x_ready(k):
                htoks.append(weigh(k, X[:, k, :], gain(2)(k), HH, HL, xt2[k], *hl))
                nx.feed(X[:, k, :], xt2[k], q=(dve, pool)[k % 2])

            for k in range(8):
                t = STT(MIX[:, k, :], MIX[:, k, :], gain(1)(k), sR.ap[:], MUL, MUL, tR, nm.t)
                xt2.append(TT(X[:, k, :], X[:, k, :], MIX[:, k, :], ADD, t, q=(pool, dve)[k % 2]))
                if k:
                    x_ready(k - 1)
            x_ready(7)
            sR.busy = [dve.last]
            hidden["free"] = [[pe.last, *xt2], [pe.last, *xt2]]
            h = Rhs(HHs, HLs, htoks)
            tsp = [[dma(sp, dx[k], xsc[:, k, :], X[:, k, :], xt2[k]), dve.last, act.last] for k in range(8)]
            nf = Norm(1024)
            XR = unit(HO, 0, [P, 8, S])
            dxr = [Dsem(f"xr{k}") for k in range(8)]
            xr = []

            def on_last(m, t):
                if m == 0:
                    xr.extend(dma(sp, dxr[k], XR[:, k, :], xsc[:, k, :], stt["ups"], *tsp[k]) for k in range(8))
                nf.feed(X[:, m, :], t)

            mlp("fa2_", *relu_up("fa1_", h, nx, lambda j: pbias[:, 12 + j:13 + j]), 8, X, [list(t) for t in tsp], norm=nx, first_copy=True, on_last=on_last)
            nf.stats()
            sR, tR = nf.spread()
            dout = Dsem("out")
            for k in range(8):
                t = STT(X[:, k, :], X[:, k, :], gain(3)(k), sR.ap[:], MUL, MUL, tR, act.last)
                t = TT(XR[:, k, :], XR[:, k, :], X[:, k, :], ADD, t, xr[k], q=(pool, dve)[k % 2])
                t = dma(sp, dout, out[:, k, :], XR[:, k, :], t)
            sp.wait(t)
        else:
            dout = Dsem("out")
            for k in range(8):
                t = dma(sp, dout, out[:, k, :], X[:, k, :], xt[k])
            sp.wait(t)
        assert ws.cur == len(wl), (ws.cur, len(wl))

        block = ctx.enter_context(nc.Block())

        @block.sync
        def _(e):
            sp.run(e)

        @block.scalar
        def _(e):
            act.run(e)

        @block.vector
        def _(e):
            dve.run(e)

        @block.gpsimd
        def _(e):
            pool.run(e)

        @block.tensor
        def _(e):
            pe.run(e)



def layout(inputs):
    g = {k: np.asarray(v) for k, v in inputs.items()}

    def tiles(w):
        k, m = w.shape
        return np.ascontiguousarray(w.reshape(k // P, P, m // P, P).transpose(2, 1, 0, 3)).reshape(m // P, P, k)

    def colv(v):
        return v.reshape(-1, P).T

    a = {}
    a["xT"] = np.ascontiguousarray(g["x"][0].T.reshape(8, P, S).transpose(1, 0, 2))
    a["metaT"] = np.ascontiguousarray(g["meta_tokens"].T.reshape(8, P, NMETA).transpose(1, 0, 2))
    w = g["w_in"][0]
    a["w_in"] = tiles(np.concatenate([w[:, :1536], w[:, 1552:]], axis=1))
    a["w_gr"] = np.ascontiguousarray(w[:, 1536:1552].reshape(8, P, 16).transpose(1, 0, 2)).reshape(P, 128)
    a["w_gate_up"] = g["w_gate_up"][0]
    a["w_out"], a["w_up"], a["w_down"] = tiles(g["w_out"][0]), tiles(g["w_up"][0]), tiles(g["w_down"][0])
    w = g["w_in_2"][0]
    a["w_in2"] = tiles(np.concatenate([w[:, :1152], w[:, 1158:]], axis=1))
    a["w_fa"] = np.ascontiguousarray(w[:, 1152:1158].reshape(8, P, W2).transpose(1, 0, 2)).reshape(P, 8 * W2)
    a["w_o2"], a["w_up2"], a["w_down2"] = tiles(g["w_o_2"][0]), tiles(g["w_up_2"][0]), tiles(g["w_down_2"][0])
    a["w_ada"] = tiles(g["w_ada_3"])
    a["w_in3"], a["w_out3"], a["w_fc1"], a["w_fc2"] = tiles(g["w_in_3"]), tiles(g["w_out_3"]), tiles(g["w_fc1_3"]), tiles(g["w_fc2_3"])
    a["w_sp"] = np.ascontiguousarray(g["w_spatial_3"].transpose(2, 0, 1))
    a["b_sp"] = g["b_spatial_3"]
    a["lnv_g"], a["lnv_b"] = g["ln_v_gain_3"], g["ln_v_bias_3"]
    a["w_pool"] = np.ascontiguousarray(g["w_pool_3"].transpose(1, 0, 2))
    cols = np.zeros((P, NCOL), np.float32)

    def put(name, v):
        s, n = COLS[name]
        cols[:v.shape[0], s:s + n] = v

    put("norm_mix", colv(g["norm_mix_w"][0]))
    put("norm_mlp", colv(g["norm_mlp_w"][0]))
    put("norm_final", colv(g["norm_final_w"]))
    put("b_gate", colv(g["b_gate"][0]))
    put("gla_norm", colv(g["gla_norm_w"][0]))
    put("conv1", g["conv_w"][0].reshape(3, 4, P).transpose(2, 1, 0).reshape(P, 12))
    put("ln1", colv(g["ln1_g_2"][0]))
    put("ln2", colv(g["ln2_g_2"][0]))
    put("g_final", colv(g["g_final_2"]))
    put("fox", colv(g["g_out_fox_2"][0]))
    put("dil", colv(g["g_out_dil_2"][0]))
    put("conv2", g["conv_w_2"][0].reshape(31, 2, P).transpose(2, 1, 0).reshape(P, 62))
    put("conv2_b", colv(g["conv_b_2"][0]))
    put("cn_g", colv(g["cnorm_g_2"][0]))
    put("cn_b", colv(g["cnorm_b_2"][0]))
    put("ffn_w", g["ffn_conv_w_2"][0].reshape(3, 44, P).transpose(2, 1, 0).reshape(P, 132))
    put("ffn_b", colv(g["ffn_conv_b_2"][0]))
    put("b_ada", colv(g["b_ada_3"]))
    put("n1pre", colv(g["norm1_pre_3"]))
    put("n1post", colv(g["norm1_post_3"]))
    put("n2pre", colv(g["norm2_pre_3"]))
    put("n2post", colv(g["norm2_post_3"]))
    put("pscale", colv(g["pool_scale_3"]))
    put("b_pool", g["b_pool_3"].T)
    put("b_forget", g["b_forget_2"][0][:, None])
    put("c", colv(g["c_3"][0]))
    rc = np.zeros((4, 16), np.float32)
    for i, w_ in enumerate((2, 4, 8, 16)):
        rc[i] = 1.0 / np.minimum(np.arange(16) + 1.0, w_)
    put("rcnt", np.broadcast_to(rc.reshape(1, 64), (P, 64)))
    a["cols"] = cols
    a["ident"] = np.eye(P, dtype=np.float32)
    j, i = np.meshgrid(np.arange(P), np.arange(P), indexing="ij")
    m = [(j // (2 * h) == i // (2 * h)) & (j % (2 * h) < h) & (i % (2 * h) >= h) for h in LEVELS] + [j == i]
    a["masks"] = np.ascontiguousarray(np.stack(m, 1).astype(np.float32)).reshape(P, 1024)
    q, k = j, i
    ok = [k >= q, k <= q, (k % 2 == q % 2) & (k <= q)]
    a["negm"] = np.ascontiguousarray(np.stack([np.where(o, 0.0, NEG) for o in ok], 1).astype(np.float32)).reshape(P, 384)
    sl = np.zeros((6, 6, P), np.float32)
    for h in range(6):
        sl[h, h] = 1.0
    a["sel"] = sl
    a["tri"] = (i >= j).astype(np.float32)
    return a


def plan_block2(plan, plan_mlp, d, upto):
    w = d["w_in2"]
    for n, m in (("gg0", 20), ("gv0", 18), ("gg1", 21), ("gv1", 19)):
        plan(n, w[m])
    plan("fa", d["w_fa"])
    for n, m in (("vb", 15), ("qb", 9), ("kb", 12), ("va", 6), ("qa", 0), ("ka", 3)):
        for j in range(3):
            plan(f"{n}{j}", w[m + j])
    for f in range(44 if upto >= 3 else 0):
        plan(f"b{f}", d["w_in3"][f] if f < 12 else d["w_fc1"][f - 12], split=False)
    for m in range(8):
        plan(f"w2o{m}", d["w_o2"][m])
    plan_mlp("w_up2", "w_down2", "fup", "fdn", 6, 8, sizes=[2] + [4] * 5, pairs=True)


def plan_block3(plan, plan_mlp, d):
    for n, m in (("zv", 4), ("zb", 8), ("zu", 0)):
        for j in range(4):
            plan(f"{n}{j}", d["w_in3"][m + j])
    for m in range(8):
        plan(f"wo3{m}", d["w_out3"][m])
    plan_mlp("w_fc1", "w_fc2", "fa1_", "fa2_", 8, 8)


def kernel(**inputs):
    import concourse.bacc as _bacc
    from concourse.bass_utils import run_bass_kernel_spmd as _run

    nc = _bacc.Bacc("TRN2", target_bir_lowering=False, num_devices=1)
    arrays = layout(inputs)
    d = {n: nc.dram_tensor("in_" + n, a.shape, mybir.dt.from_np(a.dtype), kind="ExternalInput").ap()
         for n, a in arrays.items()}
    out = nc.dram_tensor("out_0", (P, 8, S), F, kind="ExternalOutput").ap()
    build(nc, d, out)
    r = _run(nc, [{"in_" + n: a for n, a in arrays.items()}], core_ids=[0])
    o = r.results[0]["out_0"]
    return np.ascontiguousarray(o.transpose(2, 1, 0)).reshape(1, S, 1024)
```
